# Optimizing a Trainium2 kernel written in Bass

```python
import jax, jax.numpy as jnp
from jax import lax
import numpy as np
import math

D_MODEL = 1024
BATCH = 1
SEQ = 512
DEPTH = 2

HEAD_DIM = 64
ROT_DIM = HEAD_DIM // 4
ROPE_THETA = 500000.0
A_HEADS = (D_MODEL // 2) // (2 * HEAD_DIM)
B_HEADS = (D_MODEL // 2) // HEAD_DIM
KV_LORA = D_MODEL // 4
IDX_HEADS = 4
IDX_DIM = 64
TOPK_MAX = 256
QBLOCK = 128
C_WIDTH = D_MODEL // 2
CONV_W = 3
POOL_WINDOWS = (2, 4, 8, 16)
POOL_WIDTH = D_MODEL // 2
POOL_GROUP = POOL_WIDTH // len(POOL_WINDOWS)
MEM_LEN = 256
X_HEADS = 4
X_HEAD_DIM = D_MODEL // 8
D_FF = 4 * D_MODEL
EPS = 1e-6
N_EVEN = (DEPTH + 1) // 2
N_ODD = DEPTH // 2
EVEN_SPLITS = (A_HEADS * 2 * HEAD_DIM, A_HEADS * 2 * HEAD_DIM, A_HEADS * 2 * HEAD_DIM,
               B_HEADS * HEAD_DIM, KV_LORA, IDX_HEADS * IDX_DIM, IDX_DIM, IDX_HEADS)
EVEN_IN = sum(EVEN_SPLITS)
ODD_SPLITS = (C_WIDTH, C_WIDTH, C_WIDTH, POOL_WIDTH)
ODD_IN = sum(ODD_SPLITS)


def rmsnorm(x, g):
    xf = x.astype(jnp.float32)
    y = xf * lax.rsqrt(jnp.mean(xf * xf, axis=-1, keepdims=True) + EPS)
    return (y * g.astype(jnp.float32)).astype(x.dtype)

def _split(a, sizes):
    return jnp.split(a, np.cumsum(sizes)[:-1].tolist(), axis=-1)

def rope_tables(positions):
    inv = ROPE_THETA ** (-jnp.arange(0, ROT_DIM, 2, dtype=jnp.float32) / ROT_DIM)
    ang = positions.astype(jnp.float32)[..., None] * inv
    return jnp.cos(ang)[:, :, None, :], jnp.sin(ang)[:, :, None, :]

def rope(x, cos, sin):
    half = ROT_DIM // 2
    xr, xp = x[..., :ROT_DIM], x[..., ROT_DIM:]
    x1, x2 = xr[..., :half], xr[..., half:]
    rot = jnp.concatenate([x1 * cos - x2 * sin, x2 * cos + x1 * sin], axis=-1)
    return jnp.concatenate([rot.astype(x.dtype), xp], axis=-1)

def even_mixer(h, cos, sin, w_in, gq_a, gk_a, lam, lam_init, g_sub_a,
               g_kv_b, w_kv_up_b, gq_b, gk_b, g_kidx, w_out, k_sel):
    B, S, _ = h.shape
    nb = S // QBLOCK

    def to_blocks(a):
        return jnp.moveaxis(a.reshape((B, nb, QBLOCK) + a.shape[2:]), 1, 0)

    def from_blocks(o):
        return jnp.moveaxis(o, 0, 1).reshape((B, S) + o.shape[3:])

    qa, ka, va, qb, ckv, qi, ki, wi = _split(h @ w_in, EVEN_SPLITS)

    qa = rope(rmsnorm(qa.reshape(B, S, 2 * A_HEADS, HEAD_DIM), gq_a), cos, sin)
    qa = qa.reshape(B, S, A_HEADS, 2, HEAD_DIM)
    ka = rope(rmsnorm(ka.reshape(B, S, 2 * A_HEADS, HEAD_DIM), gk_a), cos, sin)
    ka = ka.reshape(B, S, A_HEADS, 2, HEAD_DIM)
    va = va.reshape(B, S, A_HEADS, 2 * HEAD_DIM)

    kb, vb = jnp.split(rmsnorm(ckv, g_kv_b) @ w_kv_up_b, 2, axis=-1)
    qb = rope(rmsnorm(qb.reshape(B, S, B_HEADS, HEAD_DIM), gq_b), cos, sin)
    kb = rope(rmsnorm(kb.reshape(B, S, B_HEADS, HEAD_DIM), gk_b), cos, sin)
    vb = vb.reshape(B, S, B_HEADS, HEAD_DIM)
    qi = rope(qi.reshape(B, S, IDX_HEADS, IDX_DIM), cos, sin)
    ki = rope(rmsnorm(ki, g_kidx)[:, :, None, :], cos, sin)[:, :, 0, :]
    wi = wi.astype(jnp.float32) * (IDX_HEADS ** -0.5 * IDX_DIM ** -0.5)

    kpos = jnp.arange(S)
    scale = HEAD_DIM ** -0.5

    def a_block(args):
        q, t0 = args
        qpos = t0 + jnp.arange(QBLOCK)
        causal = kpos[None, :] <= qpos[:, None]
        logits = jnp.einsum('bqhcd,bkhcd->bhcqk', q, ka).astype(jnp.float32) * scale
        p = jax.nn.softmax(jnp.where(causal, logits, -jnp.inf), axis=-1)
        attn = p[:, :, 0] - lam * p[:, :, 1]
        return jnp.einsum('bhqk,bkhe->bqhe', attn.astype(va.dtype), va)

    def b_block(args):
        q, qidx, widx, t0 = args
        qpos = t0 + jnp.arange(QBLOCK)
        causal = kpos[None, :] <= qpos[:, None]
        isc = jax.nn.relu(jnp.einsum('bqhd,bkd->bqhk', qidx, ki).astype(jnp.float32))
        isc = jnp.einsum('bqhk,bqh->bqk', isc, widx)
        isc = jnp.where(causal[None], isc, -jnp.inf)
        _, idx = lax.top_k(isc, k_sel)
        k_g = jax.vmap(lambda a, i: a[i])(kb, idx)
        v_g = jax.vmap(lambda a, i: a[i])(vb, idx)
        logits = jnp.einsum('bqhd,bqkhd->bhqk', q, k_g).astype(jnp.float32) * scale
        valid = (idx <= qpos[None, :, None])[:, None]
        p = jax.nn.softmax(jnp.where(valid, logits, -jnp.inf), axis=-1)
        return jnp.einsum('bhqk,bqkhd->bqhd', p.astype(vb.dtype), v_g)

    starts = jnp.arange(nb, dtype=jnp.int32) * QBLOCK
    out_a = from_blocks(lax.map(a_block, (to_blocks(qa), starts)))
    out_a = rmsnorm(out_a, g_sub_a) * (1.0 - lam_init)
    out_b = from_blocks(lax.map(b_block, (to_blocks(qb), to_blocks(qi), to_blocks(wi), starts)))
    y = jnp.concatenate([out_a.reshape(B, S, -1), out_b.reshape(B, S, -1)], axis=-1)
    return y @ w_out

def pool_mixer(z, w_pool, pool_scale):
    B, S, _ = z.shape
    zf = z.astype(jnp.float32).reshape(B, S, len(POOL_WINDOWS), POOL_GROUP)
    csp = jnp.pad(jnp.cumsum(zf, axis=1), ((0, 0), (1, 0), (0, 0), (0, 0)))
    t = jnp.arange(S)
    outs = []
    for g, w in enumerate(POOL_WINDOWS):
        lo = jnp.maximum(t + 1 - w, 0)
        win_sum = csp[:, 1:, g] - csp[:, lo, g]
        cnt = jnp.minimum(t + 1, w).astype(jnp.float32)
        outs.append(win_sum / cnt[None, :, None] - zf[:, :, g])
    pooled = jnp.stack(outs, axis=2).astype(z.dtype)
    y = jnp.einsum('bsgc,gcd->bsgd', pooled, w_pool).reshape(B, S, POOL_WIDTH)
    return y * pool_scale

def odd_mixer(h, w_in, conv_w, w_pool, pool_scale, w_out):
    gb, gc, hc, zd = _split(h @ w_in, ODD_SPLITS)
    u = gc * hc
    conv = lax.conv_general_dilated(
        u, conv_w[:, None, :].astype(u.dtype), window_strides=(1,),
        padding=[(CONV_W - 1, 0)], dimension_numbers=('NWC', 'WIO', 'NWC'),
        feature_group_count=C_WIDTH)
    yc = gb * conv
    yd = pool_mixer(zd, w_pool, pool_scale)
    return jnp.concatenate([yc, yd], axis=-1) @ w_out

def cross_attn(h, m, wq, wkv, gq, gk, wo):
    B, S, _ = h.shape
    q = rmsnorm((h @ wq).reshape(B, S, X_HEADS, X_HEAD_DIM), gq)
    k, v = jnp.split(m @ wkv, 2, axis=-1)
    k = rmsnorm(k.reshape(B, -1, X_HEADS, X_HEAD_DIM), gk)
    v = v.reshape(B, -1, X_HEADS, X_HEAD_DIM)
    logits = jnp.einsum('bqhd,bkhd->bhqk', q, k).astype(jnp.float32) * X_HEAD_DIM ** -0.5
    p = jax.nn.softmax(logits, axis=-1)
    o = jnp.einsum('bhqk,bkhd->bqhd', p.astype(v.dtype), v).reshape(B, S, -1)
    return o @ wo

def mlp(h, w_up, w_down):
    return jnp.square(jax.nn.relu(h @ w_up)) @ w_down

def first_inputs(seed: int = 0) -> dict:
    key = jax.random.key(seed)
    ks = iter(jax.random.split(key, 48))

    def nrm(shape, scale):
        return scale * jax.random.normal(next(ks), shape, jnp.float32)

    def gain(shape):
        return 1.0 + 0.05 * jax.random.normal(next(ks), shape, jnp.float32)

    d = D_MODEL
    return {
        'x': nrm((BATCH, SEQ, d), 1.0),
        'mem': nrm((BATCH, MEM_LEN, d), 1.0),
        'positions': jnp.tile(jnp.arange(SEQ, dtype=jnp.int32)[None, :], (BATCH, 1)),
        'g_mix': gain((DEPTH, d)),
        'g_xattn': gain((DEPTH, d)),
        'g_mem': gain((DEPTH, d)),
        'g_mlp': gain((DEPTH, d)),
        'wq_x': nrm((DEPTH, d, X_HEADS * X_HEAD_DIM), d ** -0.5),
        'wkv_x': nrm((DEPTH, d, 2 * X_HEADS * X_HEAD_DIM), d ** -0.5),
        'gq_x': gain((DEPTH, X_HEAD_DIM)),
        'gk_x': gain((DEPTH, X_HEAD_DIM)),
        'wo_x': nrm((DEPTH, X_HEADS * X_HEAD_DIM, d), (X_HEADS * X_HEAD_DIM) ** -0.5),
        'w_up': nrm((DEPTH, d, D_FF), d ** -0.5),
        'w_down': nrm((DEPTH, D_FF, d), D_FF ** -0.5),
        'w_in_e': nrm((N_EVEN, d, EVEN_IN), d ** -0.5),
        'gq_a': gain((N_EVEN, HEAD_DIM)),
        'gk_a': gain((N_EVEN, HEAD_DIM)),
        'lam_q1': nrm((N_EVEN, HEAD_DIM), 0.1),
        'lam_k1': nrm((N_EVEN, HEAD_DIM), 0.1),
        'lam_q2': nrm((N_EVEN, HEAD_DIM), 0.1),
        'lam_k2': nrm((N_EVEN, HEAD_DIM), 0.1),
        'g_sub_a': gain((N_EVEN, 2 * HEAD_DIM)),
        'g_kv_b': gain((N_EVEN, KV_LORA)),
        'w_kv_up_b': nrm((N_EVEN, KV_LORA, 2 * B_HEADS * HEAD_DIM), KV_LORA ** -0.5),
        'gq_b': gain((N_EVEN, HEAD_DIM)),
        'gk_b': gain((N_EVEN, HEAD_DIM)),
        'g_kidx': gain((N_EVEN, IDX_DIM)),
        'w_out_e': nrm((N_EVEN, d, d), d ** -0.5),
        'w_in_o': nrm((N_ODD, d, ODD_IN), d ** -0.5),
        'conv_w': nrm((N_ODD, CONV_W, C_WIDTH), CONV_W ** -0.5),
        'w_pool': nrm((N_ODD, len(POOL_WINDOWS), POOL_GROUP, POOL_GROUP), POOL_GROUP ** -0.5),
        'pool_scale': gain((N_ODD, POOL_WIDTH)),
        'w_out_o': nrm((N_ODD, d, d), d ** -0.5),
    }

def first_block(x, mem, positions, g_mix, g_xattn, g_mem, g_mlp, wq_x, wkv_x, gq_x, gk_x,
              wo_x, w_up, w_down, w_in_e, gq_a, gk_a, lam_q1, lam_k1, lam_q2, lam_k2,
              g_sub_a, g_kv_b, w_kv_up_b, gq_b, gk_b, g_kidx, w_out_e, w_in_o, conv_w,
              w_pool, pool_scale, w_out_o):
    S = x.shape[1]
    k_sel = min(TOPK_MAX, S // 4)
    cos, sin = rope_tables(positions)
    for i in range(DEPTH):
        j = i // 2
        h = rmsnorm(x, g_mix[i])
        if i % 2 == 0:
            lam_init = 0.8 - 0.6 * float(np.exp(-0.3 * i))
            f32 = jnp.float32
            lam = (jnp.exp(jnp.sum(lam_q1[j].astype(f32) * lam_k1[j].astype(f32)))
                   - jnp.exp(jnp.sum(lam_q2[j].astype(f32) * lam_k2[j].astype(f32)))
                   + lam_init)
            mix = even_mixer(h, cos, sin, w_in_e[j], gq_a[j], gk_a[j], lam, lam_init,
                             g_sub_a[j], g_kv_b[j], w_kv_up_b[j], gq_b[j], gk_b[j],
                             g_kidx[j], w_out_e[j], k_sel)
        else:
            mix = odd_mixer(h, w_in_o[j], conv_w[j], w_pool[j], pool_scale[j], w_out_o[j])
        x = x + mix
        x = x + cross_attn(rmsnorm(x, g_xattn[i]), rmsnorm(mem, g_mem[i]),
                           wq_x[i], wkv_x[i], gq_x[i], gk_x[i], wo_x[i])
        x = x + mlp(rmsnorm(x, g_mlp[i]), w_up[i], w_down[i])
    return x


DEPTH_2 = 1

CHUNK = 64
D_MIX = D_MODEL
GROUP_W = D_MIX // 4

SB_HEADS = 4
SB_HEAD_DIM = GROUP_W // SB_HEADS
SB_BLOCK = 128
RG_WIDTH = GROUP_W
RG_BLOCKS = 4
RG_BLOCK_DIM = RG_WIDTH // RG_BLOCKS
RG_CONV = 4
RG_C = 8.0
HG_HEADS = 4
HG_DK = GROUP_W // HG_HEADS
HG_DV = GROUP_W // HG_HEADS
M2_HEADS = 4
M2_HEAD_DIM = GROUP_W // M2_HEADS
M2_GROUPS = 2
M2_STATE = 128
M2_CONV = 4
M2_CONV_DIM = GROUP_W + 2 * M2_GROUPS * M2_STATE
N_EXPERTS = 32
TOP_K = 4
D_FF_2 = D_MODEL
SWIGLU_LIMIT = 7.0
SWIGLU_ALPHA = 1.702
MOE_BLOCK = 128

IN_WIDTHS = ([GROUP_W] * 3
             + [GROUP_W] * 2
             + [GROUP_W] * 4
             + [GROUP_W, M2_CONV_DIM, M2_HEADS])
D_IN = sum(IN_WIDTHS)


def rms_norm(x, g):
    xf = x.astype(jnp.float32)
    y = xf * lax.rsqrt(jnp.mean(xf * xf, axis=-1, keepdims=True) + EPS)
    return (y * g.astype(jnp.float32)).astype(x.dtype)

def group_rms(x, n_groups):
    shp = x.shape
    xg = x.reshape(shp[:-1] + (n_groups, shp[-1] // n_groups))
    xg = xg * lax.rsqrt(jnp.mean(xg * xg, axis=-1, keepdims=True) + EPS)
    return xg.reshape(shp)

def causal_depthwise_conv(x, w, b):
    k = w.shape[0]
    y = lax.conv_general_dilated(x, w[:, None, :], window_strides=(1,), padding=[(k - 1, 0)],
                                 dimension_numbers=("NWC", "WIO", "NWC"),
                                 feature_group_count=x.shape[-1])
    return y + b

def stick_breaking_attention(q, k, v):
    L = q.shape[2]
    scale = q.shape[-1] ** -0.5
    outs = []
    for blk in range(L // SB_BLOCK):
        q0 = blk * SB_BLOCK
        lk = q0 + SB_BLOCK
        z = jnp.einsum("bhtd,bhsd->bhts", q[:, :, q0:lk], k[:, :, :lk]).astype(jnp.float32) * scale
        t_idx = q0 + jnp.arange(SB_BLOCK)[:, None]
        s_idx = jnp.arange(lk)[None, :]
        mask = s_idx < t_idx
        log_keep = jnp.where(mask, jax.nn.log_sigmoid(-z), 0.0)
        log_remain = lax.cumsum(log_keep, axis=3, reverse=True) - log_keep
        log_a = jnp.where(mask, jax.nn.log_sigmoid(z) + log_remain, -jnp.inf)
        a = jnp.exp(log_a)
        outs.append(jnp.einsum("bhts,bhsd->bhtd", a.astype(v.dtype), v[:, :, :lk]))
    return jnp.concatenate(outs, axis=2)

def rg_lru_branch(x_in, gate_in, conv_w, conv_b, wa, ba, wx, bx, lam):
    B_, L, W = x_in.shape
    xc = causal_depthwise_conv(x_in, conv_w, conv_b)
    xb = xc.reshape(B_, L, RG_BLOCKS, RG_BLOCK_DIM)
    r = jax.nn.sigmoid((jnp.einsum("blni,nij->blnj", xb, wa).reshape(B_, L, W) + ba).astype(jnp.float32))
    ig = jax.nn.sigmoid((jnp.einsum("blni,nij->blnj", xb, wx).reshape(B_, L, W) + bx).astype(jnp.float32))
    log_a = -RG_C * r * jax.nn.softplus(-lam.astype(jnp.float32))
    a = jnp.exp(log_a)
    mult = jnp.sqrt(-jnp.expm1(2.0 * log_a))
    mult = jnp.where((jnp.arange(L) == 0)[None, :, None], 1.0, mult)
    u = mult * ig * xc.astype(jnp.float32)

    def combine(c1, c2):
        a1, b1 = c1
        a2, b2 = c2
        return a1 * a2, a2 * b1 + b2

    _, hs = lax.associative_scan(combine, (a, u), axis=1)
    return (hs * jax.nn.gelu(gate_in.astype(jnp.float32))).astype(x_in.dtype)

def hgrn2_branch(q_in, f_in, i_in, g_in, lb, norm_g):
    B_, L, W = q_in.shape
    nc = L // CHUNK
    forget = lb + (1.0 - lb) * jax.nn.sigmoid(f_in.astype(jnp.float32))
    log_f = jnp.log(forget)
    key = 1.0 - forget
    q = jax.nn.silu(q_in.astype(jnp.float32))
    v = i_in.astype(jnp.float32)

    def to_chunks(t, d):
        return t.reshape(B_, nc, CHUNK, HG_HEADS, d).transpose(1, 0, 3, 2, 4)

    qc, kc, lfc = to_chunks(q, HG_DK), to_chunks(key, HG_DK), to_chunks(log_f, HG_DK)
    vc = to_chunks(v, HG_DV)
    causal = jnp.tril(jnp.ones((CHUNK, CHUNK), bool))

    def step(state, inp):
        qb, kb, vb, lfb = inp
        bcum = jnp.cumsum(lfb, axis=2)
        diff = bcum[:, :, :, None, :] - bcum[:, :, None, :, :]
        decay = jnp.exp(jnp.where(causal[:, :, None], diff, -jnp.inf))
        scores = jnp.einsum("bhtc,bhsc,bhtsc->bhts", qb, kb, decay)
        o = jnp.einsum("bhts,bhsv->bhtv", scores, vb) + jnp.einsum("bhtc,bhcv->bhtv", qb * jnp.exp(bcum), state)
        b_last = bcum[:, :, -1:, :]
        new_state = (jnp.exp(b_last[:, :, 0, :, None]) * state
                     + jnp.einsum("bhsc,bhsv->bhcv", kb * jnp.exp(b_last - bcum), vb))
        return new_state, o

    s0 = jnp.zeros((B_, HG_HEADS, HG_DK, HG_DV), jnp.float32)
    _, o = lax.scan(step, s0, (qc, kc, vc, lfc))
    o = o.transpose(1, 0, 3, 2, 4).reshape(B_, L, W)
    o = group_rms(o, HG_HEADS) * norm_g.astype(jnp.float32) * jax.nn.silu(g_in.astype(jnp.float32))
    return o.astype(q_in.dtype)

def segsum(x):
    q = x.shape[-1]
    cs = jnp.cumsum(x, axis=-1)
    diff = cs[..., :, None] - cs[..., None, :]
    return jnp.where(jnp.tril(jnp.ones((q, q), bool)), diff, -jnp.inf)

def mamba2_branch(z, xbc, dt_raw, conv_w, conv_b, dt_bias, a_log, d_skip, norm_g):
    B_, L, _ = z.shape
    nc = L // CHUNK
    H, P, G, N = M2_HEADS, M2_HEAD_DIM, M2_GROUPS, M2_STATE
    xbc = jax.nn.silu(causal_depthwise_conv(xbc, conv_w, conv_b))
    xs = xbc[..., :GROUP_W].reshape(B_, L, H, P).astype(jnp.float32)
    bm = jnp.repeat(xbc[..., GROUP_W:GROUP_W + G * N].reshape(B_, L, G, N), H // G, axis=2).astype(jnp.float32)
    cm = jnp.repeat(xbc[..., GROUP_W + G * N:].reshape(B_, L, G, N), H // G, axis=2).astype(jnp.float32)
    dt = jax.nn.softplus(dt_raw.astype(jnp.float32) + dt_bias.astype(jnp.float32))
    da = dt * (-jnp.exp(a_log.astype(jnp.float32)))
    xd = xs * dt[..., None]
    xd_c = xd.reshape(B_, nc, CHUNK, H, P)
    b_c = bm.reshape(B_, nc, CHUNK, H, N)
    c_c = cm.reshape(B_, nc, CHUNK, H, N)
    da_c = da.reshape(B_, nc, CHUNK, H).transpose(0, 3, 1, 2)
    a_cs = jnp.cumsum(da_c, axis=-1)
    lmat = jnp.exp(segsum(da_c))
    y_diag = jnp.einsum("bclhn,bcshn,bhcls,bcshp->bclhp", c_c, b_c, lmat, xd_c)
    decay_states = jnp.exp(a_cs[..., -1:] - a_cs)
    states = jnp.einsum("bcshn,bhcs,bcshp->bchpn", b_c, decay_states, xd_c)
    chunk_decay = jnp.exp(a_cs[..., -1])

    def step(hstate, inp):
        st, dec = inp
        return dec[..., None, None] * hstate + st, hstate

    h0 = jnp.zeros((B_, H, P, N), jnp.float32)
    _, prev = lax.scan(step, h0, (states.transpose(1, 0, 2, 3, 4), chunk_decay.transpose(2, 0, 1)))
    prev = prev.transpose(1, 0, 2, 3, 4)
    y_off = jnp.einsum("bclhn,bchpn,bhcl->bclhp", c_c, prev, jnp.exp(a_cs))
    y = (y_diag + y_off).reshape(B_, L, H, P) + xs * d_skip.astype(jnp.float32)[:, None]
    y = y.reshape(B_, L, GROUP_W) * jax.nn.silu(z.astype(jnp.float32))
    y = group_rms(y, M2_GROUPS) * norm_g.astype(jnp.float32)
    return y.astype(z.dtype)

def moe_ffn(x, router_w, router_b, w_gu, b_gu, w_down, b_down):
    B_, L, D = x.shape
    n_tok = B_ * L
    xt = x.reshape(n_tok, D)
    logits = (xt @ router_w + router_b).astype(jnp.float32)
    top_logits, top_idx = lax.top_k(logits, TOP_K)
    gates = jax.nn.softmax(top_logits, axis=-1)
    n_assign = n_tok * TOP_K
    flat_e = top_idx.reshape(-1)
    order = jnp.argsort(flat_e)
    sorted_e = flat_e[order]
    sorted_tok = (order // TOP_K).astype(jnp.int32)
    counts = jnp.bincount(flat_e, length=N_EXPERTS)
    padded = (counts + MOE_BLOCK - 1) // MOE_BLOCK * MOE_BLOCK
    pad_end = jnp.cumsum(padded)
    pad_start = pad_end - padded
    start = jnp.cumsum(counts) - counts
    dest = (pad_start[sorted_e] + jnp.arange(n_assign) - start[sorted_e]).astype(jnp.int32)
    n_blocks = -(-n_assign // MOE_BLOCK) + N_EXPERTS
    slot_tok = jnp.zeros((n_blocks * MOE_BLOCK,), jnp.int32).at[dest].set(sorted_tok)
    block_expert = jnp.minimum(jnp.searchsorted(pad_end, jnp.arange(n_blocks) * MOE_BLOCK, side="right"),
                               N_EXPERTS - 1)

    def run_block(args):
        tok, e = args
        hmid = xt[tok] @ w_gu[e] + b_gu[e]
        glu = jnp.minimum(hmid[:, 0::2], SWIGLU_LIMIT)
        lin = jnp.clip(hmid[:, 1::2], -SWIGLU_LIMIT, SWIGLU_LIMIT)
        act = glu * jax.nn.sigmoid(SWIGLU_ALPHA * glu) * (lin + 1.0)
        return act @ w_down[e] + b_down[e]

    y_slots = lax.map(run_block, (slot_tok.reshape(n_blocks, MOE_BLOCK), block_expert)).reshape(-1, D)
    slot_of = jnp.zeros((n_assign,), jnp.int32).at[order].set(dest)
    y = jnp.einsum("tk,tkd->td", gates.astype(x.dtype), y_slots[slot_of].reshape(n_tok, TOP_K, D))
    return y.reshape(B_, L, D)

def second_inputs(seed: int = 0) -> dict:
    key = jax.random.key(seed)
    ks = jax.random.split(key, 32)

    def nrm(k, shape, scale):
        return jax.random.normal(k, shape, jnp.float32) * scale

    def gain(k, shape):
        return 1.0 + 0.02 * jax.random.normal(k, shape, jnp.float32)

    x = nrm(ks[0], (BATCH, SEQ, D_MODEL), 1.0)
    norm_mix_g = gain(ks[1], (DEPTH_2, D_MODEL))
    w_in = nrm(ks[2], (DEPTH_2, D_MODEL, D_IN), D_MODEL ** -0.5)
    sb_norm_g = gain(ks[3], (DEPTH_2, GROUP_W))
    rg_conv_w = nrm(ks[4], (DEPTH_2, RG_CONV, RG_WIDTH), RG_CONV ** -0.5)
    rg_conv_b = nrm(ks[5], (DEPTH_2, RG_WIDTH), 0.01)
    rg_wa = nrm(ks[6], (DEPTH_2, RG_BLOCKS, RG_BLOCK_DIM, RG_BLOCK_DIM), RG_BLOCK_DIM ** -0.5)
    rg_ba = nrm(ks[7], (DEPTH_2, RG_WIDTH), 0.01)
    rg_wx = nrm(ks[8], (DEPTH_2, RG_BLOCKS, RG_BLOCK_DIM, RG_BLOCK_DIM), RG_BLOCK_DIM ** -0.5)
    rg_bx = nrm(ks[9], (DEPTH_2, RG_WIDTH), 0.01)
    a_pow = jax.random.uniform(ks[10], (DEPTH_2, RG_WIDTH), jnp.float32, 0.9, 0.999)
    s = a_pow ** (1.0 / RG_C)
    rg_lambda = jnp.log(s) - jnp.log1p(-s)
    rg_norm_g = gain(ks[11], (DEPTH_2, GROUP_W))
    hg_lower_bounds = nrm(ks[12], (DEPTH_2, GROUP_W), 0.1)
    hg_norm_g = gain(ks[13], (DEPTH_2, GROUP_W))
    m2_conv_w = nrm(ks[14], (DEPTH_2, M2_CONV, M2_CONV_DIM), M2_CONV ** -0.5)
    m2_conv_b = nrm(ks[15], (DEPTH_2, M2_CONV_DIM), 0.01)
    dt0 = jnp.exp(jax.random.uniform(ks[16], (DEPTH_2, M2_HEADS), jnp.float32, math.log(1e-3), math.log(1e-1)))
    m2_dt_bias = dt0 + jnp.log(-jnp.expm1(-dt0))
    m2_a_log = jnp.log(jax.random.uniform(ks[17], (DEPTH_2, M2_HEADS), jnp.float32, 1.0, 16.0))
    m2_d = gain(ks[18], (DEPTH_2, M2_HEADS))
    m2_norm_g = gain(ks[19], (DEPTH_2, GROUP_W))
    w_out = nrm(ks[20], (DEPTH_2, D_MIX, D_MODEL), 0.5 * D_MIX ** -0.5)
    norm_ffn_g = gain(ks[21], (DEPTH_2, D_MODEL))
    router_w = nrm(ks[22], (DEPTH_2, D_MODEL, N_EXPERTS), D_MODEL ** -0.5)
    router_b = nrm(ks[23], (DEPTH_2, N_EXPERTS), 0.01)
    moe_w_gu = nrm(ks[24], (DEPTH_2, N_EXPERTS, D_MODEL, 2 * D_FF_2), D_MODEL ** -0.5)
    moe_b_gu = nrm(ks[25], (DEPTH_2, N_EXPERTS, 2 * D_FF_2), 0.01)
    moe_w_down = nrm(ks[26], (DEPTH_2, N_EXPERTS, D_FF_2, D_MODEL), 0.5 * D_FF_2 ** -0.5)
    moe_b_down = nrm(ks[27], (DEPTH_2, N_EXPERTS, D_MODEL), 0.01)
    final_norm_g = gain(ks[28], (D_MODEL,))
    return {"x": x, "norm_mix_g": norm_mix_g, "w_in": w_in, "sb_norm_g": sb_norm_g,
            "rg_conv_w": rg_conv_w, "rg_conv_b": rg_conv_b, "rg_wa": rg_wa, "rg_ba": rg_ba,
            "rg_wx": rg_wx, "rg_bx": rg_bx, "rg_lambda": rg_lambda, "rg_norm_g": rg_norm_g,
            "hg_lower_bounds": hg_lower_bounds, "hg_norm_g": hg_norm_g,
            "m2_conv_w": m2_conv_w, "m2_conv_b": m2_conv_b, "m2_dt_bias": m2_dt_bias,
            "m2_a_log": m2_a_log, "m2_d": m2_d, "m2_norm_g": m2_norm_g, "w_out": w_out,
            "norm_ffn_g": norm_ffn_g, "router_w": router_w, "router_b": router_b,
            "moe_w_gu": moe_w_gu, "moe_b_gu": moe_b_gu, "moe_w_down": moe_w_down,
            "moe_b_down": moe_b_down, "final_norm_g": final_norm_g}

def second_block(x, norm_mix_g, w_in, sb_norm_g, rg_conv_w, rg_conv_b, rg_wa, rg_ba, rg_wx, rg_bx,
              rg_lambda, rg_norm_g, hg_lower_bounds, hg_norm_g, m2_conv_w, m2_conv_b, m2_dt_bias,
              m2_a_log, m2_d, m2_norm_g, w_out, norm_ffn_g, router_w, router_b, moe_w_gu, moe_b_gu,
              moe_w_down, moe_b_down, final_norm_g):
    B_, L, _ = x.shape
    lbs = jnp.cumsum(jax.nn.softmax(hg_lower_bounds.astype(jnp.float32), axis=0), axis=0)
    lbs = lbs - lbs[0]
    split_at = np.cumsum(IN_WIDTHS)[:-1].tolist()

    def to_heads(t, n):
        return t.reshape(B_, L, n, -1).transpose(0, 2, 1, 3)

    h = x
    for l in range(DEPTH_2):
        u = rms_norm(h, norm_mix_g[l])
        proj = u @ w_in[l]
        (sb_q, sb_k, sb_v, rg_x, rg_g, hg_q, hg_f, hg_i, hg_g,
         m2_z, m2_xbc, m2_dt) = jnp.split(proj, split_at, axis=-1)
        o_a = stick_breaking_attention(to_heads(sb_q, SB_HEADS), to_heads(sb_k, SB_HEADS), to_heads(sb_v, SB_HEADS))
        o_a = rms_norm(o_a.transpose(0, 2, 1, 3).reshape(B_, L, GROUP_W), sb_norm_g[l])
        o_b = rms_norm(rg_lru_branch(rg_x, rg_g, rg_conv_w[l], rg_conv_b[l], rg_wa[l], rg_ba[l],
                                     rg_wx[l], rg_bx[l], rg_lambda[l]), rg_norm_g[l])
        o_c = hgrn2_branch(hg_q, hg_f, hg_i, hg_g, lbs[l], hg_norm_g[l])
        o_d = mamba2_branch(m2_z, m2_xbc, m2_dt, m2_conv_w[l], m2_conv_b[l], m2_dt_bias[l],
                            m2_a_log[l], m2_d[l], m2_norm_g[l])
        mix = jnp.concatenate([o_a, o_b, o_c, o_d], axis=-1)
        h = h + mix @ w_out[l]
        h = h + moe_ffn(rms_norm(h, norm_ffn_g[l]), router_w[l], router_b[l], moe_w_gu[l],
                        moe_b_gu[l], moe_w_down[l], moe_b_down[l])
    return rms_norm(h, final_norm_g)


_first_inputs = second_inputs


def second_inputs(seed=0):
    import zlib

    import numpy as np

    out = dict(_first_inputs(seed))
    spreads = {}
    factors = {'norm_mix_g': 2.686,
     'sb_norm_g': 50.57,
     'rg_ba': 64.0,
     'rg_bx': 64.0,
     'rg_norm_g': 48.869,
     'hg_norm_g': 26.479,
     'm2_conv_b': 45.147,
     'm2_dt_bias': 26.2,
     'm2_d': 64.0,
     'm2_norm_g': 39.808,
     'router_b': 34.449,
     'moe_b_gu': 64.0,
     'moe_b_down': 47.651,
     'final_norm_g': 7.507,
     'rg_conv_b': 6.357,
     'm2_a_log': 8.0,
     'norm_ffn_g': 8.0}
    for name, (base, spread) in spreads.items():
        noise = np.random.default_rng([zlib.crc32(name.encode()), seed]).standard_normal(out[name].shape)
        drawn = base * np.exp(spread * noise) if base else spread * noise
        out[name] = __import__('jax').numpy.asarray(drawn.astype(out[name].dtype))
    for name, factor in factors.items():
        out[name] = (out[name] * factor).astype(out[name].dtype)
    return out


_narrow_inputs = second_inputs


def second_inputs(seed=0):

    out = dict(_narrow_inputs(seed))
    wider = {'sb_norm_g': 4.43,
     'rg_norm_g': 4.47,
     'hg_norm_g': 4.09,
     'm2_d': 8.03,
     'm2_norm_g': 5.54,
     'moe_b_down': 3.87,
     'final_norm_g': 3.08}
    for name, times in wider.items():
        mean = out[name].mean()
        out[name] = (mean + times * (out[name] - mean)).astype(out[name].dtype)
    return out


def setup_inputs(seed=0):
    out = dict(first_inputs(seed))
    for name, value in second_inputs(seed + 1).items():
        if name != "x":
            out[name + "_2"] = value
    return out


def reference(
    x, mem, positions, g_mix, g_xattn, g_mem, g_mlp, wq_x, wkv_x, gq_x, gk_x, wo_x, w_up,
    w_down, w_in_e, gq_a, gk_a, lam_q1, lam_k1, lam_q2, lam_k2, g_sub_a, g_kv_b, w_kv_up_b,
    gq_b, gk_b, g_kidx, w_out_e, w_in_o, conv_w, w_pool, pool_scale, w_out_o, norm_mix_g_2,
    w_in_2, sb_norm_g_2, rg_conv_w_2, rg_conv_b_2, rg_wa_2, rg_ba_2, rg_wx_2, rg_bx_2,
    rg_lambda_2, rg_norm_g_2, hg_lower_bounds_2, hg_norm_g_2, m2_conv_w_2, m2_conv_b_2,
    m2_dt_bias_2, m2_a_log_2, m2_d_2, m2_norm_g_2, w_out_2, norm_ffn_g_2, router_w_2,
    router_b_2, moe_w_gu_2, moe_b_gu_2, moe_w_down_2, moe_b_down_2, final_norm_g_2,
):
    x = first_block(
        x, mem, positions, g_mix, g_xattn, g_mem, g_mlp, wq_x, wkv_x, gq_x, gk_x, wo_x, w_up,
        w_down, w_in_e, gq_a, gk_a, lam_q1, lam_k1, lam_q2, lam_k2, g_sub_a, g_kv_b, w_kv_up_b,
        gq_b, gk_b, g_kidx, w_out_e, w_in_o, conv_w, w_pool, pool_scale, w_out_o,
    )
    return second_block(
        x, norm_mix_g_2, w_in_2, sb_norm_g_2, rg_conv_w_2, rg_conv_b_2, rg_wa_2, rg_ba_2,
        rg_wx_2, rg_bx_2, rg_lambda_2, rg_norm_g_2, hg_lower_bounds_2, hg_norm_g_2, m2_conv_w_2,
        m2_conv_b_2, m2_dt_bias_2, m2_a_log_2, m2_d_2, m2_norm_g_2, w_out_2, norm_ffn_g_2,
        router_w_2, router_b_2, moe_w_gu_2, moe_b_gu_2, moe_w_down_2, moe_b_down_2,
        final_norm_g_2,
    )


_drawn_inputs = setup_inputs


def setup_inputs(seed=0):
    import zlib

    import numpy as np

    out = dict(_drawn_inputs(seed))
    spreads = {}
    factors = {'g_xattn': 4.033,
     'gq_x': 4.012,
     'gk_x': 3.884,
     'gq_b': 3.889,
     'gk_b': 3.334,
     'norm_ffn_g_2': 2.744}
    for name, (base, spread) in spreads.items():
        noise = np.random.default_rng([zlib.crc32(name.encode()), seed]).standard_normal(out[name].shape)
        drawn = base * np.exp(spread * noise) if base else spread * noise
        out[name] = __import__('jax').numpy.asarray(drawn.astype(out[name].dtype))
    for name, factor in factors.items():
        out[name] = (out[name] * factor).astype(out[name].dtype)
    return out
```

```python
from contextlib import ExitStack

import concourse.bass as bass
from concourse import mybir

ALU = mybir.AluOpType
ACT = mybir.ActivationFunctionType
AX = mybir.AxisListType.X
F32 = mybir.dt.float32
I32 = mybir.dt.int32
U32 = mybir.dt.uint32
F32R = mybir.dt.float32r

P = 128
D = 1024
S = 512
KT = D // P
TT = S // P
MEM = 256
EPS = 1e-6
MASKED = -1e30
TAKEN = -3e38
TOPK = 128
EXPERTS = 32
RING = 4
UNIT = 8 * 512


class Signal:

    def __init__(self, k, name):
        self.sem = k.ctx.enter_context(k.nc.semaphore(name))
        self.base = 0

    def at(self, n):
        return self.base + n

    def passed(self, n):
        self.base += n


class Chain:

    def __init__(self, k, name):
        self.sem = k.ctx.enter_context(k.nc.semaphore(name))
        self.count = 0

    def step(self, eng, ins):
        self.count += 1
        ins.then_inc(self.sem, 1)
        eng.wait_ge(self.sem, self.count)


class Unit:

    def __init__(self, source, ktiles, cols):
        self.source, self.ktiles, self.cols = source, ktiles, cols


def cut(weight, row0, ktiles, col0, cols):
    rows = weight[row0:row0 + ktiles * P, col0:col0 + cols]
    return Unit(rows.rearrange("(k p) n -> p k n", p=P), ktiles, cols)


class Parts:

    def __init__(self, whole, high, low):
        self.whole, self.high, self.low = whole, high, low

    @property
    def shape(self):
        return self.whole.shape

    def __getitem__(self, at):
        return Parts(self.whole[at], self.high[at], self.low[at])

    def round(self, act):
        return act.activation(self.high, self.whole, ACT.Copy)

    def rest(self, dve):
        return dve.tensor_tensor(self.low, self.whole, self.high.bitcast(F32), ALU.subtract)


def parts_of(k, whole, ctx):
    high, low = (k.sb(name, list(whole.shape), F32R, ctx=ctx) for name in ("high_parts", "low_parts"))
    every = tuple(slice(None) for _ in whole.shape)
    return Parts(whole[every], high[every], low[every])


def products_of(a, b):
    return [(a.high, b.high), (a.high, b.low), (a.low, b.high)]


class Core:

    def __init__(self, nc, ctx, ins, out):
        self.nc, self.ctx, self.ins, self.out = nc, ctx, ins, out
        self.tensors = 0
        self.x = self.sb("x_residual", [P, TT, D])
        self.hT = self.sb("hT", [P, KT, S])
        self.ident = self.sb("ident", [P, P])
        self.ones = self.sb("ones", [P, P])
        self.causal = self.sb("causal", [P, P])
        self.strict = self.sb("strict", [P, P])
        self.eps = self.sb("eps", [P, 1])
        self.psum = ctx.enter_context(nc.psum_tensor("psum", [P, 8, 512], F32))
        self.loaded = Signal(self, "weights_loaded")
        self.unit_rounded = Signal(self, "unit_rounded")
        self.unit_split = Signal(self, "unit_split")
        self.input_rounded = Signal(self, "input_rounded")
        self.input_split = Signal(self, "input_split")
        self.bank_full = Signal(self, "bank_full")
        self.bank_free = Signal(self, "bank_free")
        self.small_loaded = Signal(self, "small_loaded")
        self.normalised = Signal(self, "normalised")
        self.turned = Signal(self, "turned")
        self.turned_even = Signal(self, "turned_even")
        self.turned_odd = Signal(self, "turned_odd")
        self.squares = Signal(self, "squares")
        self.roots = Signal(self, "roots")
        self.rstd = Signal(self, "rstd")
        self.scores_ready = Signal(self, "scores_ready")
        self.negmax_ready = Signal(self, "negmax_ready")
        self.probs_ready = Signal(self, "probs_ready")
        self.attn_ready = Signal(self, "attn_ready")
        self.attn_turned = Signal(self, "attn_turned")
        self.attnT_ready = Signal(self, "attnT_ready")
        self.out_ready = Signal(self, "out_ready")
        self.out_saved = Signal(self, "out_saved")
        self.pe_made = Signal(self, "pe_made")
        self.dve_made = Signal(self, "dve_made")
        self.act_made = Signal(self, "act_made")
        self.pool_made = Signal(self, "pool_made")
        self.stored = Signal(self, "stored")
        self.dve = Chain(self, "dve_order")
        self.act = Chain(self, "act_order")
        self.pool = Chain(self, "pool_order")
        self.units = weight_units(ins)
        self.consumed = 0
        self.used_at = {}

    def sb(self, name, shape, dtype=F32, ctx=None):
        self.tensors += 1
        return (ctx or self.ctx).enter_context(self.nc.sbuf_tensor(f"{name}_{self.tensors}", shape, dtype))

    def col(self, name, i, n=1):
        r, at = self.place[name]
        return self.cols[:, r, at + i:at + i + n]

    def block(self):
        return self.nc.Block(no_gpsimd_drain=True)

    def hold_units(self, ctx):
        self.unit_whole = self.sb("unit_whole", [P, UNIT], ctx=ctx)
        self.unit_high = self.sb("unit_high", [P, 2, UNIT], F32R, ctx=ctx)
        self.unit_low = self.sb("unit_low", [P, 2, UNIT], F32R, ctx=ctx)

    def unit(self, u):
        kt, cols = self.units[u].ktiles, self.units[u].cols
        views = (self.unit_whole[:, 0:kt * cols], self.unit_high[:, u % 2, 0:kt * cols],
                 self.unit_low[:, u % 2, 0:kt * cols])
        return Parts(*(view.rearrange("p (k n) -> p k n", k=kt) for view in views))

    def load_unit(self, sp, u):
        if u < len(self.units):
            if u >= 1:
                sp.wait_ge(self.unit_split.sem, u)
            sp.dma_start(self.unit(u).whole, self.units[u].source).then_inc(self.loaded.sem, 16)

    def round_unit(self, act, u):
        if u < len(self.units):
            act.wait_ge(self.loaded.sem, 16 * (u + 1))
            if u >= 2:
                act.wait_ge(self.bank_full.sem, self.used_at[u - 2])
            self.unit(u).round(act).then_inc(self.unit_rounded.sem, 1)

    def rest_of_unit(self, dve, u):
        if u < len(self.units):
            dve.wait_ge(self.unit_rounded.sem, u + 1)
            self.unit(u).rest(dve).then_inc(self.unit_split.sem, 1)


def weight_units(ins):
    units = []

    def columns(weight, widths, row0=0, ktiles=KT):
        at = 0
        for w in widths:
            units.append(cut(weight, row0, ktiles, at, w))
            at += w

    def cross(i):
        columns(ins["wq_x"][i], [512])
        columns(ins["wkv_x"][i], [512, 512])
        columns(ins["wo_x"][i], [1024], ktiles=4)

    def mlp(i):
        for part in range(4):
            for half in range(2):
                units.append(cut(ins["w_up"][i], 0, KT, part * 1024 + half * 512, 512))
            for half in range(2):
                units.append(cut(ins["w_down"][i], part * 1024, KT, half * 512, 512))

    columns(ins["w_in_e"][0], EVEN_UNITS)
    units.append(cut(ins["w_kv_up_b"][0], 0, 2, 0, 1024))
    columns(ins["w_out_e"][0], [512, 512])
    cross(0)
    mlp(0)
    columns(ins["w_in_o"][0], [512] * 4)
    columns(ins["w_out_o"][0], [512, 512])
    cross(1)
    mlp(1)
    columns(ins["w_in_2"][0], SECOND_UNITS)
    columns(ins["w_out_2"][0], [512, 512])
    return units


EVEN_UNITS = [512, 512, 512, 512, 290, 290]
SECOND_UNITS = [512, 256, 512, 512, 512, 256, 512, 260]



def project(k, jobs, evacuate, inputs=()):
    total = 0
    for job in jobs:
        total += len(job["banks"])
        k.used_at[job["unit"]] = k.bank_full.at(total)
    units = sorted({job["unit"] for job in jobs})
    first_job = {u: min(j for j, job in enumerate(jobs) if job["unit"] == u) for u in units}
    tiles = [x[:, c] for x in inputs for c in range(x.shape[1])]
    with k.block() as block:
        @block.sync
        def _(sp):
            for u in units:
                k.load_unit(sp, u + 2)

        @block.scalar
        def _(act):
            for tile in tiles:
                tile.round(act).then_inc(k.input_rounded.sem, 1)
            for u in units:
                k.round_unit(act, u + 1)

        @block.tensor
        def _(pe):
            n = 0
            split = 0
            for j, job in enumerate(jobs):
                pe.wait_ge(k.unit_split.sem, job["unit"] + 1)
                for b, (products, width) in enumerate(job["banks"]):
                    if n >= 8:
                        pe.wait_ge(k.bank_free.sem, k.bank_free.at(n - 7))
                    bank = k.psum[0:products[0][0].shape[-1], n % 8, 0:width]
                    for i, (lhsT, rhs) in enumerate(products):
                        needs = job.get("inputs_before", 0) + i + 1
                        if inputs and needs > split:
                            split = needs
                            pe.wait_ge(k.input_split.sem, k.input_split.at(split))
                        parts = products_of(lhsT, rhs)
                        for m, (a, c) in enumerate(parts):
                            ins = pe.matmul(bank, a, c, start=(i == 0 and m == 0),
                                            stop=(i == len(products) - 1 and m == len(parts) - 1))
                    ins.then_inc(k.bank_full.sem, 1)
                    n += 1

        @block.vector
        def _(dve):
            for i, tile in enumerate(tiles):
                dve.wait_ge(k.input_rounded.sem, k.input_rounded.at(i + 1))
                tile.rest(dve).then_inc(k.input_split.sem, 1)
            n = 0
            for j, job in enumerate(jobs):
                if first_job[job["unit"]] == j:
                    k.rest_of_unit(dve, job["unit"] + 1)
                for b, (products, width) in enumerate(job["banks"]):
                    dve.wait_ge(k.bank_full.sem, k.bank_full.at(n + 1))
                    bank = k.psum[0:products[0][0].shape[-1], n % 8, 0:width]
                    evacuate(dve, j, b, bank).then_inc(k.bank_free.sem, 1)
                    n += 1
    k.input_rounded.passed(len(tiles))
    k.input_split.passed(len(tiles))
    k.bank_full.passed(total)
    k.bank_free.passed(total)
    k.consumed = units[-1] + 1


def token_banks(k, u, hT, tiles=TT, col0=0, cols=None):
    w = k.unit(u)
    cols = cols or w.shape[2]
    kt = w.shape[1]
    return [([(hT[:, c, t * P:(t + 1) * P], w[:, c, col0:col0 + cols]) for c in range(kt)], cols)
            for t in range(tiles)]


def feature_banks(k, u, hT, col0=0, cols=None):
    w = k.unit(u)
    cols = cols or w.shape[2]
    kt = w.shape[1]
    return [([(w[:, c, col0 + m:col0 + min(m + P, cols)], hT[:, c, :]) for c in range(kt)], hT.shape[2])
            for m in range(0, cols, P)]


def turn(k, jobs):
    with k.block() as block:
        @block.tensor
        def _(pe):
            for j, (sources, dst, gain) in enumerate(jobs):
                if j >= 8:
                    saved = k.turned_even if j % 2 == 0 else k.turned_odd
                    pe.wait_ge(saved.sem, saved.at((j - 8) // 2 + 1))
                for i, src in enumerate(sources):
                    rows, w = src.shape
                    ins = pe.transpose(k.psum[0:w, j % 8, i * P:i * P + rows], src, k.ident[0:rows, 0:rows])
                ins.then_inc(k.turned.sem, 1)

        @block.vector
        def _(dve):
            for j, (sources, dst, gain) in enumerate(jobs):
                if j % 2 == 0:
                    dve.wait_ge(k.turned.sem, k.turned.at(j + 1))
                    bank = k.psum[0:dst.shape[0], j % 8, 0:dst.shape[1]]
                    if gain is None:
                        dve.tensor_copy(dst, bank).then_inc(k.turned_even.sem, 1)
                    else:
                        dve.tensor_scalar(dst, bank, gain, None, ALU.mult).then_inc(k.turned_even.sem, 1)

        @block.scalar
        def _(act):
            for j, (sources, dst, gain) in enumerate(jobs):
                if j % 2 == 1:
                    act.wait_ge(k.turned.sem, k.turned.at(j + 1))
                    bank = k.psum[0:dst.shape[0], j % 8, 0:dst.shape[1]]
                    act.activation(dst, bank, ACT.Copy, scale=1.0 if gain is None else gain)\
                       .then_inc(k.turned_odd.sem, 1)
    k.turned.passed(len(jobs))
    k.turned_even.passed((len(jobs) + 1) // 2)
    k.turned_odd.passed(len(jobs) // 2)


def row_norm(k, x, tiles, y, ctx):
    width = x.shape[2]
    ss = k.sb("norm_ss", [P, tiles], ctx=ctx)
    rms = k.sb("norm_rms", [P, tiles], ctx=ctx)
    rstd = k.sb("norm_rstd", [P, tiles], ctx=ctx)
    with k.block() as block:
        @block.scalar
        def _(act):
            for t in range(tiles):
                act.activation(y[:, t, :], x[:, t, :], ACT.Square, accum_out=ss[:, t:t + 1])\
                   .then_inc(k.squares.sem, 1)
            act.wait_ge(k.squares.sem, k.squares.at(tiles))
            act.activation(rms[:, :], ss[:, :], ACT.Sqrt, bias=k.eps[:, 0:1], scale=1.0 / width)\
               .then_inc(k.roots.sem, 1)

        @block.vector
        def _(dve):
            dve.wait_ge(k.roots.sem, k.roots.at(1))
            dve.reciprocal(rstd[:, :], rms[:, :]).then_inc(k.rstd.sem, 1)
            dve.wait_ge(k.rstd.sem, k.rstd.at(1))
            for t in range(tiles):
                dve.tensor_scalar(y[:, t, :], x[:, t, :], rstd[:, t:t + 1], None, ALU.mult)\
                   .then_inc(k.normalised.sem, 1)
    k.squares.passed(tiles)
    k.roots.passed(1)
    k.rstd.passed(1)
    k.normalised.passed(tiles)


def norm_and_turn(k, x, tiles, gain, dst):
    with ExitStack() as ctx:
        y = k.sb("norm_y", [P, tiles, D], ctx=ctx)
        row_norm(k, x, tiles, y, ctx)
        turn(k, [([y[:, t, c * P:(c + 1) * P] for t in range(tiles)], dst[:, c, 0:tiles * P], gain[:, c:c + 1])
                 for c in range(D // P)])


def add_to_residual(k, n_halves=2):
    def evacuate(dve, j, b, bank):
        cols = slice(j * 512, (j + 1) * 512)
        return dve.tensor_tensor(k.x[:, b, cols], bank, k.x[:, b, cols], ALU.add)
    return evacuate


def project_out(k, mixT, ktiles=KT):
    u = k.consumed
    with ExitStack() as ctx:
        mix = parts_of(k, mixT, ctx)
        if ktiles == KT:
            jobs = [{"unit": u + half, "banks": token_banks(k, u + half, mix)} for half in range(2)]
        else:
            jobs = [{"unit": u, "banks": token_banks(k, u, mix, col0=half * 512, cols=512)} for half in range(2)]
        project(k, jobs, add_to_residual(k), [mix])


def score_bank(k, units, u, c):
    return k.psum[:, (u % 2) * 2 + c, 0:units[u]["keys"]]


def attention_products(k, pe, units, probs, attnT, comps):
    n = len(units)

    def scores(u):
        un = units[u]
        if u >= 2:
            pe.wait_ge(k.probs_ready.sem, k.probs_ready.at(comps * (u - 1)))
        for c in range(comps):
            last = un["mask"] is None
            ins = pe.matmul(score_bank(k, units, u, c), un["q"][c], un["k"][c], start=True, stop=last)
            if not last:
                mask, col0 = un["mask"]
                ins = pe.matmul(score_bank(k, units, u, c)[:, col0:], k.ident[:, :], mask, start=False, stop=True)
        ins.then_inc(k.scores_ready.sem, 1)

    def turn_probs(u):
        if comps == 2:
            pe.wait_ge(k.attn_ready.sem, k.attn_ready.at(u + 1))
        else:
            pe.wait_ge(k.probs_ready.sem, k.probs_ready.at(u + 1))
        if u >= 2:
            pe.wait_ge(k.attnT_ready.sem, k.attnT_ready.at(u - 1))
        for i in range(units[u]["keys"] // P):
            ins = pe.transpose(k.psum[:, 4 + u % 2, i * P:(i + 1) * P],
                               probs[:, u % 2, 0, i * P:(i + 1) * P], k.ident[:, :])
        ins.then_inc(k.attn_turned.sem, 1)

    def values(u):
        un = units[u]
        pe.wait_ge(k.attnT_ready.sem, k.attnT_ready.at(u + 1))
        if u >= 2:
            pe.wait_ge(k.out_saved.sem, k.out_saved.at(u - 1))
        tiles = un["keys"] // P
        for i in range(tiles):
            ins = pe.matmul(k.psum[:, 6 + u % 2, 0:un["v"][0].shape[-1]], attnT[:, u % 2, i, :],
                            un["v"][i], start=(i == 0), stop=(i == tiles - 1))
        ins.then_inc(k.out_ready.sem, 1)

    scores(0)
    scores(1)
    for u in range(n):
        turn_probs(u)
        if u + 2 < n:
            scores(u + 2)
        values(u)


def save_attnT(k, dve, units, attnT, u):
    dve.wait_ge(k.attn_turned.sem, k.attn_turned.at(u + 1))
    if u >= 2:
        dve.wait_ge(k.out_ready.sem, k.out_ready.at(u - 1))
    w = units[u]["keys"]
    dve.tensor_copy(attnT[:, u % 2, 0:w // P, :], k.psum[:, 4 + u % 2, 0:w].rearrange("p (i q) -> p i q", q=P))\
       .then_inc(k.attnT_ready.sem, 1)


def save_out(k, dve, units, factor, u):
    dve.wait_ge(k.out_ready.sem, k.out_ready.at(u + 1))
    out = units[u]["out"]
    bank = k.psum[:, 6 + u % 2, 0:out.shape[-1]]
    if factor is None:
        dve.tensor_copy(out, bank).then_inc(k.out_saved.sem, 1)
    else:
        dve.tensor_scalar(out, bank, factor, None, ALU.mult).then_inc(k.out_saved.sem, 1)


def attention(k, units, scale, neg_lambda=None, probs=None):
    n = len(units)
    comps = 2 if neg_lambda is not None else 1
    with ExitStack() as ctx:
        if probs is None:
            probs = k.sb("probs", [P, 2, comps, 512], ctx=ctx)
        attnT = k.sb("attnT", [P, 2, 4, P], ctx=ctx)
        top = k.sb("score_max", [P, 2, comps], ctx=ctx)
        neg = k.sb("score_negmax", [P, 2, comps], ctx=ctx)
        sums = k.sb("prob_sums", [P, 2, comps], ctx=ctx)
        inv = k.sb("prob_inv", [P, 2, comps], ctx=ctx)
        with k.block() as block:
            @block.tensor
            def _(pe):
                attention_products(k, pe, units, probs, attnT, comps)

            @block.vector
            def _(dve):
                def maxima(u):
                    dve.wait_ge(k.scores_ready.sem, k.scores_ready.at(u + 1))
                    for c in range(comps):
                        ins = dve.reduce_max(top[:, u % 2, c:c + 1], score_bank(k, units, u, c), AX)
                        if c == comps - 1:
                            k.dve.step(dve, ins)
                    if u >= 2:
                        dve.wait_ge(k.probs_ready.sem, k.probs_ready.at(comps * (u - 1)))
                    dve.tensor_scalar(neg[:, u % 2, :], top[:, u % 2, :], -scale, None, ALU.mult)\
                       .then_inc(k.negmax_ready.sem, 1)

                def weigh(u):
                    dve.wait_ge(k.probs_ready.sem, k.probs_ready.at(comps * (u + 1)))
                    if u >= 2:
                        dve.wait_ge(k.out_saved.sem, k.out_saved.at(u - 1))
                    k.dve.step(dve, dve.reciprocal(inv[:, u % 2, :], sums[:, u % 2, :]))
                    if comps == 2:
                        w = units[u]["keys"]
                        a, b = probs[:, u % 2, 0, 0:w], probs[:, u % 2, 1, 0:w]
                        k.dve.step(dve, dve.tensor_scalar(b, b, inv[:, u % 2, 1:2], neg_lambda, ALU.mult, ALU.mult))
                        dve.scalar_tensor_tensor(out=a, in0=a, scalar=inv[:, u % 2, 0:1], in1=b,
                                                 op0=ALU.mult, op1=ALU.add).then_inc(k.attn_ready.sem, 1)

                def save(u):
                    save_out(k, dve, units, None if comps == 2 else inv[:, u % 2, 0:1], u)

                maxima(0)
                maxima(1)
                for u in range(n):
                    weigh(u)
                    save_attnT(k, dve, units, attnT, u)
                    if u >= 1:
                        save(u - 1)
                    if u + 2 < n:
                        maxima(u + 2)
                save(n - 1)

            @block.scalar
            def _(act):
                for u in range(n):
                    act.wait_ge(k.negmax_ready.sem, k.negmax_ready.at(u + 1))
                    if u >= 2:
                        act.wait_ge(k.attn_turned.sem, k.attn_turned.at(u - 1))
                    for c in range(comps):
                        act.activation(probs[:, u % 2, c, 0:units[u]["keys"]], score_bank(k, units, u, c), ACT.Exp,
                                       bias=neg[:, u % 2, c:c + 1], scale=scale,
                                       accum_out=sums[:, u % 2, c:c + 1]).then_inc(k.probs_ready.sem, 1)
    for s in (k.scores_ready, k.negmax_ready, k.attn_turned, k.attnT_ready, k.out_ready, k.out_saved):
        s.passed(n)
    k.probs_ready.passed(comps * n)
    if comps == 2:
        k.attn_ready.passed(n)


def mlp(k, i):
    norm_and_turn(k, k.x, TT, k.col("g_mlp", i * KT, KT), k.hT)
    with ExitStack() as ctx:
        inputs = parts_of(k, k.hT, ctx)
        hidden = k.hT
        for part in range(4):
            u = k.consumed

            def relu_squared(dve, j, b, bank):
                h = hidden[:, 4 * j + b, :]
                k.dve.step(dve, dve.tensor_scalar(h, bank, 0.0, None, ALU.max))
                return dve.tensor_tensor(h, h, h, ALU.mult)

            project(k, [{"unit": u + half, "banks": feature_banks(k, u + half, inputs)} for half in range(2)],
                    relu_squared, [inputs] if part == 0 else [])
            project_out(k, hidden)


def heads_norm(k, groups):
    with ExitStack() as ctx:
        counts = [x.shape[1] * x.shape[2] for x, _, _ in groups]
        most = max(n * x.shape[3] for n, (x, _, _) in zip(counts, groups))
        sq = k.sb("head_squares", [P, most], ctx=ctx)
        ss = k.sb("head_ss", [P, sum(counts)], ctx=ctx)
        rms = k.sb("head_rms", [P, sum(counts)], ctx=ctx)
        inv = k.sb("head_inv", [P, sum(counts)], ctx=ctx)
        spans = [slice(sum(counts[:g]), sum(counts[:g + 1])) for g in range(len(groups))]
        with k.block() as block:
            @block.vector
            def _(dve):
                for g, (x, out, gain) in enumerate(groups):
                    _, t, h, w = x.shape
                    view = sq[:, 0:t * h * w].rearrange("p (t h w) -> p t h w", t=t, h=h)
                    k.dve.step(dve, dve.tensor_tensor(view, x, x, ALU.mult))
                    dve.reduce_sum(ss[:, spans[g]].rearrange("p (t h) -> p t h", t=t), view, AX)\
                       .then_inc(k.squares.sem, 1)
                    dve.wait_ge(k.squares.sem, k.squares.at(g + 1))
                for g, (x, out, gain) in enumerate(groups):
                    _, t, h, w = x.shape
                    dve.wait_ge(k.roots.sem, k.roots.at(g + 1))
                    k.dve.step(dve, dve.reciprocal(inv[:, spans[g]], rms[:, spans[g]]))
                    scale = inv[:, spans[g]].rearrange("p (t h) -> p t h", t=t).unsqueeze(3)
                    ins = dve.tensor_tensor(out, x, scale.broadcast_to([P, t, h, w]), ALU.mult)
                    if gain is not None:
                        k.dve.step(dve, ins)
                        spread = gain.unsqueeze(1).unsqueeze(1).broadcast_to([P, t, h, w])
                        ins = dve.tensor_tensor(out, out, spread, ALU.mult)
                    ins.then_inc(k.normalised.sem, 1)

            @block.scalar
            def _(act):
                for g, (x, out, gain) in enumerate(groups):
                    act.wait_ge(k.squares.sem, k.squares.at(g + 1))
                    act.activation(rms[:, spans[g]], ss[:, spans[g]], ACT.Sqrt, bias=k.eps[:, 0:1],
                                   scale=1.0 / x.shape[3]).then_inc(k.roots.sem, 1)
    k.squares.passed(len(groups))
    k.roots.passed(len(groups))
    k.normalised.passed(len(groups))


def rope(k, tensors):
    with ExitStack() as ctx:
        most = TT * max(x.shape[2] for x in tensors) * 8
        tmp = k.sb("rope_tmp", [P, 4, most], ctx=ctx)
        with k.block() as block:
            @block.vector
            def _(dve):
                for x in tensors:
                    h = x.shape[2]
                    a, b = x[:, :, :, 0:8], x[:, :, :, 8:16]
                    cos = k.cos[:, :, :].unsqueeze(2).broadcast_to([P, TT, h, 8])
                    sin = k.sin[:, :, :].unsqueeze(2).broadcast_to([P, TT, h, 8])
                    t = [tmp[:, i, 0:TT * h * 8].rearrange("p (t h e) -> p t h e", t=TT, h=h) for i in range(4)]
                    dve.tensor_tensor(t[0], a, cos, ALU.mult)
                    dve.tensor_tensor(t[1], b, sin, ALU.mult)
                    dve.tensor_tensor(t[2], b, cos, ALU.mult)
                    k.dve.step(dve, dve.tensor_tensor(t[3], a, sin, ALU.mult))
                    dve.tensor_tensor(a, t[0], t[1], ALU.subtract)
                    k.dve.step(dve, dve.tensor_tensor(b, t[2], t[3], ALU.add))


def by_head(x, width):
    return x.rearrange("p t (h w) -> p t h w", w=width)


def setup(k, weights):
    ins, nc = k.ins, k.nc
    rows = [[("g_mix", 16), ("g_xattn", 16), ("g_mem", 16), ("g_mlp", 16), ("norm_mix_g_2", 8),
             ("norm_ffn_g_2", 8), ("gq_x", 2), ("gk_x", 2), ("g_sub_a", 1), ("g_kv_b", 2), ("conv_w", 12),
             ("pool_scale", 4), ("sb_norm_g_2", 2), ("rg_norm_g_2", 2), ("hg_norm_g_2", 2), ("m2_norm_g_2", 2)],
            [("rg_conv_w_2", 8), ("rg_conv_b_2", 2), ("rg_ba_2", 2), ("rg_bx_2", 2), ("rg_lambda_2", 2),
             ("hg_lower_bounds_2", 2), ("m2_conv_w_2", 24), ("m2_conv_b_2", 6)]]
    k.cols = k.sb("feature_vectors", [P, 2, P])
    k.place = {}
    for r, group in enumerate(rows):
        at = 0
        for name, n in group:
            k.place[name] = (r, at)
            at += n
    k.cos = k.sb("cos", [P, TT, 8])
    k.sin = k.sb("sin", [P, TT, 8])
    k.neg_lambda = k.sb("neg_lambda", [P, 1])
    heads = ["gq_a", "gk_a", "gq_b", "gk_b", "g_kidx"]
    k.head_gain = k.sb("head_gains", [P, len(heads), 64])
    k.gain_of = {name: k.head_gain[:, i, :] for i, name in enumerate(heads)}
    lam_init = 0.8 - 0.6
    k.hold_units(weights)
    with ExitStack() as ctx:
        raw = k.sb("vector_rows", [P, 2, P], ctx=ctx)
        lam = k.sb("lam", [P, 4, 64], ctx=ctx)
        lam_sum = k.sb("lam_sum", [P, 2], ctx=ctx)
        pos_i = k.sb("pos_i", [P, TT], I32, ctx=ctx)
        pos = k.sb("pos", [P, TT], ctx=ctx)
        angle = k.sb("angle", [P, 2, TT, 8], ctx=ctx)
        turns = k.sb("turns", [P, 2, TT, 8], ctx=ctx)
        inv_freq = k.sb("inv_freq", [P, 8], ctx=ctx)
        small = 0
        with k.block() as block:
            @block.sync
            def _(sp):
                k.load_unit(sp, 0)

            @block.gpsimd
            def _(pool):
                k.pool.step(pool, pool.memset(k.ident[:, :], 0.0))
                k.pool.step(pool, pool.memset(k.causal[:, :], 0.0))
                k.pool.step(pool, pool.memset(k.strict[:, :], 0.0))
                k.pool.step(pool, pool.memset(k.ones[:, :], 1.0))
                k.pool.step(pool, pool.memset(raw[:, :, :], 0.0))
                k.pool.step(pool, pool.affine_select(out=k.ident[:, :], in_=k.ident[:, :], compare_op=ALU.not_equal,
                                                     fill=1.0, base=0, pattern=[[-1, P]], channel_multiplier=1))
                k.pool.step(pool, pool.affine_select(out=k.causal[:, :], in_=k.causal[:, :], compare_op=ALU.is_ge,
                                                     fill=MASKED, base=0, pattern=[[-1, P]], channel_multiplier=1))
                pool.affine_select(out=k.strict[:, :], in_=k.strict[:, :], compare_op=ALU.is_gt,
                                   fill=MASKED, base=0, pattern=[[-1, P]], channel_multiplier=1)\
                    .then_inc(k.pool_made.sem, 1)

            @block.scalar
            def _(act):
                n = 0
                act.dma_start(k.x[:, :, :], ins["x"][0].rearrange("(t p) d -> p t d", p=P))\
                   .then_inc(k.small_loaded.sem, 16)
                act.wait_ge(k.pool_made.sem, k.pool_made.at(1))
                for r, group in enumerate(rows):
                    for name, count in group:
                        a = ins[name]
                        if len(a.shape) == 3:
                            a = a.rearrange("a b c -> (a b) c")
                        src = a.rearrange("a (b c) -> (a b) c", c=P)
                        at = k.place[name][1]
                        act.dma_start(raw[at:at + count, r, :], src).then_inc(k.small_loaded.sem, 16)
                        n += 1
                for i, name in enumerate(heads):
                    act.dma_start(k.head_gain[:, i, :], ins[name][0].partition_broadcast(P))\
                       .then_inc(k.small_loaded.sem, 16)
                for i, name in enumerate(["lam_q1", "lam_k1", "lam_q2", "lam_k2"]):
                    act.dma_start(lam[:, i, :], ins[name][0].partition_broadcast(P)).then_inc(k.small_loaded.sem, 16)
                with nc.allow_non_contiguous_dma(reason="512 positions, once"):
                    act.dma_start(pos_i[:, :], ins["positions"][0].rearrange("(t p) -> p t", p=P))\
                       .then_inc(k.small_loaded.sem, 16)
                total = k.small_loaded.at(16 * (1 + n + len(heads) + 4 + 1))
                act.wait_ge(k.small_loaded.sem, total)
                act.activation(pos[:, :], pos_i[:, :], ACT.Copy).then_inc(k.act_made.sem, 1)
                act.wait_ge(k.dve_made.sem, k.dve_made.at(1))
                act.activation(lam_sum[:, :], lam_sum[:, :], ACT.Exp).then_inc(k.act_made.sem, 1)
                act.wait_ge(k.dve_made.sem, k.dve_made.at(2))
                act.activation(k.sin[:, :, :], angle[:, 0], ACT.Sin)
                act.activation(k.cos[:, :, :], angle[:, 1], ACT.Sin).then_inc(k.act_made.sem, 1)

            @block.vector
            def _(dve):
                dve.memset(k.eps[:, :], EPS)
                for i in range(8):
                    ins_ = dve.memset(inv_freq[:, i:i + 1], INV_FREQ[i])
                k.dve.step(dve, ins_)
                dve.wait_ge(k.act_made.sem, k.act_made.at(1))
                k.dve.step(dve, dve.tensor_tensor(lam[:, 0::2, :], lam[:, 0::2, :], lam[:, 1::2, :], ALU.mult))
                dve.reduce_sum(lam_sum[:, :], lam[:, 0::2, :], AX).then_inc(k.dve_made.sem, 1)
                k.dve.step(dve, dve.tensor_tensor(angle[:, 0], pos[:, :].unsqueeze(2).broadcast_to([P, TT, 8]),
                                                  inv_freq[:, :].unsqueeze(1).broadcast_to([P, TT, 8]), ALU.mult))
                k.dve.step(dve, dve.tensor_scalar(angle[:, 1], angle[:, 0], HALF_PI, None, ALU.add))
                k.dve.step(dve, dve.tensor_scalar(turns[:], angle[:], 1.0 / TWO_PI, ROUND, ALU.mult, ALU.add))
                k.dve.step(dve, dve.tensor_scalar(turns[:], turns[:], ROUND, None, ALU.subtract))
                for part in TWO_PI_PARTS:
                    k.dve.step(dve, dve.scalar_tensor_tensor(out=angle[:], in0=turns[:], scalar=-part, in1=angle[:],
                                                             op0=ALU.mult, op1=ALU.add))
                dve.tensor_scalar(angle[:], angle[:], -PI_BELOW, PI_BELOW, ALU.max, ALU.min)\
                   .then_inc(k.dve_made.sem, 1)
                dve.wait_ge(k.act_made.sem, k.act_made.at(2))
                k.dve.step(dve, dve.tensor_tensor(k.neg_lambda[:, :], lam_sum[:, 1:2], lam_sum[:, 0:1], ALU.subtract))
                k.dve.step(dve, dve.tensor_scalar(k.neg_lambda[:, :], k.neg_lambda[:, :], lam_init, None,
                                                  ALU.subtract))
        k.act_made.passed(3)
        k.dve_made.passed(2)
        k.pool_made.passed(1)
        k.small_loaded.passed(16 * (1 + sum(len(g) for g in rows) + len(heads) + 5))
        turn(k, [([raw[:, r, :]], k.cols[:, r, :], None) for r in range(2)])
    with k.block() as block:
        @block.sync
        def _(sp):
            k.load_unit(sp, 1)

        @block.scalar
        def _(act):
            k.round_unit(act, 0)

        @block.vector
        def _(dve):
            k.rest_of_unit(dve, 0)
            g_sub = k.col("g_sub_a", 0)
            k.dve.step(dve, dve.tensor_scalar(g_sub, g_sub, 1.0 - lam_init, None, ALU.mult))


PI = 3.141592653589793
TWO_PI = 2 * PI
HALF_PI = PI / 2
PI_BELOW = 3.1415925
ROUND = 12582912.0
TWO_PI_PARTS = [6.28125, 0.0019353071795864769]
INV_FREQ = [float(500000.0 ** (-(2 * i) / 16)) for i in range(8)]


def cross(k, i):
    with ExitStack() as ctx:
        memT = k.sb("memT", [P, KT, MEM], ctx=ctx)
        with ExitStack() as inner:
            mem = k.sb("mem", [P, MEM // P, D], ctx=inner)
            with k.block() as block:
                @block.scalar
                def _(act):
                    act.dma_start(mem[:, :, :], k.ins["mem"][0].rearrange("(t p) d -> p t d", p=P))\
                       .then_inc(k.small_loaded.sem, 16)
                    act.wait_ge(k.small_loaded.sem, k.small_loaded.at(16))
            k.small_loaded.passed(16)
            norm_and_turn(k, mem, MEM // P, k.col("g_mem", i * KT, KT), memT)
        norm_and_turn(k, k.x, TT, k.col("g_xattn", i * KT, KT), k.hT)
        q = k.sb("cross_q", [P, TT, 512], ctx=ctx)
        kk = k.sb("cross_k", [P, MEM // P, 512], ctx=ctx)
        v = k.sb("cross_v", [P, MEM // P, 512], ctx=ctx)
        u = k.consumed
        outs = [q, kk, v]
        projection = ctx.enter_context(ExitStack())
        tokens = parts_of(k, k.hT, projection)
        memory = parts_of(k, memT, projection)
        project(k, [{"unit": u, "banks": token_banks(k, u, tokens)},
                    {"unit": u + 1, "banks": token_banks(k, u + 1, memory, tiles=MEM // P), "inputs_before": KT},
                    {"unit": u + 2, "banks": token_banks(k, u + 2, memory, tiles=MEM // P), "inputs_before": KT}],
                lambda dve, j, b, bank: dve.tensor_copy(outs[j][:, b, :], bank), [tokens, memory])
        projection.close()
        qT = k.sb("cross_qT", [P, 4, S], ctx=ctx)
        kT = k.sb("cross_kT", [P, 4, MEM], ctx=ctx)
        o = k.sb("cross_o", [P, TT, 512], ctx=ctx)
        per_head = [by_head(a[:, :, :], P) for a in (q, kk)]
        heads_norm(k, [(a, a, None) for a in per_head])
        turn(k, [([q[:, t, h * P:(h + 1) * P] for t in range(TT)], qT[:, h, :], k.col("gq_x", i)) for h in range(4)]
             + [([kk[:, t, h * P:(h + 1) * P] for t in range(MEM // P)], kT[:, h, :], k.col("gk_x", i))
                for h in range(4)])
        attention(k, [{"q": [qT[:, h, t * P:(t + 1) * P]], "k": [kT[:, h, :]], "keys": MEM, "mask": None,
                       "v": [v[:, m, h * P:(h + 1) * P] for m in range(MEM // P)],
                       "out": o[:, t, h * P:(h + 1) * P]} for h in range(4) for t in range(TT)],
                  float(P) ** -0.5)
        oT = qT
        turn(k, [([o[:, t, h * P:(h + 1) * P] for t in range(TT)], oT[:, h, :], None) for h in range(4)])
        project_out(k, oT, ktiles=4)


def even_mixer(k):
    norm_and_turn(k, k.x, TT, k.col("g_mix", 0, KT), k.hT)
    with ExitStack() as ctx:
        proj = k.sb("even_proj", [P, TT, sum(EVEN_UNITS)], ctx=ctx)
        starts = [sum(EVEN_UNITS[:i]) for i in range(len(EVEN_UNITS) + 1)]
        u = k.consumed
        with ExitStack() as inner:
            tokens = parts_of(k, k.hT, inner)
            project(k, [{"unit": u + j, "banks": token_banks(k, u + j, tokens)} for j in range(len(EVEN_UNITS))],
                    lambda dve, j, b, bank: dve.tensor_copy(proj[:, b, starts[j]:starts[j + 1]], bank), [tokens])
        qa, ka, va, qb = (proj[:, :, j * 512:(j + 1) * 512] for j in range(4))
        ckv, qi, ki = proj[:, :, 2048:2304], proj[:, :, 2304:2560], proj[:, :, 2560:2624]
        wi = proj[:, :, 2624:2628]
        kvb = k.sb("even_kvb", [P, TT, 2, 512], ctx=ctx)
        kb, vb = kvb[:, :, 0, :], kvb[:, :, 1, :]
        ckvT = k.hT[:, 0:2, :]
        heads_norm(k, [(by_head(ckv, 256), by_head(ckv, 256), None)])
        turn(k, [([ckv[:, t, c * P:(c + 1) * P] for t in range(TT)], ckvT[:, c, :], k.col("g_kv_b", c))
                 for c in range(2)])
        u = k.consumed
        with ExitStack() as inner:
            latent = parts_of(k, ckvT, inner)
            project(k, [{"unit": u, "banks": token_banks(k, u, latent, col0=0, cols=512)},
                        {"unit": u, "banks": token_banks(k, u, latent, col0=512, cols=512)}],
                    lambda dve, j, b, bank: dve.tensor_copy(kvb[:, b, j, :], bank), [latent])
        heads = [by_head(a, 64) for a in (qa, ka, qb, kb, ki)]
        heads_norm(k, [(a, a, k.gain_of[g]) for a, g in zip(heads, ("gq_a", "gk_a", "gq_b", "gk_b", "g_kidx"))])
        rope(k, heads + [by_head(qi, 64)])
        inner = ctx.enter_context(ExitStack())
        ki2 = proj[:, :, 2048:2048 + P]
        with k.block() as block:
            @block.vector
            def _(dve):
                dve.tensor_copy(ki2[:, :, 0:64], ki)
                k.dve.step(dve, dve.tensor_copy(ki2[:, :, 64:128], ki))
        qaT, kaT = k.hT[:, 0:4, :], k.hT[:, 4:8, :]
        qbT = k.sb("qbT", [P, 4, S], ctx=inner)
        kbT = k.sb("kbT", [P, 4, S], ctx=inner)
        qiT = k.sb("qiT", [P, 2, S], ctx=inner)
        kiT = k.sb("kiT", [P, 1, S], ctx=inner)
        turn(k, [([src[:, t, c * P:(c + 1) * P] for t in range(TT)], dst[:, c, :], None)
                 for src, dst in ((qa, qaT), (ka, kaT), (qb, qbT), (kb, kbT), (qi, qiT), (ki2, kiT))
                 for c in range(dst.shape[1])])
        unselected = k.sb("unselected", [P, TT, S], ctx=inner)
        select_keys(k, qiT, kiT, wi, unselected, ka)
        out_a, out_b = proj[:, :, 0:512], proj[:, :, 1536:2048]

        def half(a, h, cols):
            return a[64 * (h % 2):64 * (h % 2) + 64, h // 2, cols]

        attention(k, [{"q": [half(qaT, 2 * h + c, slice(t * P, (t + 1) * P)) for c in range(2)],
                       "k": [half(kaT, 2 * h + c, slice(0, (t + 1) * P)) for c in range(2)],
                       "keys": (t + 1) * P, "mask": (k.causal[:, :], t * P),
                       "v": [va[:, m, h * P:(h + 1) * P] for m in range(t + 1)],
                       "out": out_a[:, t, h * P:(h + 1) * P]} for h in range(4) for t in range(TT)],
                  64 ** -0.5, neg_lambda=k.neg_lambda[:, 0:1], probs=kb.rearrange("p (u c) s -> p u c s", u=2))
        attention(k, [{"q": [half(qbT, h, slice(t * P, (t + 1) * P))],
                       "k": [half(kbT, h, slice(0, (t + 1) * P))],
                       "keys": (t + 1) * P, "mask": (unselected[:, t, 0:(t + 1) * P], 0),
                       "v": [vb[:, m, h * 64:(h + 1) * 64] for m in range(t + 1)],
                       "out": out_b[:, t, h * 64:(h + 1) * 64]} for h in range(8) for t in range(TT)],
                  64 ** -0.5, probs=kb.rearrange("p (u c) s -> p u c s", u=2))
        inner.close()
        heads_norm(k, [(by_head(out_a, P), by_head(out_a, P), None)])
        turn(k, [([src[:, t, c * P:(c + 1) * P] for t in range(TT)], k.hT[:, 4 * i + c, :],
                  k.col("g_sub_a", 0) if i == 0 else None)
                 for i, src in enumerate((out_a, out_b)) for c in range(4)])
    project_out(k, k.hT)


def select_keys(k, qiT, kiT, wi, unselected, relu):
    with ExitStack() as ctx:
        score = k.sb("index_score", [P, S], ctx=ctx)
        w = k.sb("index_weight", [P, TT, 4], ctx=ctx)
        best = k.sb("index_best", [P, 8], ctx=ctx)
        with k.block() as block:
            @block.tensor
            def _(pe):
                for t in range(TT):
                    if t >= 2:
                        pe.wait_ge(k.act_made.sem, k.act_made.at(t - 1))
                    for h in range(4):
                        rows = slice(64 * (h % 2), 64 * (h % 2) + 64)
                        ins = pe.matmul(k.psum[:, 4 * (t % 2) + h, 0:(t + 1) * P], qiT[rows, h // 2, t * P:(t + 1) * P],
                                        kiT[rows, 0, 0:(t + 1) * P], start=True, stop=True)
                    ins.then_inc(k.pe_made.sem, 1)

            @block.scalar
            def _(act):
                for t in range(TT):
                    act.wait_ge(k.pe_made.sem, k.pe_made.at(t + 1))
                    if t >= 1:
                        act.wait_ge(k.dve_made.sem, k.dve_made.at(t))
                    n = (t + 1) * P
                    act.activation(relu[:, :, 0:n], k.psum[:, 4 * (t % 2):4 * (t % 2) + 4, 0:n], ACT.Relu)\
                       .then_inc(k.act_made.sem, 1)

            @block.vector
            def _(dve):
                k.dve.step(dve, dve.tensor_scalar(w[:, :, :], wi, (4 * 64) ** -0.5, None, ALU.mult))
                for t in range(TT):
                    n = (t + 1) * P
                    dve.wait_ge(k.act_made.sem, k.act_made.at(t + 1))
                    s = score[:, 0:n]
                    k.dve.step(dve, dve.tensor_scalar(s, relu[:, 0, 0:n], w[:, t, 0:1], None, ALU.mult))
                    for h in range(1, 4):
                        k.dve.step(dve, dve.scalar_tensor_tensor(out=s, in0=relu[:, h, 0:n], scalar=w[:, t, h:h + 1],
                                                                 in1=s, op0=ALU.mult, op1=ALU.add))
                    diagonal = score[:, t * P:n]
                    k.dve.step(dve, dve.tensor_tensor(diagonal, diagonal, k.causal[:, :], ALU.add))
                    dve.tensor_copy(unselected[:, t, t * P:n], k.causal[:, :]).then_inc(k.dve_made.sem, 1)
                    if n > TOPK:
                        for r in range(TOPK // 8):
                            k.dve.step(dve, dve.max(best[:, :], s))
                            k.dve.step(dve, dve.match_replace(s, best[:, :], s, TAKEN))
                        dve.wait_ge(k.dve_made.sem, k.dve_made.at(t + 1))
                        k.dve.step(dve, dve.tensor_scalar(unselected[:, t, 0:n], s, TAKEN / 2, MASKED,
                                                          ALU.is_gt, ALU.mult))
    k.pe_made.passed(TT)
    k.act_made.passed(TT)
    k.dve_made.passed(TT)
def odd_mixer(k):
    norm_and_turn(k, k.x, TT, k.col("g_mix", KT, KT), k.hT)
    PAD = 16
    with ExitStack() as ctx:
        gb = k.sb("odd_gb", [P, 4, S], ctx=ctx)
        gc = k.sb("odd_gc", [P, 4, S], ctx=ctx)
        hc = k.sb("odd_hc", [P, 4, PAD + S], ctx=ctx)
        zd = k.sb("odd_zd", [P, 4, PAD + S], ctx=ctx)
        sums = k.sb("odd_sums", [P, 2, PAD + S], ctx=ctx)
        acc = k.sb("odd_acc", [P, S], ctx=ctx)
        wp = k.sb("odd_w_pool", [P, 4, P], ctx=ctx)
        with k.block() as block:
            @block.gpsimd
            def _(pool):
                pool.memset(sums[:, :, 0:PAD], 0.0)
                pool.memset(hc[:, :, 0:PAD], 0.0)
                k.pool.step(pool, pool.memset(zd[:, :, 0:PAD], 0.0))

            @block.scalar
            def _(act):
                act.dma_start(wp[:, :, :], k.ins["w_pool"][0].rearrange("g c d -> c g d"))\
                   .then_inc(k.small_loaded.sem, 16)
                act.wait_ge(k.small_loaded.sem, k.small_loaded.at(16))
        k.small_loaded.passed(16)
        u = k.consumed
        outs = [gb[:, :, :], gc[:, :, :], hc[:, :, PAD:], zd[:, :, PAD:]]
        with ExitStack() as inner:
            tokens = parts_of(k, k.hT, inner)
            project(k, [{"unit": u + j, "banks": feature_banks(k, u + j, tokens)} for j in range(4)],
                    lambda dve, j, b, bank: dve.tensor_copy(outs[j][:, b, :], bank), [tokens])
        mixT = k.hT
        with k.block() as block:
            @block.vector
            def _(dve):
                k.dve.step(dve, dve.tensor_tensor(hc[:, :, PAD:], hc[:, :, PAD:], gc[:, :, :], ALU.mult))
                for g in range(4):
                    k.dve.step(dve, dve.tensor_scalar(acc[:, :], hc[:, g, PAD - 2:PAD - 2 + S],
                                                      k.col("conv_w", g), None, ALU.mult))
                    for tap in (1, 2):
                        at = PAD - 2 + tap
                        k.dve.step(dve, dve.scalar_tensor_tensor(out=acc[:, :], in0=hc[:, g, at:at + S],
                                                                 scalar=k.col("conv_w", 4 * tap + g), in1=acc[:, :],
                                                                 op0=ALU.mult, op1=ALU.add))
                    k.dve.step(dve, dve.tensor_tensor(mixT[:, g, :], acc[:, :], gb[:, g, :], ALU.mult))
                for g in range(4):
                    src = zd[:, g, :]
                    for r in range(g + 1):
                        dst = sums[:, r % 2, :]
                        back = 2 ** r
                        k.dve.step(dve, dve.tensor_tensor(dst[:, PAD:], src[:, PAD:], src[:, PAD - back:PAD - back + S],
                                                          ALU.add))
                        src = dst
                    window = 2 ** (g + 1)
                    for t in range(window - 1):
                        k.dve.step(dve, dve.tensor_scalar(src[:, PAD + t:PAD + t + 1], src[:, PAD + t:PAD + t + 1],
                                                          window / (t + 1), None, ALU.mult))
                    dve.scalar_tensor_tensor(out=gb[:, g, :], in0=src[:, PAD:], scalar=1.0 / window,
                                             in1=zd[:, g, PAD:], op0=ALU.mult, op1=ALU.subtract)\
                       .then_inc(k.dve_made.sem, 1)
                    dve.wait_ge(k.dve_made.sem, k.dve_made.at(g + 1))
                for g in range(4):
                    dve.wait_ge(k.pe_made.sem, k.pe_made.at(g + 1))
                    k.dve.step(dve, dve.tensor_scalar(mixT[:, 4 + g, :], k.psum[:, g, :], k.col("pool_scale", g),
                                                      None, ALU.mult))

            @block.tensor
            def _(pe):
                for g in range(4):
                    pe.wait_ge(k.dve_made.sem, k.dve_made.at(g + 1))
                    pe.matmul(k.psum[:, g, :], wp[:, g, :], gb[:, g, :], start=True, stop=True)\
                      .then_inc(k.pe_made.sem, 1)
        k.dve_made.passed(4)
        k.pe_made.passed(4)
    project_out(k, k.hT)


PAD = 4


def stick_breaking(k, units, scale):
    n = len(units)
    with ExitStack() as ctx:
        probs = k.sb("sb_probs", [P, 2, 1, 512], ctx=ctx)
        attnT = k.sb("sb_attnT", [P, 2, 4, P], ctx=ctx)
        soft = k.sb("sb_soft", [P, 2, 512], ctx=ctx)
        pos = k.sb("sb_pos", [P, 512], ctx=ctx)
        run = k.sb("sb_run", [P, 2, 1 + 512], ctx=ctx)
        log_a = k.sb("sb_log_a", [P, 2, 512], ctx=ctx)
        neg_total = k.sb("sb_neg_total", [P, 2, 1], ctx=ctx)
        with k.block() as block:
            @block.tensor
            def _(pe):
                attention_products(k, pe, units, probs, attnT, 1)

            @block.scalar
            def _(act):
                def softs(u):
                    w = units[u]["keys"]
                    s = soft[:, u % 2, 0:w]
                    act.wait_ge(k.scores_ready.sem, k.scores_ready.at(u + 1))
                    if u >= 2:
                        act.wait_ge(k.negmax_ready.sem, k.negmax_ready.at(u - 1))
                    k.act.step(act, act.activation(s, score_bank(k, units, u, 0), ACT.Abs, scale=scale))
                    k.act.step(act, act.activation(s, s, ACT.Exp, scale=-1.0))
                    act.activation(s, s, ACT.Ln, bias=1.0).then_inc(k.act_made.sem, 1)

                softs(0)
                softs(1)
                for u in range(n):
                    w = units[u]["keys"]
                    act.wait_ge(k.negmax_ready.sem, k.negmax_ready.at(u + 1))
                    if u >= 2:
                        act.wait_ge(k.attn_turned.sem, k.attn_turned.at(u - 1))
                    act.activation(probs[:, u % 2, 0, 0:w], log_a[:, u % 2, 0:w], ACT.Exp,
                                   bias=neg_total[:, u % 2, :]).then_inc(k.probs_ready.sem, 1)
                    if u + 2 < n:
                        softs(u + 2)

            @block.vector
            def _(dve):
                k.dve.step(dve, dve.memset(run[:, :, 0:1], 0.0))

                def logs(u):
                    w = units[u]["keys"]
                    z = score_bank(k, units, u, 0)
                    r = run[:, u % 2, :]
                    dve.wait_ge(k.act_made.sem, k.act_made.at(u + 1))
                    if u >= 2:
                        dve.wait_ge(k.probs_ready.sem, k.probs_ready.at(u - 1))
                    k.dve.step(dve, dve.tensor_scalar(pos[:, 0:w], z, scale, 0.0, ALU.mult, ALU.max))
                    k.dve.step(dve, dve.tensor_tensor_scan(r[:, 1:1 + w], pos[:, 0:w], soft[:, u % 2, 0:w], 0.0,
                                                           ALU.add, ALU.add))
                    k.dve.step(dve, dve.scalar_tensor_tensor(out=log_a[:, u % 2, 0:w], in0=z, scalar=scale,
                                                             in1=r[:, 0:w], op0=ALU.mult, op1=ALU.add))
                    dve.tensor_scalar(neg_total[:, u % 2, :], r[:, w:w + 1], -1.0, None, ALU.mult)\
                       .then_inc(k.negmax_ready.sem, 1)

                logs(0)
                logs(1)
                for u in range(n):
                    save_attnT(k, dve, units, attnT, u)
                    if u >= 1:
                        save_out(k, dve, units, None, u - 1)
                    if u + 2 < n:
                        logs(u + 2)
                save_out(k, dve, units, None, n - 1)
    for s in (k.scores_ready, k.negmax_ready, k.attn_turned, k.attnT_ready, k.out_ready, k.out_saved, k.act_made,
              k.probs_ready):
        s.passed(n)


def conv4(k, dve, x, c, weight, bias, tiles, out):
    first = PAD - 3
    k.dve.step(dve, dve.tensor_scalar(out, x[:, c, first:first + S], k.col(weight, c), k.col(bias, c),
                                      ALU.mult, ALU.add))
    for tap in (1, 2, 3):
        at = first + tap
        k.dve.step(dve, dve.scalar_tensor_tensor(out=out, in0=x[:, c, at:at + S], scalar=k.col(weight, tiles * tap + c),
                                                 in1=out, op0=ALU.mult, op1=ALU.add))


def log1p_series(k, dve, e, w, sq, out):
    k.dve.step(dve, dve.tensor_scalar(w, e, 2.0, None, ALU.add))
    k.dve.step(dve, dve.reciprocal(w, w))
    k.dve.step(dve, dve.tensor_tensor(w, w, e, ALU.mult))
    k.dve.step(dve, dve.tensor_tensor(sq, w, w, ALU.mult))
    k.dve.step(dve, dve.tensor_scalar(out, sq, 2.0 / 17, 2.0 / 15, ALU.mult, ALU.add))
    for odd in (13, 11, 9, 7, 5, 3, 1):
        k.dve.step(dve, dve.tensor_tensor(out, out, sq, ALU.mult))
        k.dve.step(dve, dve.tensor_scalar(out, out, 2.0 / odd, None, ALU.add))
    k.dve.step(dve, dve.tensor_tensor(out, out, w, ALU.mult))


def feature_norm(k, o, ones, width, gain, dst, sq, rms, factor=None):
    both = width == 2 * P
    with k.block() as block:
        @block.vector
        def _(dve):
            dve.tensor_tensor(sq[:, :, :], o[:, :, :], o[:, :, :], ALU.mult).then_inc(k.dve_made.sem, 1)
            dve.wait_ge(k.act_made.sem, k.act_made.at(2))
            k.dve.step(dve, dve.reciprocal(rms[:, :, :], rms[:, :, :]))
            for c in range(2):
                ins = dve.scalar_tensor_tensor(out=dst[:, c, :], in0=o[:, c, :], scalar=k.col(gain, c),
                                               in1=rms[:, c, :], op0=ALU.mult, op1=ALU.mult)
            k.dve.step(dve, ins)
            if factor is not None:
                k.dve.step(dve, dve.tensor_tensor(dst, dst, factor, ALU.mult))

        @block.tensor
        def _(pe):
            pe.wait_ge(k.dve_made.sem, k.dve_made.at(1))
            for c in range(2):
                if both:
                    pe.matmul(k.psum[:, c, :], ones, sq[:, 0, :], start=True, stop=False)
                    ins = pe.matmul(k.psum[:, c, :], ones, sq[:, 1, :], start=False, stop=True)
                else:
                    ins = pe.matmul(k.psum[:, c, :], ones, sq[:, c, :], start=True, stop=True)
                ins.then_inc(k.pe_made.sem, 1)

        @block.scalar
        def _(act):
            for c in range(2):
                act.wait_ge(k.pe_made.sem, k.pe_made.at(c + 1))
                act.activation(rms[:, c, :], k.psum[:, c, :], ACT.Sqrt, bias=k.eps[:, 0:1], scale=1.0 / width)\
                   .then_inc(k.act_made.sem, 1)
    k.dve_made.passed(1)
    k.pe_made.passed(2)
    k.act_made.passed(2)


def rg_lru(k, x, gate, dst):
    with ExitStack() as ctx:
        wbd = k.sb("rg_weights", [P, 2, 2, P], ctx=ctx)
        xc = k.sb("rg_xc", [P, 2, S], ctx=ctx)
        r = k.sb("rg_r", [P, 2, S], ctx=ctx)
        ig = k.sb("rg_ig", [P, 2, S], ctx=ctx)
        a = k.sb("rg_a", [P, 2, S], ctx=ctx)
        th = k.sb("rg_tanh", [P, 2, S], ctx=ctx)
        mult = k.sb("rg_mult", [P, 2, S], ctx=ctx)
        g3 = k.sb("rg_gelu", [P, 2, S], ctx=ctx)
        tiny = k.sb("rg_tiny", [P, 6, 2], ctx=ctx)
        lam = k.col("rg_lambda_2", 0, 2)
        with k.block() as block:
            @block.gpsimd
            def _(pool):
                pool.memset(wbd[:], 0.0).then_inc(k.pool_made.sem, 1)

            @block.sync
            def _(sp):
                sp.wait_ge(k.pool_made.sem, k.pool_made.at(1))
                for i, name in enumerate(("rg_wa_2", "rg_wx_2")):
                    for c in range(2):
                        for n in range(2):
                            at = slice(64 * n, 64 * n + 64)
                            sp.dma_start(wbd[at, i, c, at], k.ins[name][0, 2 * c + n]).then_inc(k.small_loaded.sem, 16)

            @block.vector
            def _(dve):
                for c in range(2):
                    conv4(k, dve, x, c, "rg_conv_w_2", "rg_conv_b_2", 2, xc[:, c, :])
                dve.tensor_scalar(tiny[:, 0, :], lam, -1.0, None, ALU.mult).then_inc(k.dve_made.sem, 1)
                k.dve.step(dve, dve.tensor_tensor(g3[:, :, :], gate[:, :, :], gate[:, :, :], ALU.mult))
                k.dve.step(dve, dve.tensor_scalar(g3[:, :, :], g3[:, :, :], 0.044715, 1.0, ALU.mult, ALU.add))
                k.dve.step(dve, dve.tensor_tensor(g3[:, :, :], g3[:, :, :], gate[:, :, :], ALU.mult))
                dve.wait_ge(k.act_made.sem, k.act_made.at(1))
                log1p_series(k, dve, tiny[:, 1, :], tiny[:, 2, :], tiny[:, 3, :], tiny[:, 4, :])
                k.dve.step(dve, dve.tensor_scalar(tiny[:, 5, :], tiny[:, 0, :], 0.0, None, ALU.max))
                k.dve.step(dve, dve.tensor_tensor(tiny[:, 5, :], tiny[:, 5, :], tiny[:, 4, :], ALU.add))
                dve.tensor_scalar(tiny[:, 5, :], tiny[:, 5, :], -8.0, None, ALU.mult).then_inc(k.dve_made.sem, 1)
                dve.wait_ge(k.act_made.sem, k.act_made.at(2))
                k.dve.step(dve, dve.tensor_scalar(mult[:, :, :], th[:, :, :], -1.0, 1.0, ALU.mult, ALU.add))
                k.dve.step(dve, dve.reciprocal(mult[:, :, :], mult[:, :, :]))
                dve.scalar_tensor_tensor(out=mult[:, :, :], in0=th[:, :, :], scalar=-2.0, in1=mult[:, :, :],
                                         op0=ALU.mult, op1=ALU.mult).then_inc(k.dve_made.sem, 1)
                k.dve.step(dve, dve.tensor_tensor(xc[:, :, :], xc[:, :, :], ig[:, :, :], ALU.mult))
                dve.wait_ge(k.act_made.sem, k.act_made.at(3))
                k.dve.step(dve, dve.memset(mult[:, :, 0:1], 1.0))
                k.dve.step(dve, dve.tensor_tensor(xc[:, :, :], xc[:, :, :], mult[:, :, :], ALU.mult))
                for c in range(2):
                    ins = dve.tensor_tensor_scan(r[:, c, :], a[:, c, :], xc[:, c, :], 0.0, ALU.mult, ALU.add)
                k.dve.step(dve, ins)
                k.dve.step(dve, dve.tensor_tensor(r[:, :, :], r[:, :, :], gate[:, :, :], ALU.mult))
                k.dve.step(dve, dve.tensor_scalar(g3[:, :, :], g3[:, :, :], 0.5, 0.5, ALU.mult, ALU.add))
                k.dve.step(dve, dve.tensor_tensor(r[:, :, :], r[:, :, :], g3[:, :, :], ALU.mult))

            @block.tensor
            def _(pe):
                pe.wait_ge(k.dve_made.sem, k.dve_made.at(1))
                pe.wait_ge(k.small_loaded.sem, k.small_loaded.at(16 * 8))
                for i in range(2):
                    for c in range(2):
                        ins = pe.matmul(k.psum[:, 2 * i + c, :], wbd[:, i, c, :], xc[:, c, :], start=True, stop=True)
                ins.then_inc(k.pe_made.sem, 1)

            @block.scalar
            def _(act):
                act.wait_ge(k.dve_made.sem, k.dve_made.at(1))
                k.act.step(act, act.activation(tiny[:, 1, :], tiny[:, 0, :], ACT.Abs))
                act.activation(tiny[:, 1, :], tiny[:, 1, :], ACT.Exp, scale=-1.0).then_inc(k.act_made.sem, 1)
                act.wait_ge(k.pe_made.sem, k.pe_made.at(1))
                for c in range(2):
                    act.activation(r[:, c, :], k.psum[:, c, :], ACT.Sigmoid, bias=k.col("rg_ba_2", c))
                    ins = act.activation(ig[:, c, :], k.psum[:, 2 + c, :], ACT.Sigmoid, bias=k.col("rg_bx_2", c))
                k.act.step(act, ins)
                act.wait_ge(k.dve_made.sem, k.dve_made.at(2))
                for c in range(2):
                    act.activation(th[:, c, :], r[:, c, :], ACT.Tanh, scale=tiny[:, 5, c:c + 1])
                act.activation(g3[:, :, :], g3[:, :, :], ACT.Tanh, scale=0.7978845608028654)
                for c in range(2):
                    ins = act.activation(a[:, c, :], r[:, c, :], ACT.Exp, scale=tiny[:, 5, c:c + 1])
                ins.then_inc(k.act_made.sem, 1)
                act.wait_ge(k.dve_made.sem, k.dve_made.at(3))
                act.activation(mult[:, :, :], mult[:, :, :], ACT.Sqrt).then_inc(k.act_made.sem, 1)
        k.dve_made.passed(3)
        k.act_made.passed(3)
        k.pe_made.passed(1)
        k.pool_made.passed(1)
        k.small_loaded.passed(16 * 8)
        feature_norm(k, r, k.ones[:, :], 256, "rg_norm_g_2", dst, a, th)


def hgrn2(k, q, f, v, g, dst, scratch):
    with ExitStack() as ctx:
        key, state, read = scratch
        drive = v
        values = parts_of(k, v, ctx)
        pick = k.sb("hg_pick", [P, 3 * 64], ctx=ctx)
        pair = k.sb("hg_pair", [P, P], ctx=ctx)
        spread = k.sb("hg_spread", [P, 64, P], F32R, ctx=ctx)
        lb = k.sb("hg_lb", [P, 3, 2], ctx=ctx)
        with k.block() as block:
            @block.gpsimd
            def _(pool):
                k.pool.step(pool, pool.memset(pick[:, :], 0.0))
                k.pool.step(pool, pool.memset(pair[:, :], 0.0))
                pool.memset(pair[0:64, 0:64], 1.0)
                pool.memset(pair[64:P, 64:P], 1.0)
                pool.memset(pick[0:64, 63:64], 1.0)
                k.pool.step(pool, pool.memset(pick[64:P, 127:P], 1.0))

            @block.vector
            def _(dve):
                src = k.ident[:, :].rearrange("p (h v) -> p v h", h=2).unsqueeze(3).broadcast_to([P, 64, 2, 64])
                dve.tensor_copy(spread[:, :, :].rearrange("p v (h m) -> p v h m", h=2), src)
                dve.wait_ge(k.input_rounded.sem, k.input_rounded.at(1))
                values.rest(dve)
                x = k.col("hg_lower_bounds_2", 0, 2)
                dve.tensor_tensor(lb[:, 0, :], x, x, ALU.subtract).then_inc(k.dve_made.sem, 1)
                dve.wait_ge(k.act_made.sem, k.act_made.at(1))
                k.dve.step(dve, dve.reciprocal(lb[:, 1, :], lb[:, 0, :]))
                k.dve.step(dve, dve.tensor_tensor(lb[:, 0, :], lb[:, 0, :], lb[:, 1, :], ALU.mult))
                k.dve.step(dve, dve.tensor_tensor(lb[:, 1, :], lb[:, 0, :], lb[:, 0, :], ALU.subtract))
                k.dve.step(dve, dve.tensor_scalar(lb[:, 2, :], lb[:, 1, :], -1.0, 1.0, ALU.mult, ALU.add))
                for c in range(2):
                    ins = dve.tensor_scalar(f[:, c, :], f[:, c, :], lb[:, 2, c:c + 1], lb[:, 1, c:c + 1],
                                            ALU.mult, ALU.add)
                k.dve.step(dve, ins)
                k.dve.step(dve, dve.tensor_scalar(key[:, :, :], f[:, :, :], -1.0, 1.0, ALU.mult, ALU.add))
                k.dve.step(dve, dve.tensor_tensor(q[:, :, :], q[:, :, :], read, ALU.mult))
                dve.wait_ge(k.act_made.sem, k.act_made.at(2))
                k.dve.step(dve, dve.tensor_tensor(g[:, :, :], g[:, :, :], state[:, :, :], ALU.mult))

            @block.scalar
            def _(act):
                values.round(act).then_inc(k.input_rounded.sem, 1)
                act.wait_ge(k.dve_made.sem, k.dve_made.at(1))
                act.activation(lb[:, 0, :], lb[:, 0, :], ACT.Exp)
                act.activation(f[:, :, :], f[:, :, :], ACT.Sigmoid)
                act.activation(read, q[:, :, :], ACT.Sigmoid).then_inc(k.act_made.sem, 1)
                act.activation(state[:, :, :], g[:, :, :], ACT.Sigmoid).then_inc(k.act_made.sem, 1)
        k.dve_made.passed(1)
        k.act_made.passed(2)
        k.input_rounded.passed(1)
        n = 2 * 64
        with k.block() as block:
            @block.tensor
            def _(pe):
                def spread_values(i):
                    c, w = divmod(i, 64)
                    if i >= 2:
                        pe.wait_ge(k.dve_made.sem, k.dve_made.at(i - 1))
                    pe.matmul(k.psum[:, i % 2, :], spread[:, w, :], values.high[:, c, :], start=True, stop=False)
                    pe.matmul(k.psum[:, i % 2, :], spread[:, w, :], values.low[:, c, :], start=False, stop=True)\
                      .then_inc(k.pe_made.sem, 1)

                def gather(i):
                    c, w = divmod(i, 64)
                    pe.wait_ge(k.pool_made.sem, k.pool_made.at(i + 1))
                    pe.matmul(k.psum[:, 2 + c, :], pick[:, 63 - w:63 - w + P], read[:, i % 2, :],
                              start=(w == 0), stop=(w == 63)).then_inc(k.out_ready.sem, 1)

                spread_values(0)
                spread_values(1)
                for i in range(n):
                    if i + 2 < n:
                        spread_values(i + 2)
                    gather(i)

            @block.vector
            def _(dve):
                for i in range(n):
                    c = i // 64
                    dve.wait_ge(k.pe_made.sem, k.pe_made.at(i + 1))
                    if i >= 2:
                        dve.wait_ge(k.attn_ready.sem, k.attn_ready.at(i - 1))
                    dve.tensor_tensor(drive[:, i % 2, :], k.psum[:, i % 2, :], key[:, c, :], ALU.mult)\
                       .then_inc(k.dve_made.sem, 1)
                    dve.wait_ge(k.dve_made.sem, k.dve_made.at(i + 1))
                    if i >= 2:
                        dve.wait_ge(k.pool_made.sem, k.pool_made.at(i - 1))
                    dve.tensor_tensor_scan(state[:, i % 2, :], f[:, c, :], drive[:, i % 2, :], 0.0,
                                           ALU.mult, ALU.add).then_inc(k.attn_ready.sem, 1)

            @block.gpsimd
            def _(pool):
                for i in range(n):
                    pool.wait_ge(k.attn_ready.sem, k.attn_ready.at(i + 1))
                    if i >= 2:
                        pool.wait_ge(k.out_ready.sem, k.out_ready.at(i - 1))
                    pool.tensor_tensor(read[:, i % 2, :], state[:, i % 2, :], q[:, i // 64, :], ALU.mult)\
                        .then_inc(k.pool_made.sem, 1)

            @block.scalar
            def _(act):
                for c in range(2):
                    act.wait_ge(k.out_ready.sem, k.out_ready.at(64 * (c + 1)))
                    act.activation(dst[:, c, :], k.psum[:, 2 + c, :], ACT.Copy).then_inc(k.act_made.sem, 1)
        k.pe_made.passed(n)
        k.dve_made.passed(n)
        k.attn_ready.passed(n)
        k.pool_made.passed(n)
        k.out_ready.passed(n)
        k.act_made.passed(2)
        feature_norm(k, dst, pair[:, :], 64, "hg_norm_g_2", dst, drive, state, factor=g[:, :, :])


def mamba2(k, z, xbc, dt, out, w_all):
    with ExitStack() as ctx:
        sig = k.sb("m2_sig", [P, 6, S], ctx=ctx)
        four = k.sb("m2_four", [4, 6, S], ctx=ctx)
        small = k.sb("m2_small", [4, 4], ctx=ctx)
        sel = k.sb("m2_sel", [4, 4, P], ctx=ctx)
        dtcs = k.sb("m2_dt_cs", [P, TT, 2, 4], ctx=ctx)
        xs = k.sb("m2_xs", [P, TT, 256], ctx=ctx)
        xd = k.sb("m2_xd", [P, TT, 256], ctx=ctx)
        skip = k.sb("m2_skip", [P, 4], ctx=ctx)
        later = k.sb("m2_later", [P, P], ctx=ctx)
        e, w, sq, cs, zero, lg = (four[:, i, :] for i in range(6))
        with k.block() as block:
            @block.gpsimd
            def _(pool):
                k.pool.step(pool, pool.memset(later[:, :], 0.0))
                k.pool.step(pool, pool.affine_select(out=later[:, :], in_=later[:, :], compare_op=ALU.is_ge,
                                                     fill=MASKED, base=0, pattern=[[1, P]], channel_multiplier=-1))

            @block.sync
            def _(sp):
                sp.dma_start(skip[:, :], k.ins["m2_d_2"][0].partition_broadcast(P)).then_inc(k.small_loaded.sem, 16)
                sp.dma_start(small[:, 0:1], k.ins["m2_dt_bias_2"][0].unsqueeze(1)).then_inc(k.small_loaded.sem, 16)
                sp.dma_start(small[:, 1:2], k.ins["m2_a_log_2"][0].unsqueeze(1)).then_inc(k.small_loaded.sem, 16)
                sp.wait_ge(k.small_loaded.sem, k.small_loaded.at(48))

            @block.vector
            def _(dve):
                for c in range(6):
                    conv4(k, dve, xbc, c, "m2_conv_w_2", "m2_conv_b_2", 6, sig[:, c, :])
                    dve.tensor_copy(xbc[:, c, PAD:], sig[:, c, :]).then_inc(k.dve_made.sem, 1)
                dve.wait_ge(k.small_loaded.sem, k.small_loaded.at(48))
                k.dve.step(dve, dve.tensor_scalar(dt, dt, small[:, 0:1], None, ALU.add))
                dve.tensor_scalar(lg, dt, 0.0, None, ALU.max).then_inc(k.dve_made.sem, 1)
                dve.wait_ge(k.act_made.sem, k.act_made.at(1))
                log1p_series(k, dve, e, w, sq, zero)
                k.dve.step(dve, dve.tensor_tensor(dt, zero, lg, ALU.add))
                k.dve.step(dve, dve.tensor_scalar(e, dt, small[:, 2:3], -1.0, ALU.mult, ALU.mult))
                k.dve.step(dve, dve.memset(zero, 0.0))
                dve.tensor_tensor_scan(cs, e, zero, 0.0, ALU.add, ALU.add).then_inc(k.dve_made.sem, 1)
                k.dve.step(dve, dve.tensor_copy(sel[:, :, :], k.ident[0:4, 0:4].unsqueeze(2).broadcast_to([4, 4, P])))
                for c in range(6):
                    dve.wait_ge(k.act_made.sem, k.act_made.at(c + 2))
                    ins = dve.tensor_tensor(xbc[:, c, PAD:], xbc[:, c, PAD:], sig[:, c, :], ALU.mult)
                k.dve.step(dve, ins)

            @block.scalar
            def _(act):
                act.wait_ge(k.dve_made.sem, k.dve_made.at(7))
                k.act.step(act, act.activation(e, dt, ACT.Abs))
                act.activation(small[:, 2:3], small[:, 1:2], ACT.Exp)
                act.activation(e, e, ACT.Exp, scale=-1.0).then_inc(k.act_made.sem, 1)
                for c in range(6):
                    act.activation(sig[:, c, :], sig[:, c, :], ACT.Sigmoid).then_inc(k.act_made.sem, 1)
        k.dve_made.passed(8)
        k.act_made.passed(7)
        k.small_loaded.passed(48)
        turn(k, [([xbc[:, c, PAD + t * P:PAD + (t + 1) * P] for c in range(2)], xs[:, t, :], None) for t in range(TT)]
             + [([a[:, t * P:(t + 1) * P]], dtcs[:, t, i, :], None)
                for t in range(TT) for i, a in enumerate((dt, cs))])
        arg = k.sb("m2_decay", [P, 2, S], ctx=ctx)
        steps = [(h, s) for h in range(4) for s in range(TT)]
        B, C = (xbc[:, 2:4, PAD:], xbc[:, 4:6, PAD:])
        with k.block() as block:
            @block.tensor
            def _(pe):
                for h in range(4):
                    if h >= 1:
                        pe.wait_ge(k.dve_made.sem, k.dve_made.at(1 + TT * h))
                    for s in range(TT):
                        pe.matmul(k.psum[:, s, 0:S - s * P], B[:, h // 2, s * P:(s + 1) * P], C[:, h // 2, s * P:],
                                  start=True, stop=True)
                    pe.matmul(k.psum[:, 4, :], sel[:, h, :], cs, start=True, stop=True).then_inc(k.pe_made.sem, 1)
                    pe.wait_ge(k.dve_made.sem, k.dve_made.at(1 + TT * (h + 1)))
                    if h >= 2:
                        pe.wait_ge(k.out_saved.sem, k.out_saved.at(h - 1))
                    for t in range(TT):
                        for s in range(t + 1):
                            ins = pe.matmul(k.psum[:, 5 + h % 2, t * 64:(t + 1) * 64],
                                            w_all[:, s, (t - s) * P:(t - s + 1) * P], xd[:, s, h * 64:(h + 1) * 64],
                                            start=(s == 0), stop=(s == t))
                    ins.then_inc(k.out_ready.sem, 1)

            @block.vector
            def _(dve):
                for h in range(4):
                    cols = slice(h * 64, (h + 1) * 64)
                    ins = dve.tensor_tensor(xd[:, :, cols], xs[:, :, cols],
                                            dtcs[:, :, 0, h:h + 1].broadcast_to([P, TT, 64]), ALU.mult)
                ins.then_inc(k.dve_made.sem, 1)

                def exponents(i):
                    h, s = steps[i]
                    n = S - s * P
                    a = arg[:, i % 2, 0:n]
                    if s == 0:
                        dve.wait_ge(k.pe_made.sem, k.pe_made.at(h + 1))
                    if i >= 2:
                        dve.wait_ge(k.dve_made.sem, k.dve_made.at(1 + i - 1))
                    k.dve.step(dve, dve.tensor_scalar(a, k.psum[:, 4, s * P:], dtcs[:, s, 1, h:h + 1], None,
                                                      ALU.subtract))
                    dve.tensor_tensor(a[:, 0:P], a[:, 0:P], later[:, :], ALU.add).then_inc(k.scores_ready.sem, 1)

                def weights(i):
                    h, s = steps[i]
                    n = S - s * P
                    dve.wait_ge(k.probs_ready.sem, k.probs_ready.at(i + 1))
                    if s == 0 and h >= 1:
                        dve.wait_ge(k.out_ready.sem, k.out_ready.at(h))
                    dve.tensor_tensor(w_all[:, s, 0:n], arg[:, i % 2, 0:n], k.psum[:, s, 0:n], ALU.mult)\
                       .then_inc(k.dve_made.sem, 1)

                def save(h):
                    dve.wait_ge(k.out_ready.sem, k.out_ready.at(h + 1))
                    cols = slice(h * 64, (h + 1) * 64)
                    y = k.psum[:, 5 + h % 2, 0:TT * 64].rearrange("p (t e) -> p t e", t=TT)
                    dve.scalar_tensor_tensor(out=out[:, :, cols], in0=xs[:, :, cols], scalar=skip[:, h:h + 1], in1=y,
                                             op0=ALU.mult, op1=ALU.add).then_inc(k.out_saved.sem, 1)

                for h in range(4):
                    exponents(TT * h)
                    for s in range(TT):
                        if s + 1 < TT:
                            exponents(TT * h + s + 1)
                        weights(TT * h + s)
                    if h >= 1:
                        save(h - 1)
                save(3)
                dve.wait_ge(k.out_saved.sem, k.out_saved.at(4))
                k.dve.step(dve, dve.tensor_tensor(out, out, z, ALU.mult))
                dve.wait_ge(k.act_made.sem, k.act_made.at(1))
                k.dve.step(dve, dve.tensor_tensor(out, out, sig[:, 0:2, :].rearrange("p a (b e) -> p (a b) e", b=2),
                                                  ALU.mult))

            @block.scalar
            def _(act):
                act.activation(sig[:, 0:2, :].rearrange("p a (b e) -> p (a b) e", b=2), z, ACT.Sigmoid)\
                   .then_inc(k.act_made.sem, 1)
                for i, (h, s) in enumerate(steps):
                    act.wait_ge(k.scores_ready.sem, k.scores_ready.at(i + 1))
                    a = arg[:, i % 2, 0:S - s * P]
                    act.activation(a, a, ACT.Exp).then_inc(k.probs_ready.sem, 1)
        k.pe_made.passed(4)
        k.out_ready.passed(4)
        k.out_saved.passed(4)
        k.dve_made.passed(1 + len(steps))
        k.scores_ready.passed(len(steps))
        k.probs_ready.passed(len(steps))
        k.act_made.passed(1)


def second_mixer(k, probe=None):
    norm_and_turn(k, k.x, TT, k.col("norm_mix_g_2", 0, KT), k.hT)
    with ExitStack() as ctx:
        sb_o = k.sb("sb_o", [P, TT, 256], ctx=ctx)
        rg_x = k.sb("rg_x", [P, 2, PAD + S], ctx=ctx)
        rg_g = k.sb("rg_g", [P, 2, S], ctx=ctx)
        hg = k.sb("hg_qfvg", [P, 8, S], ctx=ctx)
        z = k.sb("m2_z", [P, TT, 256], ctx=ctx)
        xbc = k.sb("m2_xbc", [P, 6, PAD + S], ctx=ctx)
        dt = k.sb("m2_dt", [4, S], ctx=ctx)
        inner = ctx.enter_context(ExitStack())
        sb_qk = k.sb("sb_qk", [P, 4, S], ctx=inner)
        sb_v = k.sb("sb_v", [P, TT, 256], ctx=inner)
        with k.block() as block:
            @block.gpsimd
            def _(pool):
                pool.memset(rg_x[:, :, 0:PAD], 0.0)
                k.pool.step(pool, pool.memset(xbc[:, :, 0:PAD], 0.0))
        u = k.consumed
        projection = inner.enter_context(ExitStack())
        tokens = parts_of(k, k.hT, projection)
        banks = [feature_banks(k, u, tokens), token_banks(k, u + 1, tokens), feature_banks(k, u + 2, tokens),
                 feature_banks(k, u + 3, tokens), feature_banks(k, u + 4, tokens), token_banks(k, u + 5, tokens),
                 feature_banks(k, u + 6, tokens), feature_banks(k, u + 7, tokens)]
        homes = [[sb_qk[:, b, :] for b in range(4)], [sb_v[:, t, :] for t in range(TT)],
                 [rg_x[:, 0, PAD:], rg_x[:, 1, PAD:], rg_g[:, 0, :], rg_g[:, 1, :]],
                 [hg[:, b, :] for b in range(4)], [hg[:, 4 + b, :] for b in range(4)],
                 [z[:, t, :] for t in range(TT)], [xbc[:, b, PAD:] for b in range(4)],
                 [xbc[:, 4, PAD:], xbc[:, 5, PAD:], dt[:, :]]]
        project(k, [{"unit": u + j, "banks": b} for j, b in enumerate(banks)],
                lambda dve, j, b, bank: dve.tensor_copy(homes[j][b], bank), [tokens])
        projection.close()
        mixT = k.hT

        def half(h, first, cols):
            return sb_qk[64 * (h % 2):64 * (h % 2) + 64, first + h // 2, cols]

        stick_breaking(k, [{"q": [half(h, 0, slice(t * P, (t + 1) * P))], "k": [half(h, 2, slice(0, (t + 1) * P))],
                            "keys": (t + 1) * P, "mask": (k.strict[:, :], t * P),
                            "v": [sb_v[:, m, h * 64:(h + 1) * 64] for m in range(t + 1)],
                            "out": sb_o[:, t, h * 64:(h + 1) * 64]} for h in range(4) for t in range(TT)],
                       64 ** -0.5)
        inner.close()
        heads_norm(k, [(by_head(sb_o[:, :, :], 256), by_head(sb_o[:, :, :], 256), None)])
        turn(k, [([sb_o[:, t, c * P:(c + 1) * P] for t in range(TT)], mixT[:, c, :], k.col("sb_norm_g_2", c))
                 for c in range(2)])
        rg_lru(k, rg_x, rg_g, mixT[:, 2:4, :])
        scratch = [sb_o[:, :, :].rearrange("p (c t) d -> p c (t d)", c=2), rg_g[:, :, :], rg_x[:, :, PAD:]]
        hgrn2(k, hg[:, 0:2, :], hg[:, 2:4, :], hg[:, 4:6, :], hg[:, 6:8, :], mixT[:, 4:6, :], scratch)
        mamba2(k, z[:, :, :], xbc, dt[:, :], sb_o[:, :, :], hg[:, 0:TT, :])
        heads_norm(k, [(by_head(sb_o[:, :, :], P), by_head(sb_o[:, :, :], P), None)])
        turn(k, [([sb_o[:, t, c * P:(c + 1) * P] for t in range(TT)], mixT[:, 6 + c, :], k.col("m2_norm_g_2", c))
                 for c in range(2)])
    if probe:
        probe(k)
    project_out(k, k.hT)
FF = 1024
ROUNDS = S // P
MOST_EXTRA = 4 * S // P - 1
BLOCKS = EXPERTS + MOST_EXTRA
HALF = P // 2
NOT_CHOSEN = -4096.0
PER_EXPERT = 6


class Experts:

    def __init__(self, k, name, ctx, tables, one_by_one):
        def signal(what):
            return k.ctx.enter_context(k.nc.semaphore(f"{name}_{what}"))

        self.k, self.tables = k, tables
        self.one_by_one = one_by_one
        self.ahead = 1 if one_by_one else 0
        self.loaded = [signal(f"loaded{r}") for r in range(RING)]
        self.bias_loaded = signal("bias_loaded")
        self.sel_plain = signal("sel_plain")
        self.sel_ready = signal("sel_ready")
        self.gathered = signal("gathered")
        self.xg_ready = signal("xg_ready")
        self.sel_turned = signal("sel_turned")
        self.selT_ready = signal("selT_ready")
        self.up_full = signal("up_full")
        self.glu_ready = signal("glu_ready")
        self.gate_ready = signal("gate_ready")
        self.lin_ready = signal("lin_ready")
        self.prod_ready = signal("prod_ready")
        self.act_ready = signal("act_ready")
        self.act_turned = signal("act_turned")
        self.actT_ready = signal("actT_ready")
        self.down_full = signal("down_full")
        self.o_ready = signal("o_ready")
        self.scat_full = signal("scat_full")
        self.scat_added = signal("scat_added")

    def make_sel(self, dve, j):
        k, T = self.k, self.tables
        at = bass.ds(j, 1)
        if not self.one_by_one and self.waits_from(j, 1):
            dve.wait_ge(self.sel_turned, j)
        place = T.place[:, :, at].broadcast_to([P, TT, P])
        dve.tensor_tensor(T.sel[:, 0], T.iota[:, :].unsqueeze(1).broadcast_to([P, TT, P]), place, ALU.is_equal)\
           .then_inc(self.sel_plain, 1)
        dve.wait_ge(self.sel_plain, j + 1)
        dve.tensor_tensor(T.sel[:, 1], T.sel[:, 0], T.gate[:, :, at].broadcast_to([P, TT, P]), ALU.mult)\
           .then_inc(self.sel_ready, 1)

    def save_gather(self, dve, j, par):
        k, T = self.k, self.tables
        dve.wait_ge(self.gathered, j + 1)
        for b in range(2):
            gain = T.gain[:, 4 * b:4 * b + 4].unsqueeze(2).broadcast_to([P, 4, P])
            ins = dve.tensor_tensor(T.xg[:, 4 * b:4 * b + 4, :], k.psum[:, b, :].rearrange("p (f s) -> p f s", f=4),
                                    gain, ALU.mult)
        ins.then_inc(self.xg_ready, 1)
        dve.wait_ge(self.sel_turned, j + 1)
        dve.tensor_copy(T.selT[:, par, :], k.psum[:, 2, :]).then_inc(self.selT_ready, 1)

    def activate(self, dve, j, n):
        k, T = self.k, self.tables
        q = 4 * j + n
        bank = k.psum[:, 2 + n % 2, :].rearrange("p (f two) -> p f two", two=2)
        dve.wait_ge(self.up_full, q + 1)
        if n >= 2:
            dve.wait_ge(self.act_ready, q - 1)
        elif not self.one_by_one and self.waits_from(j, 1):
            dve.wait_ge(self.act_ready, q - 1)
        dve.tensor_scalar(T.glu[:, n % 2, :], bank[:, :, 0], 7.0, None, ALU.min).then_inc(self.glu_ready, 1)
        dve.tensor_scalar(T.lin[:, n % 2, :], bank[:, :, 1], 7.0, -7.0, ALU.min, ALU.max).then_inc(self.lin_ready, 1)
        dve.wait_ge(self.gate_ready, q + 1)
        dve.wait_ge(self.lin_ready, q + 1)
        dve.scalar_tensor_tensor(out=T.lin[:, n % 2, :], in0=T.lin[:, n % 2, :], scalar=1.0, in1=T.sig[:, n % 2, :],
                                 op0=ALU.add, op1=ALU.mult).then_inc(self.prod_ready, 1)
        dve.wait_ge(self.prod_ready, q + 1)
        dve.tensor_tensor(T.act[:, n * 256:(n + 1) * 256], T.lin[:, n % 2, :], T.glu[:, n % 2, :], ALU.mult)\
           .then_inc(self.act_ready, 1)

    def add(self, dve, j):
        k = self.k
        for s in range(8):
            dve.wait_ge(self.scat_full, 8 * j + s + 1)
            x = k.x[:, s // 2, (s % 2) * 512:(s % 2) * 512 + 512]
            dve.tensor_tensor(x, k.psum[:, SCATTER_BANKS[s % 4], :], x, ALU.add).then_inc(self.scat_added, 1)

    def sigmoids(self, act, j):
        T = self.tables
        for n in range(4):
            act.wait_ge(self.glu_ready, 4 * j + n + 1)
            act.activation(T.sig[:, n % 2, :], T.glu[:, n % 2, :], ACT.Sigmoid, scale=1.702)\
               .then_inc(self.gate_ready, 1)

    def save_act(self, act, j):
        k, T = self.k, self.tables
        act.wait_ge(self.act_turned, j + 1)
        act.activation(T.actT[:, :, :].rearrange("p (b f) s -> p b (f s)", b=2), k.psum[:, 4:6, :], ACT.Copy)\
           .then_inc(self.actT_ready, 1)

    def save_down(self, act, j):
        k, T = self.k, self.tables
        for half in range(2):
            act.wait_ge(self.down_full, 2 * j + half + 1)
            act.activation(T.o[:, half * 512:half * 512 + 512], k.psum[:, 6 + half, :], ACT.Copy)\
               .then_inc(self.o_ready, 1)

    def gather(self, pe, j):
        k, T = self.k, self.tables
        pe.wait_ge(self.sel_ready, j + 1)
        if self.one_by_one:
            pe.wait_ge(self.scat_added, 8 * j + 1)
        elif self.waits_from(j, 2):
            pe.wait_ge(self.scat_added, 8 * j - 8)
        for f in range(KT):
            for t in range(TT):
                ins = pe.matmul(k.psum[:, f // 4, (f % 4) * P:(f % 4 + 1) * P], T.y[:, t, f * P:(f + 1) * P],
                                T.sel[:, 0, t, :], start=(t == 0), stop=(t == TT - 1))
        ins.then_inc(self.gathered, 1)
        for t in range(TT):
            ins = pe.transpose(k.psum[:, 2, t * P:(t + 1) * P], T.sel[:, 1, t, :], k.ident[:, :])
        ins.then_inc(self.sel_turned, 1)

    def up(self, pe, j, wait_unit, par):
        k, T = self.k, self.tables
        pe.wait_ge(self.xg_ready, j + 1)
        pe.wait_ge(self.selT_ready, j + 1)
        pe.wait_ge(self.bias_loaded, 16 * (j + 1))
        for n in range(4):
            w = wait_unit(pe, n)
            if n >= 2:
                pe.wait_ge(self.act_ready, 4 * j + n - 1)
            bank = k.psum[:, 2 + n % 2, :]
            for c in range(KT):
                pe.matmul(bank, T.xg[:, c, :], w[:, c, :], start=(c == 0), stop=False)
            pe.matmul(bank, T.top[:, :], T.bias[:, par, n * 512:(n + 1) * 512], start=False, stop=True)\
              .then_inc(self.up_full, 1)

    def up_half(self, pe, j, wait_unit, par):
        k, T = self.k, self.tables
        pe.wait_ge(self.xg_ready, j + 1)
        pe.wait_ge(self.selT_ready, j + 1)
        pe.wait_ge(self.bias_loaded, 16 * (j + 1))
        for pair in range(2):
            w = [wait_unit(pe, 2 * pair), wait_unit(pe, 2 * pair + 1)]
            banks = [k.psum[64 * g:64 * g + 64, 2 + pair, :] for g in range(2)]
            for c in range(KT):
                for g in range(2):
                    pe.matmul(banks[g], T.xg[:, c, 0:HALF], w[g][:, c, :], start=(c == 0), stop=False)
            for g in range(2):
                cols = slice((2 * pair + g) * 512, (2 * pair + g + 1) * 512)
                pe.matmul(banks[g], T.top[:, 0:HALF], T.bias[:, par, cols], start=False, stop=True)\
                  .then_inc(self.up_full, 1)

    def turn_act_half(self, pe, j):
        k, T = self.k, self.tables
        pe.wait_ge(self.act_ready, 4 * j + 4)
        for i in range(4):
            ins = pe.transpose(k.psum[:, 4, i * P:(i + 1) * P], T.act[:, i * P:(i + 1) * P], k.ident[:, :])
        ins.then_inc(self.act_turned, 1)

    def down_half(self, pe, j, wait_unit):
        k, T = self.k, self.tables
        pe.wait_ge(self.actT_ready, j + 1)
        if self.waits_from(j, 1):
            pe.wait_ge(self.scat_added, 8 * j)
        w = [wait_unit(pe, 4), wait_unit(pe, 5)]
        for c in range(KT):
            for g in range(2):
                ins = pe.matmul(k.psum[64 * g:64 * g + 64, 6, :], T.actT[:, c, 0:HALF], w[g][:, c, :],
                                start=(c == 0), stop=(c == KT - 1))
                if c == KT - 1:
                    ins.then_inc(self.down_full, 1)

    def activate_half(self, dve, j, pair):
        k, T = self.k, self.tables
        q = 4 * j + 2 * pair + 2
        bank = k.psum[:, 2 + pair, :].rearrange("p (f two) -> p f two", two=2)
        dve.wait_ge(self.up_full, q)
        if self.waits_from(j, 1) or pair:
            dve.wait_ge(self.act_ready, q - 2)
        dve.tensor_scalar(T.glu[:, pair, :], bank[:, :, 0], 7.0, None, ALU.min).then_inc(self.glu_ready, 2)
        dve.tensor_scalar(T.lin[:, pair, :], bank[:, :, 1], 7.0, -7.0, ALU.min, ALU.max).then_inc(self.lin_ready, 2)
        dve.wait_ge(self.gate_ready, q)
        dve.wait_ge(self.lin_ready, q)
        dve.scalar_tensor_tensor(out=T.lin[:, pair, :], in0=T.lin[:, pair, :], scalar=1.0, in1=T.sig[:, pair, :],
                                 op0=ALU.add, op1=ALU.mult).then_inc(self.prod_ready, 2)
        dve.wait_ge(self.prod_ready, q)
        dve.tensor_tensor(T.act[:, pair * 256:(pair + 1) * 256], T.lin[:, pair, :], T.glu[:, pair, :], ALU.mult)\
           .then_inc(self.act_ready, 2)

    def sigmoids_half(self, act, j):
        T = self.tables
        for pair in range(2):
            act.wait_ge(self.glu_ready, 4 * j + 2 * pair + 2)
            act.activation(T.sig[:, pair, :], T.glu[:, pair, :], ACT.Sigmoid, scale=1.702).then_inc(self.gate_ready, 2)

    def save_act_half(self, act, j):
        k, T = self.k, self.tables
        act.wait_ge(self.act_turned, j + 1)
        turned = k.psum[:, 4, :].rearrange("p (pair h g s) -> p pair g h s", pair=2, h=2, g=2)
        home = T.actT[:, :, :].rearrange("p (pair g h) s -> p pair g h s", pair=2, g=2)
        act.activation(home[:, 0, :, :, 0:HALF], turned[:, 0], ACT.Copy)
        act.activation(home[:, 1, :, :, 0:HALF], turned[:, 1], ACT.Copy).then_inc(self.actT_ready, 1)

    def save_down_half(self, act, j):
        k, T = self.k, self.tables
        act.wait_ge(self.down_full, 2 * j + 2)
        for g in range(2):
            act.activation(T.o[0:HALF, g * 512:g * 512 + 512], k.psum[64 * g:64 * g + 64, 6, :], ACT.Copy)\
               .then_inc(self.o_ready, 1)

    def turn_act(self, pe, j):
        k, T = self.k, self.tables
        pe.wait_ge(self.act_ready, 4 * j + 4)
        for f in range(KT):
            ins = pe.transpose(k.psum[:, 4 + f // 4, (f % 4) * P:(f % 4 + 1) * P], T.act[:, f * P:(f + 1) * P],
                               k.ident[:, :])
        ins.then_inc(self.act_turned, 1)

    def down(self, pe, j, wait_unit):
        k, T = self.k, self.tables
        pe.wait_ge(self.actT_ready, j + 1)
        if not self.one_by_one and self.waits_from(j, 1):
            pe.wait_ge(self.scat_added, 8 * j)
        for half in range(2):
            w = wait_unit(pe, 4 + half)
            for c in range(KT):
                ins = pe.matmul(k.psum[:, 6 + half, :], T.actT[:, c, :], w[:, c, :], start=(c == 0),
                                stop=(c == KT - 1))
            ins.then_inc(self.down_full, 1)

    def scatter(self, pe, j, par):
        k, T = self.k, self.tables
        pe.wait_ge(self.o_ready, 2 * j + 2)
        for s in range(8):
            if s >= 4:
                pe.wait_ge(self.scat_added, 8 * j + s - 3 + self.ahead)
            t, half = s // 2, s % 2
            pe.matmul(k.psum[:, SCATTER_BANKS[s % 4], :], T.selT[:, par, t * P:(t + 1) * P],
                      T.o[:, half * 512:half * 512 + 512], start=True, stop=True).then_inc(self.scat_full, 1)

    def unit_used(self, eng, j, n):
        if n < 4:
            eng.wait_ge(self.up_full, 4 * j + n + 1)
        else:
            eng.wait_ge(self.down_full, 2 * j + n - 3)

    @staticmethod
    def waits_from(j, first):
        return not isinstance(j, int) or j >= first


SCATTER_BANKS = [6, 7, 0, 1]


class Tables:
    pass


def expert_unit(k, e, n):
    if n < 4:
        w = k.ins["moe_w_gu_2"][0][bass.ds(e, 1), :, n * 512:(n + 1) * 512]
    else:
        w = k.ins["moe_w_down_2"][0][bass.ds(e, 1), :, (n - 4) * 512:(n - 3) * 512]
    return w.rearrange("e (k p) n -> p (e k) n", p=P)


def ring_view(k, slot):
    return k.ring[:, slot, :].rearrange("p (k n) -> p k n", k=KT)


def experts(k):
    with ExitStack() as ctx:
        k.ring = k.sb("expert_ring", [P, RING, UNIT], ctx=ctx)
        T = Tables()
        T.y = k.sb("moe_y", [P, TT, D], ctx=ctx)
        T.gain = k.col("norm_ffn_g_2", 0, KT)
        T.place = k.sb("moe_place", [P, TT, BLOCKS], ctx=ctx)
        T.gate = k.sb("moe_gate", [P, TT, BLOCKS], ctx=ctx)
        T.iota = k.sb("moe_iota", [P, P], ctx=ctx)
        T.ints = k.sb("moe_ints", [P, 1 + MOST_EXTRA], I32, ctx=ctx)
        T.count = k.sb("moe_count", [P, EXPERTS], I32, ctx=ctx)
        with k.block() as block:
            base = Experts(k, "first", ctx, T, False)

            @block.sync
            def _(sp):
                for n in range(RING):
                    sp.dma_start(ring_view(k, n), expert_unit(k, 0, n)).then_inc(base.loaded[n], 16)
        row_norm(k, k.x, TT, T.y, ctx)
        turn(k, [([T.y[:, t, c * P:(c + 1) * P] for t in range(TT)], k.hT[:, c, :], T.gain[:, c:c + 1])
                 for c in range(KT)])
        route(k, T)
        T.sel = k.sb("moe_sel", [P, 2, TT, P], ctx=ctx)
        T.selT = k.sb("moe_selT", [P, 2, S], ctx=ctx)
        T.xg = k.sb("moe_xg", [P, KT, P], ctx=ctx)
        T.glu = k.sb("moe_glu", [P, 2, 256], ctx=ctx)
        T.lin = k.sb("moe_lin", [P, 2, 256], ctx=ctx)
        T.sig = k.sb("moe_sig", [P, 2, 256], ctx=ctx)
        T.act = k.sb("moe_act", [P, FF], ctx=ctx)
        T.actT = k.sb("moe_actT", [P, KT, P], ctx=ctx)
        T.o = k.sb("moe_o", [P, D], ctx=ctx)
        T.bias = k.sb("moe_bias", [P, 2, 2 * FF], ctx=ctx)
        T.top = k.sb("moe_top", [P, P], ctx=ctx)
        with k.block() as block:
            @block.gpsimd
            def _(pool):
                pool.memset(T.bias[:, :, :], 0.0)
                pool.memset(T.o[:, :], 0.0)
                k.pool.step(pool, pool.memset(T.top[:, :], 0.0))
                k.pool.step(pool, pool.memset(T.top[0:1, :], 1.0))
        first_blocks(k, base, T)
        extra_blocks(k, Experts(k, "extra", ctx, T, True), T)


def first_blocks(k, E, T):
    rounds = EXPERTS // 2
    bias_rows = k.ins["moe_b_gu_2"][0]
    with k.block() as block:
        def wait_unit_of(i, h):
            def wait_unit(pe, n):
                m = PER_EXPERT * h + n
                pe.wait_ge(E.loaded[m % RING], 16 * (3 * i + m // RING + 1))
                return ring_view(k, m % RING)
            return wait_unit

        @block.sync
        def _(sp):
            def load_bias(j, par):
                sp.dma_start(T.bias[0:1, par, :], bias_rows[bass.ds(j, 1), :]).then_inc(E.bias_loaded, 16)

            def round_of_loads(i, last):
                for m in range(2 * PER_EXPERT):
                    h, n = divmod(m, PER_EXPERT)
                    if last and m + RING >= 2 * PER_EXPERT and n != 0:
                        continue
                    E.unit_used(sp, 2 * i + h, n)
                    if n == 0 and not (last and h == 1):
                        load_bias(2 * i + h + 1, (h + 1) % 2)
                    ahead = m + RING
                    if ahead < 2 * PER_EXPERT:
                        e = 2 * i + ahead // PER_EXPERT
                    elif last:
                        continue
                    else:
                        e = 2 * i + 2
                    sp.dma_start(ring_view(k, m % RING), expert_unit(k, e, ahead % PER_EXPERT))\
                      .then_inc(E.loaded[m % RING], 16)

            load_bias(0, 0)
            with sp.Fori(0, rounds - 1) as i:
                round_of_loads(i, False)
            round_of_loads(rounds - 1, True)

        def is_half(eng, j):
            return eng.value_load(T.count[0:1, bass.ds(j, 1)], min_val=0, max_val=S) < HALF + 1

        @block.tensor
        def _(pe):
            def step(i, h, before=True, after=True):
                j = 2 * i + h
                half = is_half(pe, j)
                with pe.If(half):
                    E.up_half(pe, j, wait_unit_of(i, h), h)
                with pe.Else():
                    E.up(pe, j, wait_unit_of(i, h), h)
                if before:
                    E.scatter(pe, j - 1, 1 - h)
                with pe.If(half):
                    E.turn_act_half(pe, j)
                with pe.Else():
                    E.turn_act(pe, j)
                if after:
                    E.gather(pe, j + 1)
                with pe.If(half):
                    E.down_half(pe, j, wait_unit_of(i, h))
                with pe.Else():
                    E.down(pe, j, wait_unit_of(i, h))

            E.gather(pe, 0)
            step(0, 0, before=False)
            step(0, 1)
            with pe.Fori(1, rounds - 1) as i:
                step(i, 0)
                step(i, 1)
            step(rounds - 1, 0)
            step(rounds - 1, 1, after=False)
            E.scatter(pe, EXPERTS - 1, 1)

        @block.vector
        def _(dve):
            def step(i, h, before=True, gathers=True, selects=True):
                j = 2 * i + h
                with dve.If(is_half(dve, j)):
                    E.activate_half(dve, j, 0)
                    E.activate_half(dve, j, 1)
                with dve.Else():
                    for n in range(4):
                        E.activate(dve, j, n)
                if before:
                    E.add(dve, j - 1)
                if gathers:
                    E.save_gather(dve, j + 1, 1 - h)
                if selects:
                    E.make_sel(dve, j + 2)

            E.make_sel(dve, 0)
            E.save_gather(dve, 0, 0)
            E.make_sel(dve, 1)
            step(0, 0, before=False)
            step(0, 1)
            with dve.Fori(1, rounds - 1) as i:
                step(i, 0)
                step(i, 1)
            step(rounds - 1, 0, selects=False)
            step(rounds - 1, 1, gathers=False, selects=False)
            E.add(dve, EXPERTS - 1)

        @block.scalar
        def _(act):
            def step(j):
                with act.If(is_half(act, j)):
                    E.sigmoids_half(act, j)
                    E.save_act_half(act, j)
                    E.save_down_half(act, j)
                with act.Else():
                    E.sigmoids(act, j)
                    E.save_act(act, j)
                    E.save_down(act, j)

            step(0)
            step(1)
            with act.Fori(1, rounds - 1) as i:
                step(2 * i)
                step(2 * i + 1)
            step(EXPERTS - 2)
            step(EXPERTS - 1)


def extra_blocks(k, E, T):
    place, gate = T.place, T.gate
    T.place, T.gate = place[:, :, EXPERTS:BLOCKS], gate[:, :, EXPERTS:BLOCKS]
    bias_rows = k.ins["moe_b_gu_2"][0]
    with k.block() as block:
        def each(eng, body):
            count = eng.value_load(T.ints[0:1, 0:1], min_val=0, max_val=MOST_EXTRA)
            with eng.Fori(0, MOST_EXTRA) as b:
                with eng.If(b < count):
                    body(b)

        def wait_unit_of(b):
            def wait_unit(pe, n):
                slot = n % RING
                per_block = 2 if slot < PER_EXPERT - RING else 1
                pe.wait_ge(E.loaded[slot], 16 * (per_block * b + n // RING + 1))
                return ring_view(k, slot)
            return wait_unit

        @block.sync
        def _(sp):
            def body(b):
                e = sp.value_load(T.ints[0:1, bass.ds(b + 1, 1)], min_val=0, max_val=EXPERTS - 1)
                sp.wait_ge(E.scat_added, 8 * b + 1)
                sp.dma_start(T.bias[0:1, 0, :], bias_rows[bass.ds(e, 1), :]).then_inc(E.bias_loaded, 16)
                for n in range(PER_EXPERT):
                    if n >= RING:
                        E.unit_used(sp, b, n - RING)
                    sp.dma_start(ring_view(k, n % RING), expert_unit(k, e, n)).then_inc(E.loaded[n % RING], 16)
            each(sp, body)

        @block.tensor
        def _(pe):
            def body(b):
                E.gather(pe, b)
                E.up(pe, b, wait_unit_of(b), 0)
                E.turn_act(pe, b)
                E.down(pe, b, wait_unit_of(b))
                E.scatter(pe, b, 0)
            each(pe, body)

        @block.vector
        def _(dve):
            def body(b):
                E.make_sel(dve, b)
                E.save_gather(dve, b, 0)
                for n in range(4):
                    E.activate(dve, b, n)
                E.add(dve, b)
            dve.memset(T.glu[:, 0, 0:1], 0.0).then_inc(E.scat_added, 1)
            each(dve, body)

        @block.scalar
        def _(act):
            def body(b):
                E.sigmoids(act, b)
                E.save_act(act, b)
                E.save_down(act, b)
            each(act, body)


def route(k, T):
    NC = (ROUNDS - 1) * EXPERTS
    with ExitStack() as ctx:
        wr = k.sb("router_w", [P, KT, EXPERTS], ctx=ctx)
        br = k.sb("router_b", [P, EXPERTS], ctx=ctx)
        bd = k.sb("b_down", [EXPERTS, D], ctx=ctx)
        logits = k.sb("logits", [P, TT, EXPERTS], ctx=ctx)
        best = k.sb("best", [P, TT, 8], ctx=ctx)
        index = k.sb("best_index", [P, TT, 8], U32, ctx=ctx)
        index_f = k.sb("best_index_f", [P, TT, 8], ctx=ctx)
        gates = k.sb("gates", [P, TT, 4], ctx=ctx)
        neg = k.sb("neg_best", [P, TT], ctx=ctx)
        total = k.sb("gate_total", [P, TT], ctx=ctx)
        ids = k.sb("expert_ids", [P, EXPERTS], ctx=ctx)
        hot = k.sb("chosen_one", [P, TT, EXPERTS], ctx=ctx)
        chosen = k.sb("chosen", [P, TT, EXPERTS], ctx=ctx)
        before = k.sb("before", [P, P], ctx=ctx)
        placeT = k.sb("gateT", [EXPERTS, S], ctx=ctx)
        count = k.sb("counts", [P, EXPERTS], ctx=ctx)
        flag = k.sb("extra_flag", [P, ROUNDS - 1, EXPERTS], ctx=ctx)
        order = k.sb("extra_order", [P, 1 + NC], ctx=ctx)
        zero = k.sb("extra_zero", [P, NC], ctx=ctx)
        nth = k.sb("extra_nth", [P, MOST_EXTRA], ctx=ctx)
        pick = k.sb("extra_pick", [P, MOST_EXTRA, NC], ctx=ctx)
        prod = k.sb("extra_prod", [P, MOST_EXTRA, NC], ctx=ctx)
        cand = k.sb("extra_cand", [P, 2, ROUNDS - 1, EXPERTS], ctx=ctx)
        num = k.sb("extra_num", [P, 1 + MOST_EXTRA], ctx=ctx)
        place, gate = T.place[:, :, 0:EXPERTS], T.gate[:, :, 0:EXPERTS]
        with k.block() as block:
            @block.gpsimd
            def _(pool):
                pool.iota(T.iota[:, :], pattern=[[1, P]], base=0, channel_multiplier=0,
                          allow_small_or_imprecise_dtypes=True)
                pool.iota(ids[:, :], pattern=[[1, EXPERTS]], base=0, channel_multiplier=0,
                          allow_small_or_imprecise_dtypes=True)
                pool.iota(nth[:, :], pattern=[[1, MOST_EXTRA]], base=0, channel_multiplier=0,
                          allow_small_or_imprecise_dtypes=True)
                k.pool.step(pool, pool.memset(before[:, :], 1.0))
                pool.affine_select(out=before[:, :], in_=before[:, :], compare_op=ALU.is_gt, fill=0.0, base=0,
                                   pattern=[[1, P]], channel_multiplier=-1).then_inc(k.pool_made.sem, 1)

            @block.sync
            def _(sp):
                sp.dma_start(wr[:, :, :], k.ins["router_w_2"][0].rearrange("(k p) e -> p k e", p=P))\
                  .then_inc(k.small_loaded.sem, 16)
                sp.dma_start(br[:, :], k.ins["router_b_2"][0].partition_broadcast(P)).then_inc(k.small_loaded.sem, 16)
                sp.dma_start(bd[:, :], k.ins["moe_b_down_2"][0]).then_inc(k.small_loaded.sem, 16)

            @block.tensor
            def _(pe):
                pe.wait_ge(k.small_loaded.sem, k.small_loaded.at(48))
                for t in range(TT):
                    for c in range(KT):
                        ins = pe.matmul(k.psum[:, 0, t * EXPERTS:(t + 1) * EXPERTS], k.hT[:, c, t * P:(t + 1) * P],
                                        wr[:, c, :], start=(c == 0), stop=(c == KT - 1))
                ins.then_inc(k.pe_made.sem, 1)
                pe.wait_ge(k.dve_made.sem, k.dve_made.at(2))
                pe.wait_ge(k.pool_made.sem, k.pool_made.at(1))
                for t in range(TT):
                    for s in range(t + 1):
                        pe.matmul(k.psum[:, 1, t * EXPERTS:(t + 1) * EXPERTS],
                                  before[:, :] if s == t else k.ones[:, :], chosen[:, s, :],
                                  start=(s == 0), stop=(s == t))
                for s in range(TT):
                    ins = pe.matmul(k.psum[:, 2, 0:EXPERTS], k.ones[:, :], chosen[:, s, :], start=(s == 0),
                                    stop=(s == TT - 1))
                ins.then_inc(k.pe_made.sem, 1)
                pe.wait_ge(k.dve_made.sem, k.dve_made.at(3))
                for t in range(TT):
                    ins = pe.transpose(k.psum[0:EXPERTS, 3, t * P:(t + 1) * P], gate[:, t, :], k.ident[:, :])
                ins.then_inc(k.pe_made.sem, 1)
                pe.wait_ge(k.act_made.sem, k.act_made.at(2))
                for s in range(8):
                    if s >= 4:
                        pe.wait_ge(k.out_saved.sem, k.out_saved.at(s - 3))
                    pe.matmul(k.psum[:, 4 + s % 4, :], placeT[:, (s // 2) * P:(s // 2 + 1) * P],
                              bd[:, (s % 2) * 512:(s % 2) * 512 + 512], start=True, stop=True)\
                      .then_inc(k.out_ready.sem, 1)

            @block.vector
            def _(dve):
                step = lambda ins: k.dve.step(dve, ins)
                dve.wait_ge(k.pe_made.sem, k.pe_made.at(1))
                dve.wait_ge(k.pool_made.sem, k.pool_made.at(1))
                step(dve.tensor_tensor(logits[:, :, :], k.psum[:, 0, 0:TT * EXPERTS].rearrange("p (t e) -> p t e", t=TT),
                                       br[:, :].unsqueeze(1).broadcast_to([P, TT, EXPERTS]), ALU.add))
                for t in range(TT):
                    step(dve.max(best[:, t, :], logits[:, t, :]))
                    step(dve.max_index(index[:, t, :], best[:, t, :], logits[:, t, :]))
                dve.tensor_scalar(neg[:, :], best[:, :, 0], -1.0, None, ALU.mult).then_inc(k.dve_made.sem, 1)
                step(dve.tensor_copy(index_f[:, :, :], index[:, :, :]))
                every = ids[:, :].unsqueeze(1).broadcast_to([P, TT, EXPERTS])
                step(dve.memset(chosen[:, :, :], 0.0))
                for n in range(4):
                    which = index_f[:, :, n:n + 1].broadcast_to([P, TT, EXPERTS])
                    step(dve.tensor_tensor(hot[:, :, :], every, which, ALU.is_equal))
                    if n < 3:
                        step(dve.tensor_tensor(chosen[:, :, :], chosen[:, :, :], hot[:, :, :], ALU.add))
                    else:
                        dve.tensor_tensor(chosen[:, :, :], chosen[:, :, :], hot[:, :, :], ALU.add)\
                           .then_inc(k.dve_made.sem, 1)
                dve.wait_ge(k.act_made.sem, k.act_made.at(1))
                step(dve.reciprocal(total[:, :], total[:, :]))
                step(dve.tensor_tensor(gates[:, :, :], gates[:, :, :],
                                       total[:, :].unsqueeze(2).broadcast_to([P, TT, 4]), ALU.mult))
                dve.wait_ge(k.dve_made.sem, k.dve_made.at(2))
                step(dve.memset(gate, 0.0))
                for n in range(4):
                    which = index_f[:, :, n:n + 1].broadcast_to([P, TT, EXPERTS])
                    step(dve.tensor_tensor(hot[:, :, :], every, which, ALU.is_equal))
                    step(dve.tensor_tensor(hot[:, :, :], hot[:, :, :],
                                           gates[:, :, n:n + 1].broadcast_to([P, TT, EXPERTS]), ALU.mult))
                    if n < 3:
                        step(dve.tensor_tensor(gate, gate, hot[:, :, :], ALU.add))
                    else:
                        dve.tensor_tensor(gate, gate, hot[:, :, :], ALU.add).then_inc(k.dve_made.sem, 1)
                dve.wait_ge(k.pe_made.sem, k.pe_made.at(2))
                dve.wait_ge(k.dve_made.sem, k.dve_made.at(3))
                step(dve.tensor_scalar(hot[:, :, :], chosen[:, :, :], -NOT_CHOSEN, NOT_CHOSEN, ALU.mult, ALU.add))
                step(dve.tensor_tensor(place, k.psum[:, 1, 0:TT * EXPERTS].rearrange("p (t e) -> p t e", t=TT),
                                       hot[:, :, :], ALU.add))
                step(dve.tensor_copy(count[:, :], k.psum[:, 2, 0:EXPERTS]))
                step(dve.tensor_copy(T.count[:, :], count[:, :]))
                for r in range(1, ROUNDS):
                    ins = dve.tensor_scalar(flag[:, r - 1, :], count[:, :], float(r * P), None, ALU.is_gt)
                step(ins)
                dve.memset(zero[:, :], 0.0)
                step(dve.memset(order[:, 0:1], 0.0))
                flat = flag[:, :, :].rearrange("p r e -> p (r e)")
                step(dve.tensor_tensor_scan(order[:, 1:], flat, zero[:, :], 0.0, ALU.add, ALU.add))
                step(dve.tensor_tensor(pick[:, :, :], order[:, 0:NC].unsqueeze(1).broadcast_to([P, MOST_EXTRA, NC]),
                                       nth[:, :].unsqueeze(2).broadcast_to([P, MOST_EXTRA, NC]), ALU.is_equal))
                step(dve.tensor_tensor(pick[:, :, :], pick[:, :, :],
                                       flat.unsqueeze(1).broadcast_to([P, MOST_EXTRA, NC]), ALU.mult))
                step(dve.tensor_copy(num[:, 0:1], order[:, NC:NC + 1]))
                step(dve.tensor_copy(cand[:, 0], ids[:, :].unsqueeze(1).broadcast_to([P, ROUNDS - 1, EXPERTS])))

                def look_up(values, out):
                    spread = values.rearrange("p r e -> p (r e)").unsqueeze(1).broadcast_to([P, MOST_EXTRA, NC])
                    step(dve.tensor_tensor(prod[:, :, :], pick[:, :, :], spread, ALU.mult))
                    step(dve.reduce_sum(out, prod[:, :, :], AX))

                look_up(cand[:, 0], num[:, 1:])
                step(dve.tensor_copy(T.ints[:, :], num[:, :]))
                for t in range(TT):
                    for r in range(1, ROUNDS):
                        step(dve.tensor_scalar(cand[:, 0, r - 1, :], place[:, t, :], float(r * P), None, ALU.subtract))
                        step(dve.tensor_copy(cand[:, 1, r - 1, :], gate[:, t, :]))
                    look_up(cand[:, 0], T.place[:, t, EXPERTS:BLOCKS])
                    look_up(cand[:, 1], T.gate[:, t, EXPERTS:BLOCKS])
                for s in range(8):
                    dve.wait_ge(k.out_ready.sem, k.out_ready.at(s + 1))
                    x = k.x[:, s // 2, (s % 2) * 512:(s % 2) * 512 + 512]
                    dve.tensor_tensor(x, k.psum[:, 4 + s % 4, :], x, ALU.add).then_inc(k.out_saved.sem, 1)

            @block.scalar
            def _(act):
                act.wait_ge(k.dve_made.sem, k.dve_made.at(1))
                for t in range(TT):
                    ins = act.activation(gates[:, t, :], best[:, t, 0:4], ACT.Exp, bias=neg[:, t:t + 1],
                                         accum_out=total[:, t:t + 1])
                ins.then_inc(k.act_made.sem, 1)
                act.wait_ge(k.pe_made.sem, k.pe_made.at(3))
                act.activation(placeT[:, :], k.psum[0:EXPERTS, 3, :], ACT.Copy).then_inc(k.act_made.sem, 1)
        k.small_loaded.passed(48)
        k.pool_made.passed(1)
        k.pe_made.passed(3)
        k.dve_made.passed(3)
        k.act_made.passed(2)
        k.out_ready.passed(8)
        k.out_saved.passed(8)


def finish(k):
    with ExitStack() as ctx:
        y = k.sb("final_y", [P, TT, D], ctx=ctx)
        gain = k.sb("final_gain", [P, D], ctx=ctx)
        row_norm(k, k.x, TT, y, ctx)
        with k.block() as block:
            @block.sync
            def _(sp):
                sp.dma_start(gain[:, :], k.ins["final_norm_g_2"].partition_broadcast(P))\
                  .then_inc(k.small_loaded.sem, 16)
                out = k.out[0].rearrange("(t p) d -> t p d", p=P)
                for t in range(TT):
                    sp.wait_ge(k.dve_made.sem, k.dve_made.at(t + 1))
                    sp.dma_start(out[t], y[:, t, :]).then_inc(k.stored.sem, 16)
                sp.wait_ge(k.stored.sem, k.stored.at(16 * TT))

            @block.vector
            def _(dve):
                dve.wait_ge(k.small_loaded.sem, k.small_loaded.at(16))
                for t in range(TT):
                    dve.tensor_tensor(y[:, t, :], y[:, t, :], gain[:, :], ALU.mult).then_inc(k.dve_made.sem, 1)
        k.stored.passed(16 * TT)


def build(nc, ins, out):
    with ExitStack() as ctx:
        k = Core(nc, ctx, ins, out)
        with ExitStack() as weights:
            setup(k, weights)
            even_mixer(k)
            cross(k, 0)
            mlp(k, 0)
            odd_mixer(k)
            cross(k, 1)
            mlp(k, 1)
            second_mixer(k)
        experts(k)
        finish(k)


def kernel(**inputs):
    import numpy as np
    import concourse.bacc as bacc
    from concourse.bass_utils import run_bass_kernel_spmd

    nc = bacc.Bacc("TRN2", target_bir_lowering=False, num_devices=1)
    arrays, ins = {}, {}
    for name, value in inputs.items():
        a = np.ascontiguousarray(value)
        arrays[f"in_{name}"] = a
        ins[name] = nc.dram_tensor(f"in_{name}", a.shape, mybir.dt.from_np(a.dtype), kind="ExternalInput").ap()
    out = nc.dram_tensor("out", (1, S, D), F32, kind="ExternalOutput").ap()
    build(nc, ins, out)
    result = run_bass_kernel_spmd(nc, [arrays], core_ids=[0])
    return result.results[0]["out"]
```

```python
from contextlib import ExitStack

import concourse.bass as bass
from concourse import mybir

ALU = mybir.AluOpType
ACT = mybir.ActivationFunctionType
AX = mybir.AxisListType.X
F32 = mybir.dt.float32
I32 = mybir.dt.int32
U32 = mybir.dt.uint32
F32R = mybir.dt.float32r
BF16 = mybir.dt.bfloat16

P = 128
D = 1024
S = 512
KT = D // P
TT = S // P
MEM = 256
EPS = 1e-6
MASKED = -1e30
TAKEN = -3e38
TOPK = 128
EXPERTS = 32
RING = 4
UNIT = 8 * 512


class Signal:

    def __init__(self, k, name):
        self.sem = k.ctx.enter_context(k.nc.semaphore(name))
        self.base = 0

    def at(self, n):
        return self.base + n

    def passed(self, n):
        self.base += n


class Chain:

    def __init__(self, k, name):
        self.sem = k.ctx.enter_context(k.nc.semaphore(name))
        self.count = 0

    def step(self, eng, ins):
        self.count += 1
        ins.then_inc(self.sem, 1)
        eng.wait_ge(self.sem, self.count)


class Unit:

    def __init__(self, source, ktiles, cols):
        self.source, self.ktiles, self.cols = source, ktiles, cols


def cut(weight, row0, ktiles, col0, cols):
    rows = weight[row0:row0 + ktiles * P, col0:col0 + cols]
    return Unit(rows.rearrange("(k p) n -> p k n", p=P), ktiles, cols)


class Parts:

    def __init__(self, whole, high, low):
        self.whole, self.high, self.low = whole, high, low

    @property
    def shape(self):
        return self.whole.shape

    def __getitem__(self, at):
        return Parts(self.whole[at], self.high[at], self.low[at])

    def round(self, act):
        return act.activation(self.high, self.whole, ACT.Copy)

    def rest(self, dve):
        return dve.tensor_tensor(self.low, self.whole, self.high.bitcast(F32), ALU.subtract)


def parts_of(k, whole, ctx):
    high, low = (k.sb(name, list(whole.shape), F32R, ctx=ctx) for name in ("high_parts", "low_parts"))
    every = tuple(slice(None) for _ in whole.shape)
    return Parts(whole[every], high[every], low[every])


def products_of(a, b):
    return [(a.high, b.high), (a.high, b.low), (a.low, b.high)]


class Core:

    def __init__(self, nc, ctx, ins, out):
        self.nc, self.ctx, self.ins, self.out = nc, ctx, ins, out
        self.tensors = 0
        self.x = self.sb("x_residual", [P, TT, D])
        self.hT = self.sb("hT", [P, KT, S])
        self.ident = self.sb("ident", [P, P])
        self.ones = self.sb("ones", [P, P])
        self.causal = self.sb("causal", [P, P])
        self.strict = self.sb("strict", [P, P])
        self.eps = self.sb("eps", [P, 1])
        self.psum = ctx.enter_context(nc.psum_tensor("psum", [P, 8, 512], F32))
        self.loaded = Signal(self, "weights_loaded")
        self.unit_rounded = Signal(self, "unit_rounded")
        self.unit_split = Signal(self, "unit_split")
        self.input_rounded = Signal(self, "input_rounded")
        self.input_split = Signal(self, "input_split")
        self.bank_full = Signal(self, "bank_full")
        self.bank_free = Signal(self, "bank_free")
        self.small_loaded = Signal(self, "small_loaded")
        self.normalised = Signal(self, "normalised")
        self.turned = Signal(self, "turned")
        self.turned_even = Signal(self, "turned_even")
        self.turned_odd = Signal(self, "turned_odd")
        self.squares = Signal(self, "squares")
        self.roots = Signal(self, "roots")
        self.rstd = Signal(self, "rstd")
        self.scores_ready = Signal(self, "scores_ready")
        self.negmax_ready = Signal(self, "negmax_ready")
        self.probs_ready = Signal(self, "probs_ready")
        self.attn_ready = Signal(self, "attn_ready")
        self.attn_turned = Signal(self, "attn_turned")
        self.attnT_ready = Signal(self, "attnT_ready")
        self.out_ready = Signal(self, "out_ready")
        self.out_saved = Signal(self, "out_saved")
        self.pe_made = Signal(self, "pe_made")
        self.dve_made = Signal(self, "dve_made")
        self.act_made = Signal(self, "act_made")
        self.pool_made = Signal(self, "pool_made")
        self.bias_loaded = Signal(self, "bias_loaded")
        self.bias_rounded = Signal(self, "bias_rounded")
        self.bias_rest = Signal(self, "bias_rest")
        self.stored = Signal(self, "stored")
        self.dve = Chain(self, "dve_order")
        self.act = Chain(self, "act_order")
        self.pool = Chain(self, "pool_order")
        self.units = weight_units(ins)
        self.consumed = 0
        self.used_at = {}

    def sb(self, name, shape, dtype=F32, ctx=None):
        self.tensors += 1
        return (ctx or self.ctx).enter_context(self.nc.sbuf_tensor(f"{name}_{self.tensors}", shape, dtype))

    def col(self, name, i, n=1):
        r, at = self.place[name]
        return self.cols[:, r, at + i:at + i + n]

    def block(self):
        return self.nc.Block(no_gpsimd_drain=True)

    def hold_units(self, ctx):
        self.unit_whole = self.sb("unit_whole", [P, UNIT], ctx=ctx)
        self.unit_high = self.sb("unit_high", [P, 2, UNIT], F32R, ctx=ctx)
        self.unit_low = self.sb("unit_low", [P, 2, UNIT], F32R, ctx=ctx)

    def unit(self, u):
        kt, cols = self.units[u].ktiles, self.units[u].cols
        views = (self.unit_whole[:, 0:kt * cols], self.unit_high[:, u % 2, 0:kt * cols],
                 self.unit_low[:, u % 2, 0:kt * cols])
        return Parts(*(view.rearrange("p (k n) -> p k n", k=kt) for view in views))

    def load_unit(self, sp, u):
        if u < len(self.units):
            if u >= 1:
                sp.wait_ge(self.unit_split.sem, u)
            sp.dma_start(self.unit(u).whole, self.units[u].source).then_inc(self.loaded.sem, 16)

    def round_unit(self, act, u):
        if u < len(self.units):
            act.wait_ge(self.loaded.sem, 16 * (u + 1))
            if u >= 2:
                act.wait_ge(self.bank_full.sem, self.used_at[u - 2])
            self.unit(u).round(act).then_inc(self.unit_rounded.sem, 1)

    def rest_of_unit(self, dve, u):
        if u < len(self.units):
            dve.wait_ge(self.unit_rounded.sem, u + 1)
            self.unit(u).rest(dve).then_inc(self.unit_split.sem, 1)


def weight_units(ins):
    units = []

    def columns(weight, widths, row0=0, ktiles=KT):
        at = 0
        for w in widths:
            units.append(cut(weight, row0, ktiles, at, w))
            at += w

    def cross(i):
        columns(ins["wq_x"][i], [512])
        columns(ins["wkv_x"][i], [512, 512])
        columns(ins["wo_x"][i], [1024], ktiles=4)

    def mlp(i):
        for part in range(4):
            for half in range(2):
                units.append(cut(ins["w_up"][i], 0, KT, part * 1024 + half * 512, 512))
            for half in range(2):
                units.append(cut(ins["w_down"][i], part * 1024, KT, half * 512, 512))

    columns(ins["w_in_e"][0], EVEN_UNITS)
    units.append(cut(ins["w_kv_up_b"][0], 0, 2, 0, 1024))
    columns(ins["w_out_e"][0], [512, 512])
    cross(0)
    mlp(0)
    columns(ins["w_in_o"][0], [512] * 4)
    columns(ins["w_out_o"][0], [512, 512])
    cross(1)
    mlp(1)
    columns(ins["w_in_2"][0], SECOND_UNITS)
    columns(ins["w_out_2"][0], [512, 512])
    return units


EVEN_UNITS = [512, 512, 512, 512, 290, 290]
SECOND_UNITS = [512, 256, 512, 512, 512, 256, 512, 260]



def project(k, jobs, evacuate, inputs=()):
    total = 0
    for job in jobs:
        total += len(job["banks"])
        k.used_at[job["unit"]] = k.bank_full.at(total)
    units = sorted({job["unit"] for job in jobs})
    first_job = {u: min(j for j, job in enumerate(jobs) if job["unit"] == u) for u in units}
    tiles = [x[:, c] for x in inputs for c in range(x.shape[1])]
    with k.block() as block:
        @block.sync
        def _(sp):
            for u in units:
                k.load_unit(sp, u + 2)

        @block.scalar
        def _(act):
            for tile in tiles:
                tile.round(act).then_inc(k.input_rounded.sem, 1)
            for u in units:
                k.round_unit(act, u + 1)

        @block.tensor
        def _(pe):
            n = 0
            split = 0
            for j, job in enumerate(jobs):
                pe.wait_ge(k.unit_split.sem, job["unit"] + 1)
                for b, (products, width) in enumerate(job["banks"]):
                    if n >= 8:
                        pe.wait_ge(k.bank_free.sem, k.bank_free.at(n - 7))
                    bank = k.psum[0:products[0][0].shape[-1], n % 8, 0:width]
                    for i, (lhsT, rhs) in enumerate(products):
                        needs = job.get("inputs_before", 0) + i + 1
                        if inputs and needs > split:
                            split = needs
                            pe.wait_ge(k.input_split.sem, k.input_split.at(split))
                        parts = products_of(lhsT, rhs)
                        for m, (a, c) in enumerate(parts):
                            ins = pe.matmul(bank, a, c, start=(i == 0 and m == 0),
                                            stop=(i == len(products) - 1 and m == len(parts) - 1))
                    ins.then_inc(k.bank_full.sem, 1)
                    n += 1

        @block.vector
        def _(dve):
            for i, tile in enumerate(tiles):
                dve.wait_ge(k.input_rounded.sem, k.input_rounded.at(i + 1))
                tile.rest(dve).then_inc(k.input_split.sem, 1)
            n = 0
            for j, job in enumerate(jobs):
                if first_job[job["unit"]] == j:
                    k.rest_of_unit(dve, job["unit"] + 1)
                for b, (products, width) in enumerate(job["banks"]):
                    dve.wait_ge(k.bank_full.sem, k.bank_full.at(n + 1))
                    bank = k.psum[0:products[0][0].shape[-1], n % 8, 0:width]
                    evacuate(dve, j, b, bank).then_inc(k.bank_free.sem, 1)
                    n += 1
    k.input_rounded.passed(len(tiles))
    k.input_split.passed(len(tiles))
    k.bank_full.passed(total)
    k.bank_free.passed(total)
    k.consumed = units[-1] + 1


def token_banks(k, u, hT, tiles=TT, col0=0, cols=None):
    w = k.unit(u)
    cols = cols or w.shape[2]
    kt = w.shape[1]
    return [([(hT[:, c, t * P:(t + 1) * P], w[:, c, col0:col0 + cols]) for c in range(kt)], cols)
            for t in range(tiles)]


def feature_banks(k, u, hT, col0=0, cols=None):
    w = k.unit(u)
    cols = cols or w.shape[2]
    kt = w.shape[1]
    return [([(w[:, c, col0 + m:col0 + min(m + P, cols)], hT[:, c, :]) for c in range(kt)], hT.shape[2])
            for m in range(0, cols, P)]


def turn(k, jobs):
    with k.block() as block:
        @block.tensor
        def _(pe):
            for j, (sources, dst, gain) in enumerate(jobs):
                if j >= 8:
                    saved = k.turned_even if j % 2 == 0 else k.turned_odd
                    pe.wait_ge(saved.sem, saved.at((j - 8) // 2 + 1))
                for i, src in enumerate(sources):
                    rows, w = src.shape
                    ins = pe.transpose(k.psum[0:w, j % 8, i * P:i * P + rows], src, k.ident[0:rows, 0:rows])
                ins.then_inc(k.turned.sem, 1)

        @block.vector
        def _(dve):
            for j, (sources, dst, gain) in enumerate(jobs):
                if j % 2 == 0:
                    dve.wait_ge(k.turned.sem, k.turned.at(j + 1))
                    bank = k.psum[0:dst.shape[0], j % 8, 0:dst.shape[1]]
                    if gain is None:
                        dve.tensor_copy(dst, bank).then_inc(k.turned_even.sem, 1)
                    else:
                        dve.tensor_scalar(dst, bank, gain, None, ALU.mult).then_inc(k.turned_even.sem, 1)

        @block.scalar
        def _(act):
            for j, (sources, dst, gain) in enumerate(jobs):
                if j % 2 == 1:
                    act.wait_ge(k.turned.sem, k.turned.at(j + 1))
                    bank = k.psum[0:dst.shape[0], j % 8, 0:dst.shape[1]]
                    act.activation(dst, bank, ACT.Copy, scale=1.0 if gain is None else gain)\
                       .then_inc(k.turned_odd.sem, 1)
    k.turned.passed(len(jobs))
    k.turned_even.passed((len(jobs) + 1) // 2)
    k.turned_odd.passed(len(jobs) // 2)


def row_norm(k, x, tiles, y, ctx):
    width = x.shape[2]
    ss = k.sb("norm_ss", [P, tiles], ctx=ctx)
    rms = k.sb("norm_rms", [P, tiles], ctx=ctx)
    rstd = k.sb("norm_rstd", [P, tiles], ctx=ctx)
    with k.block() as block:
        @block.scalar
        def _(act):
            for t in range(tiles):
                act.activation(y[:, t, :], x[:, t, :], ACT.Square, accum_out=ss[:, t:t + 1])\
                   .then_inc(k.squares.sem, 1)
            act.wait_ge(k.squares.sem, k.squares.at(tiles))
            act.activation(rms[:, :], ss[:, :], ACT.Sqrt, bias=k.eps[:, 0:1], scale=1.0 / width)\
               .then_inc(k.roots.sem, 1)

        @block.vector
        def _(dve):
            dve.wait_ge(k.roots.sem, k.roots.at(1))
            dve.reciprocal(rstd[:, :], rms[:, :]).then_inc(k.rstd.sem, 1)
            dve.wait_ge(k.rstd.sem, k.rstd.at(1))
            for t in range(tiles):
                dve.tensor_scalar(y[:, t, :], x[:, t, :], rstd[:, t:t + 1], None, ALU.mult)\
                   .then_inc(k.normalised.sem, 1)
    k.squares.passed(tiles)
    k.roots.passed(1)
    k.rstd.passed(1)
    k.normalised.passed(tiles)


def norm_and_turn(k, x, tiles, gain, dst, y=None):
    with ExitStack() as ctx:
        if y is None:
            y = k.sb("norm_y", [P, tiles, D], ctx=ctx)
        ss = k.sb("norm_ss", [P, tiles], ctx=ctx)
        rms = k.sb("norm_rms", [P, tiles], ctx=ctx)
        rstd = k.sb("norm_rstd", [P, tiles], ctx=ctx)
        with k.block() as block:
            @block.scalar
            def _(act):
                def root(t):
                    act.wait_ge(k.squares.sem, k.squares.at(t + 1))
                    act.activation(rms[:, t:t + 1], ss[:, t:t + 1], ACT.Sqrt, bias=k.eps[:, 0:1], scale=1.0 / D)\
                       .then_inc(k.roots.sem, 1)

                for t in range(tiles):
                    act.activation(y[:, t, :], x[:, t, :], ACT.Square, accum_out=ss[:, t:t + 1])\
                       .then_inc(k.squares.sem, 1)
                    if t >= 1:
                        root(t - 1)
                root(tiles - 1)
                for c in range(1, KT, 2):
                    act.wait_ge(k.turned.sem, k.turned.at(c + 1))
                    act.activation(dst[:, c, 0:tiles * P], k.psum[:, c, 0:tiles * P], ACT.Copy,
                                   scale=gain[:, c:c + 1]).then_inc(k.turned_odd.sem, 1)

            @block.vector
            def _(dve):
                for t in range(tiles):
                    dve.wait_ge(k.roots.sem, k.roots.at(t + 1))
                    dve.reciprocal(rstd[:, t:t + 1], rms[:, t:t + 1]).then_inc(k.rstd.sem, 1)
                    dve.wait_ge(k.rstd.sem, k.rstd.at(t + 1))
                    dve.tensor_scalar(y[:, t, :], x[:, t, :], rstd[:, t:t + 1], None, ALU.mult)\
                       .then_inc(k.normalised.sem, 1)
                for c in range(0, KT, 2):
                    dve.wait_ge(k.turned.sem, k.turned.at(c + 1))
                    dve.tensor_scalar(dst[:, c, 0:tiles * P], k.psum[:, c, 0:tiles * P], gain[:, c:c + 1], None,
                                      ALU.mult).then_inc(k.turned_even.sem, 1)

            @block.tensor
            def _(pe):
                for t in range(tiles):
                    pe.wait_ge(k.normalised.sem, k.normalised.at(t + 1))
                    for c in range(KT):
                        ins = pe.transpose(k.psum[:, c, t * P:(t + 1) * P], y[:, t, c * P:(c + 1) * P],
                                           k.ident[:, :])
                        if t == tiles - 1:
                            ins.then_inc(k.turned.sem, 1)
    for s in (k.squares, k.roots, k.rstd, k.normalised):
        s.passed(tiles)
    k.turned.passed(KT)
    k.turned_even.passed(KT // 2)
    k.turned_odd.passed(KT // 2)


def add_to_residual(k, n_halves=2):
    def evacuate(dve, j, b, bank):
        cols = slice(j * 512, (j + 1) * 512)
        return dve.tensor_tensor(k.x[:, b, cols], bank, k.x[:, b, cols], ALU.add)
    return evacuate


def project_out(k, mixT, ktiles=KT):
    u = k.consumed
    with ExitStack() as ctx:
        mix = parts_of(k, mixT, ctx)
        if ktiles == KT:
            jobs = [{"unit": u + half, "banks": token_banks(k, u + half, mix)} for half in range(2)]
        else:
            jobs = [{"unit": u, "banks": token_banks(k, u, mix, col0=half * 512, cols=512)} for half in range(2)]
        project(k, jobs, add_to_residual(k), [mix])


def score_bank(k, units, u, c):
    return k.psum[:, (u % 2) * 2 + c, 0:units[u]["keys"]]


def attention_products(k, pe, units, probs, attnT, comps):
    n = len(units)

    def scores(u):
        un = units[u]
        if u >= 2:
            pe.wait_ge(k.probs_ready.sem, k.probs_ready.at(comps * (u - 1)))
        for c in range(comps):
            last = un["mask"] is None
            ins = pe.matmul(score_bank(k, units, u, c), un["q"][c], un["k"][c], start=True, stop=last)
            if not last:
                mask, col0 = un["mask"]
                ins = pe.matmul(score_bank(k, units, u, c)[:, col0:], k.ident[:, :], mask, start=False, stop=True)
        ins.then_inc(k.scores_ready.sem, 1)

    def turn_probs(u):
        if comps == 2:
            pe.wait_ge(k.attn_ready.sem, k.attn_ready.at(u + 1))
        else:
            pe.wait_ge(k.probs_ready.sem, k.probs_ready.at(u + 1))
        if u >= 2:
            pe.wait_ge(k.attnT_ready.sem, k.attnT_ready.at(u - 1))
        for i in range(units[u]["keys"] // P):
            ins = pe.transpose(k.psum[:, 4 + u % 2, i * P:(i + 1) * P],
                               probs[:, u % 2, 0, i * P:(i + 1) * P], k.ident[:, :])
        ins.then_inc(k.attn_turned.sem, 1)

    def values(u):
        un = units[u]
        pe.wait_ge(k.attnT_ready.sem, k.attnT_ready.at(u + 1))
        if u >= 2:
            pe.wait_ge(k.out_saved.sem, k.out_saved.at(u - 1))
        tiles = un["keys"] // P
        for i in range(tiles):
            ins = pe.matmul(k.psum[:, 6 + u % 2, 0:P], attnT[:, u % 2, i, :],
                            un["v"][i], start=(i == 0), stop=(i == tiles - 1))
        ins.then_inc(k.out_ready.sem, 1)

    scores(0)
    scores(1)
    for u in range(n):
        turn_probs(u)
        if u + 2 < n:
            scores(u + 2)
        values(u)


def save_attnT(k, dve, units, attnT, u):
    dve.wait_ge(k.attn_turned.sem, k.attn_turned.at(u + 1))
    if u >= 2:
        dve.wait_ge(k.out_ready.sem, k.out_ready.at(u - 1))
    w = units[u]["keys"]
    dve.tensor_copy(attnT[:, u % 2, 0:w // P, :], k.psum[:, 4 + u % 2, 0:w].rearrange("p (i q) -> p i q", q=P))\
       .then_inc(k.attnT_ready.sem, 1)


def save_out(k, dve, units, factor, u):
    dve.wait_ge(k.out_ready.sem, k.out_ready.at(u + 1))
    out = units[u]["out"]
    first = units[u].get("first", 0)
    bank = k.psum[:, 6 + u % 2, first:first + out.shape[-1]]
    if factor is None:
        dve.tensor_copy(out, bank).then_inc(k.out_saved.sem, 1)
    else:
        dve.tensor_scalar(out, bank, factor, None, ALU.mult).then_inc(k.out_saved.sem, 1)


def attention(k, units, scale, neg_lambda=None, probs=None):
    n = len(units)
    comps = 2 if neg_lambda is not None else 1
    with ExitStack() as ctx:
        if probs is None:
            probs = k.sb("probs", [P, 2, comps, 512], ctx=ctx)
        attnT = k.sb("attnT", [P, 2, 4, P], ctx=ctx)
        top = k.sb("score_max", [P, 2, comps], ctx=ctx)
        neg = k.sb("score_negmax", [P, 2, comps], ctx=ctx)
        sums = k.sb("prob_sums", [P, 2, comps], ctx=ctx)
        inv = k.sb("prob_inv", [P, 2, comps], ctx=ctx)
        with k.block() as block:
            @block.tensor
            def _(pe):
                attention_products(k, pe, units, probs, attnT, comps)

            @block.vector
            def _(dve):
                def maxima(u):
                    dve.wait_ge(k.scores_ready.sem, k.scores_ready.at(u + 1))
                    for c in range(comps):
                        ins = dve.reduce_max(top[:, u % 2, c:c + 1], score_bank(k, units, u, c), AX)
                        if c == comps - 1:
                            k.dve.step(dve, ins)
                    if u >= 2:
                        dve.wait_ge(k.probs_ready.sem, k.probs_ready.at(comps * (u - 1)))
                    dve.tensor_scalar(neg[:, u % 2, :], top[:, u % 2, :], -scale, None, ALU.mult)\
                       .then_inc(k.negmax_ready.sem, 1)

                def weigh(u):
                    dve.wait_ge(k.probs_ready.sem, k.probs_ready.at(comps * (u + 1)))
                    if u >= 2:
                        dve.wait_ge(k.out_saved.sem, k.out_saved.at(u - 1))
                    k.dve.step(dve, dve.reciprocal(inv[:, u % 2, :], sums[:, u % 2, :]))
                    if comps == 2:
                        w = units[u]["keys"]
                        a, b = probs[:, u % 2, 0, 0:w], probs[:, u % 2, 1, 0:w]
                        k.dve.step(dve, dve.tensor_scalar(b, b, inv[:, u % 2, 1:2], neg_lambda, ALU.mult, ALU.mult))
                        dve.scalar_tensor_tensor(out=a, in0=a, scalar=inv[:, u % 2, 0:1], in1=b,
                                                 op0=ALU.mult, op1=ALU.add).then_inc(k.attn_ready.sem, 1)

                def save(u):
                    save_out(k, dve, units, None if comps == 2 else inv[:, u % 2, 0:1], u)

                maxima(0)
                maxima(1)
                for u in range(n):
                    weigh(u)
                    save_attnT(k, dve, units, attnT, u)
                    if u >= 1:
                        save(u - 1)
                    if u + 2 < n:
                        maxima(u + 2)
                save(n - 1)

            @block.scalar
            def _(act):
                for u in range(n):
                    act.wait_ge(k.negmax_ready.sem, k.negmax_ready.at(u + 1))
                    if u >= 2:
                        act.wait_ge(k.attn_turned.sem, k.attn_turned.at(u - 1))
                    for c in range(comps):
                        act.activation(probs[:, u % 2, c, 0:units[u]["keys"]], score_bank(k, units, u, c), ACT.Exp,
                                       bias=neg[:, u % 2, c:c + 1], scale=scale,
                                       accum_out=sums[:, u % 2, c:c + 1]).then_inc(k.probs_ready.sem, 1)
    for s in (k.scores_ready, k.negmax_ready, k.attn_turned, k.attnT_ready, k.out_ready, k.out_saved):
        s.passed(n)
    k.probs_ready.passed(comps * n)
    if comps == 2:
        k.attn_ready.passed(n)


def mlp(k, i):
    norm_and_turn(k, k.x, TT, k.col("g_mlp", i * KT, KT), k.hT)
    with ExitStack() as ctx:
        inputs = parts_of(k, k.hT, ctx)
        hidden = k.hT
        for part in range(4):
            u = k.consumed

            def relu_squared(dve, j, b, bank):
                h = hidden[:, 4 * j + b, :]
                k.dve.step(dve, dve.tensor_scalar(h, bank, 0.0, None, ALU.max))
                return dve.tensor_tensor(h, h, h, ALU.mult)

            project(k, [{"unit": u + half, "banks": feature_banks(k, u + half, inputs)} for half in range(2)],
                    relu_squared, [inputs] if part == 0 else [])
            project_out(k, hidden)


def heads_norm(k, groups):
    with ExitStack() as ctx:
        counts = [x.shape[1] * x.shape[2] for x, _, _ in groups]
        most = max(n * x.shape[3] for n, (x, _, _) in zip(counts, groups))
        sq = k.sb("head_squares", [P, 2, most], ctx=ctx)
        ss = k.sb("head_ss", [P, sum(counts)], ctx=ctx)
        rms = k.sb("head_rms", [P, sum(counts)], ctx=ctx)
        inv = k.sb("head_inv", [P, sum(counts)], ctx=ctx)
        spans = [slice(sum(counts[:g]), sum(counts[:g + 1])) for g in range(len(groups))]

        def squares(g):
            _, t, h, w = groups[g][0].shape
            return sq[:, g % 2, 0:t * h * w].rearrange("p (t h w) -> p t h w", t=t, h=h)

        with k.block() as block:
            @block.vector
            def _(dve):
                for g, (x, out, gain) in enumerate(groups):
                    dve.wait_ge(k.act_made.sem, k.act_made.at(g + 1))
                    dve.reduce_sum(ss[:, spans[g]].rearrange("p (t h) -> p t h", t=x.shape[1]), squares(g), AX)\
                       .then_inc(k.squares.sem, 1)
                for g, (x, out, gain) in enumerate(groups):
                    _, t, h, w = x.shape
                    dve.wait_ge(k.roots.sem, k.roots.at(g + 1))
                    k.dve.step(dve, dve.reciprocal(inv[:, spans[g]], rms[:, spans[g]]))
                    scale = inv[:, spans[g]].rearrange("p (t h) -> p t h", t=t).unsqueeze(3)
                    ins = dve.tensor_tensor(out, x, scale.broadcast_to([P, t, h, w]), ALU.mult)
                    if gain is not None:
                        k.dve.step(dve, ins)
                        spread = gain.unsqueeze(1).unsqueeze(1).broadcast_to([P, t, h, w])
                        ins = dve.tensor_tensor(out, out, spread, ALU.mult)
                    ins.then_inc(k.normalised.sem, 1)

            @block.scalar
            def _(act):
                def square(g):
                    act.activation(squares(g), groups[g][0], ACT.Square).then_inc(k.act_made.sem, 1)

                for g in range(min(2, len(groups))):
                    square(g)
                for g, (x, out, gain) in enumerate(groups):
                    act.wait_ge(k.squares.sem, k.squares.at(g + 1))
                    if g + 2 < len(groups):
                        square(g + 2)
                    act.activation(rms[:, spans[g]], ss[:, spans[g]], ACT.Sqrt, bias=k.eps[:, 0:1],
                                   scale=1.0 / x.shape[3]).then_inc(k.roots.sem, 1)
    for s in (k.act_made, k.squares, k.roots, k.normalised):
        s.passed(len(groups))


def rope(k, tensors):
    with ExitStack() as ctx:
        most = TT * max(x.shape[2] for x in tensors) * 8
        tmp = k.sb("rope_tmp", [P, 4, most], ctx=ctx)
        with k.block() as block:
            @block.vector
            def _(dve):
                for x in tensors:
                    h = x.shape[2]
                    a, b = x[:, :, :, 0:8], x[:, :, :, 8:16]
                    cos = k.cos[:, :, :].unsqueeze(2).broadcast_to([P, TT, h, 8])
                    sin = k.sin[:, :, :].unsqueeze(2).broadcast_to([P, TT, h, 8])
                    t = [tmp[:, i, 0:TT * h * 8].rearrange("p (t h e) -> p t h e", t=TT, h=h) for i in range(4)]
                    dve.tensor_tensor(t[0], a, cos, ALU.mult)
                    dve.tensor_tensor(t[1], b, sin, ALU.mult)
                    dve.tensor_tensor(t[2], b, cos, ALU.mult)
                    k.dve.step(dve, dve.tensor_tensor(t[3], a, sin, ALU.mult))
                    dve.tensor_tensor(a, t[0], t[1], ALU.subtract)
                    k.dve.step(dve, dve.tensor_tensor(b, t[2], t[3], ALU.add))


def by_head(x, width):
    return x.rearrange("p t (h w) -> p t h w", w=width)


def setup(k, weights):
    ins, nc = k.ins, k.nc
    rows = [[("g_mix", 16), ("g_xattn", 16), ("g_mem", 16), ("g_mlp", 16), ("norm_mix_g_2", 8),
             ("norm_ffn_g_2", 8), ("gq_x", 2), ("gk_x", 2), ("g_sub_a", 1), ("g_kv_b", 2), ("conv_w", 12),
             ("pool_scale", 4), ("sb_norm_g_2", 2), ("rg_norm_g_2", 2), ("hg_norm_g_2", 2), ("m2_norm_g_2", 2)],
            [("rg_conv_w_2", 8), ("rg_conv_b_2", 2), ("rg_ba_2", 2), ("rg_bx_2", 2), ("rg_lambda_2", 2),
             ("hg_lower_bounds_2", 2), ("m2_conv_w_2", 24), ("m2_conv_b_2", 6)]]
    k.cols = k.sb("feature_vectors", [P, 2, P])
    k.place = {}
    for r, group in enumerate(rows):
        at = 0
        for name, n in group:
            k.place[name] = (r, at)
            at += n
    k.cos = k.sb("cos", [P, TT, 8])
    k.sin = k.sb("sin", [P, TT, 8])
    k.neg_lambda = k.sb("neg_lambda", [P, 1])
    heads = ["gq_a", "gk_a", "gq_b", "gk_b", "g_kidx"]
    k.head_gain = k.sb("head_gains", [P, len(heads), 64])
    k.gain_of = {name: k.head_gain[:, i, :] for i, name in enumerate(heads)}
    lam_init = 0.8 - 0.6
    k.hold_units(weights)
    with ExitStack() as ctx:
        raw = k.sb("vector_rows", [P, 2, P], ctx=ctx)
        lam = k.sb("lam", [P, 4, 64], ctx=ctx)
        lam_sum = k.sb("lam_sum", [P, 2], ctx=ctx)
        pos_i = k.sb("pos_i", [P, TT], I32, ctx=ctx)
        pos = k.sb("pos", [P, TT], ctx=ctx)
        angle = k.sb("angle", [P, 2, TT, 8], ctx=ctx)
        turns = k.sb("turns", [P, 2, TT, 8], ctx=ctx)
        inv_freq = k.sb("inv_freq", [P, 8], ctx=ctx)
        vectors = []
        for r, group in enumerate(rows):
            for name, count in group:
                a = ins[name]
                if len(a.shape) == 3:
                    a = a.rearrange("a b c -> (a b) c")
                at = k.place[name][1]
                vectors.append((raw[at:at + count, r, :], a.rearrange("a (b c) -> (a b) c", c=P)))
        for i, name in enumerate(heads):
            vectors.append((k.head_gain[:, i, :], ins[name][0].partition_broadcast(P)))
        for i, name in enumerate(["lam_q1", "lam_k1", "lam_q2", "lam_k2"]):
            vectors.append((lam[:, i, :], ins[name][0].partition_broadcast(P)))
        with k.block() as block:
            @block.sync
            def _(sp):
                k.load_unit(sp, 0)
                sp.wait_ge(k.pool_made.sem, k.pool_made.at(1))
                for dst, src in vectors[1::2]:
                    sp.dma_start(dst, src).then_inc(k.small_loaded.sem, 16)
                k.load_unit(sp, 1)

            @block.gpsimd
            def _(pool):
                k.pool.step(pool, pool.memset(k.ident[:, :], 0.0))
                k.pool.step(pool, pool.memset(k.causal[:, :], 0.0))
                k.pool.step(pool, pool.memset(k.strict[:, :], 0.0))
                k.pool.step(pool, pool.memset(k.ones[:, :], 1.0))
                k.pool.step(pool, pool.memset(raw[:, :, :], 0.0))
                k.pool.step(pool, pool.affine_select(out=k.ident[:, :], in_=k.ident[:, :], compare_op=ALU.not_equal,
                                                     fill=1.0, base=0, pattern=[[-1, P]], channel_multiplier=1))
                k.pool.step(pool, pool.affine_select(out=k.causal[:, :], in_=k.causal[:, :], compare_op=ALU.is_ge,
                                                     fill=MASKED, base=0, pattern=[[-1, P]], channel_multiplier=1))
                pool.affine_select(out=k.strict[:, :], in_=k.strict[:, :], compare_op=ALU.is_gt,
                                   fill=MASKED, base=0, pattern=[[-1, P]], channel_multiplier=1)\
                    .then_inc(k.pool_made.sem, 1)

            @block.scalar
            def _(act):
                act.dma_start(k.x[:, :, :], ins["x"][0].rearrange("(t p) d -> p t d", p=P))\
                   .then_inc(k.small_loaded.sem, 16)
                with nc.allow_non_contiguous_dma(reason="512 positions, once"):
                    act.dma_start(pos_i[:, :], ins["positions"][0].rearrange("(t p) -> p t", p=P))\
                       .then_inc(k.small_loaded.sem, 16)
                act.wait_ge(k.pool_made.sem, k.pool_made.at(1))
                for dst, src in vectors[0::2]:
                    act.dma_start(dst, src).then_inc(k.small_loaded.sem, 16)
                k.round_unit(act, 0)
                total = k.small_loaded.at(16 * (2 + len(vectors)))
                act.wait_ge(k.small_loaded.sem, total)
                act.activation(pos[:, :], pos_i[:, :], ACT.Copy).then_inc(k.act_made.sem, 1)
                act.wait_ge(k.dve_made.sem, k.dve_made.at(1))
                act.activation(lam_sum[:, :], lam_sum[:, :], ACT.Exp).then_inc(k.act_made.sem, 1)
                act.wait_ge(k.dve_made.sem, k.dve_made.at(2))
                act.activation(k.sin[:, :, :], angle[:, 0], ACT.Sin)
                act.activation(k.cos[:, :, :], angle[:, 1], ACT.Sin).then_inc(k.act_made.sem, 1)

            @block.vector
            def _(dve):
                dve.memset(k.eps[:, :], EPS)
                for i in range(8):
                    ins_ = dve.memset(inv_freq[:, i:i + 1], INV_FREQ[i])
                k.dve.step(dve, ins_)
                k.rest_of_unit(dve, 0)
                dve.wait_ge(k.act_made.sem, k.act_made.at(1))
                k.dve.step(dve, dve.tensor_tensor(lam[:, 0::2, :], lam[:, 0::2, :], lam[:, 1::2, :], ALU.mult))
                dve.reduce_sum(lam_sum[:, :], lam[:, 0::2, :], AX).then_inc(k.dve_made.sem, 1)
                k.dve.step(dve, dve.tensor_tensor(angle[:, 0], pos[:, :].unsqueeze(2).broadcast_to([P, TT, 8]),
                                                  inv_freq[:, :].unsqueeze(1).broadcast_to([P, TT, 8]), ALU.mult))
                k.dve.step(dve, dve.tensor_scalar(angle[:, 1], angle[:, 0], HALF_PI, None, ALU.add))
                k.dve.step(dve, dve.tensor_scalar(turns[:], angle[:], 1.0 / TWO_PI, ROUND, ALU.mult, ALU.add))
                k.dve.step(dve, dve.tensor_scalar(turns[:], turns[:], ROUND, None, ALU.subtract))
                for part in TWO_PI_PARTS:
                    k.dve.step(dve, dve.scalar_tensor_tensor(out=angle[:], in0=turns[:], scalar=-part, in1=angle[:],
                                                             op0=ALU.mult, op1=ALU.add))
                dve.tensor_scalar(angle[:], angle[:], -PI_BELOW, PI_BELOW, ALU.max, ALU.min)\
                   .then_inc(k.dve_made.sem, 1)
                dve.wait_ge(k.act_made.sem, k.act_made.at(2))
                k.dve.step(dve, dve.tensor_tensor(k.neg_lambda[:, :], lam_sum[:, 1:2], lam_sum[:, 0:1], ALU.subtract))
                k.dve.step(dve, dve.tensor_scalar(k.neg_lambda[:, :], k.neg_lambda[:, :], lam_init, None,
                                                  ALU.subtract))
        k.act_made.passed(3)
        k.dve_made.passed(2)
        k.pool_made.passed(1)
        k.small_loaded.passed(16 * (2 + len(vectors)))
        turn(k, [([raw[:, r, :]], k.cols[:, r, :], None) for r in range(2)])
    with k.block() as block:
        @block.vector
        def _(dve):
            g_sub = k.col("g_sub_a", 0)
            k.dve.step(dve, dve.tensor_scalar(g_sub, g_sub, 1.0 - lam_init, None, ALU.mult))


PI = 3.141592653589793
TWO_PI = 2 * PI
HALF_PI = PI / 2
PI_BELOW = 3.1415925
ROUND = 12582912.0
TWO_PI_PARTS = [6.28125, 0.0019353071795864769]
INV_FREQ = [float(500000.0 ** (-(2 * i) / 16)) for i in range(8)]


def cross(k, i):
    with ExitStack() as ctx:
        memT = k.sb("memT", [P, KT, MEM], ctx=ctx)
        with ExitStack() as inner:
            mem = k.sb("mem", [P, MEM // P, D], ctx=inner)
            with k.block() as block:
                @block.scalar
                def _(act):
                    act.dma_start(mem[:, :, :], k.ins["mem"][0].rearrange("(t p) d -> p t d", p=P))\
                       .then_inc(k.small_loaded.sem, 16)
            norm_and_turn(k, k.x, TT, k.col("g_xattn", i * KT, KT), k.hT)
            with k.block() as block:
                @block.scalar
                def _(act):
                    act.wait_ge(k.small_loaded.sem, k.small_loaded.at(16))
            k.small_loaded.passed(16)
            norm_and_turn(k, mem, MEM // P, k.col("g_mem", i * KT, KT), memT)
        q = k.sb("cross_q", [P, TT, 512], ctx=ctx)
        kk = k.sb("cross_k", [P, MEM // P, 512], ctx=ctx)
        v = k.sb("cross_v", [P, MEM // P, 512], ctx=ctx)
        u = k.consumed
        outs = [q, kk, v]
        projection = ctx.enter_context(ExitStack())
        tokens = parts_of(k, k.hT, projection)
        memory = parts_of(k, memT, projection)
        project(k, [{"unit": u, "banks": token_banks(k, u, tokens)},
                    {"unit": u + 1, "banks": token_banks(k, u + 1, memory, tiles=MEM // P), "inputs_before": KT},
                    {"unit": u + 2, "banks": token_banks(k, u + 2, memory, tiles=MEM // P), "inputs_before": KT}],
                lambda dve, j, b, bank: dve.tensor_copy(outs[j][:, b, :], bank), [tokens, memory])
        projection.close()
        qT = k.sb("cross_qT", [P, 4, S], ctx=ctx)
        kT = k.sb("cross_kT", [P, 4, MEM], ctx=ctx)
        o = k.sb("cross_o", [P, TT, 512], ctx=ctx)
        per_head = [by_head(a[:, :, :], P) for a in (q, kk)]
        heads_norm(k, [(a, a, None) for a in per_head])
        turn(k, [([q[:, t, h * P:(h + 1) * P] for t in range(TT)], qT[:, h, :], k.col("gq_x", i)) for h in range(4)]
             + [([kk[:, t, h * P:(h + 1) * P] for t in range(MEM // P)], kT[:, h, :], k.col("gk_x", i))
                for h in range(4)])
        attention(k, [{"q": [qT[:, h, t * P:(t + 1) * P]], "k": [kT[:, h, :]], "keys": MEM, "mask": None,
                       "v": [v[:, m, h * P:(h + 1) * P] for m in range(MEM // P)],
                       "out": o[:, t, h * P:(h + 1) * P]} for h in range(4) for t in range(TT)],
                  float(P) ** -0.5)
        oT = qT
        turn(k, [([o[:, t, h * P:(h + 1) * P] for t in range(TT)], oT[:, h, :], None) for h in range(4)])
        project_out(k, oT, ktiles=4)


def even_mixer(k):
    norm_and_turn(k, k.x, TT, k.col("g_mix", 0, KT), k.hT)
    with ExitStack() as ctx:
        proj = k.sb("even_proj", [P, TT, sum(EVEN_UNITS)], ctx=ctx)
        starts = [sum(EVEN_UNITS[:i]) for i in range(len(EVEN_UNITS) + 1)]
        u = k.consumed
        with ExitStack() as inner:
            tokens = parts_of(k, k.hT, inner)
            project(k, [{"unit": u + j, "banks": token_banks(k, u + j, tokens)} for j in range(len(EVEN_UNITS))],
                    lambda dve, j, b, bank: dve.tensor_copy(proj[:, b, starts[j]:starts[j + 1]], bank), [tokens])
        qa, ka, va, qb = (proj[:, :, j * 512:(j + 1) * 512] for j in range(4))
        ckv, qi, ki = proj[:, :, 2048:2304], proj[:, :, 2304:2560], proj[:, :, 2560:2624]
        wi = proj[:, :, 2624:2628]
        kvb = k.sb("even_kvb", [P, TT, 2, 512], ctx=ctx)
        kb, vb = kvb[:, :, 0, :], kvb[:, :, 1, :]
        ckvT = k.hT[:, 0:2, :]
        heads_norm(k, [(by_head(ckv, 256), by_head(ckv, 256), None)])
        turn(k, [([ckv[:, t, c * P:(c + 1) * P] for t in range(TT)], ckvT[:, c, :], k.col("g_kv_b", c))
                 for c in range(2)])
        u = k.consumed
        with ExitStack() as inner:
            latent = parts_of(k, ckvT, inner)
            project(k, [{"unit": u, "banks": token_banks(k, u, latent, col0=0, cols=512)},
                        {"unit": u, "banks": token_banks(k, u, latent, col0=512, cols=512)}],
                    lambda dve, j, b, bank: dve.tensor_copy(kvb[:, b, j, :], bank), [latent])
        heads = [by_head(a, 64) for a in (qa, ka, qb, kb, ki)]
        heads_norm(k, [(a, a, k.gain_of[g]) for a, g in zip(heads, ("gq_a", "gk_a", "gq_b", "gk_b", "g_kidx"))])
        rope(k, heads + [by_head(qi, 64)])
        inner = ctx.enter_context(ExitStack())
        ki2 = proj[:, :, 2048:2048 + P]
        with k.block() as block:
            @block.vector
            def _(dve):
                dve.tensor_copy(ki2[:, :, 0:64], ki)
                k.dve.step(dve, dve.tensor_copy(ki2[:, :, 64:128], ki))
        qaT, kaT = k.hT[:, 0:4, :], k.hT[:, 4:8, :]
        qbT = k.sb("qbT", [P, 4, S], ctx=inner)
        kbT = k.sb("kbT", [P, 4, S], ctx=inner)
        qiT = k.sb("qiT", [P, 2, S], ctx=inner)
        kiT = k.sb("kiT", [P, 1, S], ctx=inner)
        turn(k, [([src[:, t, c * P:(c + 1) * P] for t in range(TT)], dst[:, c, :], None)
                 for src, dst in ((qa, qaT), (ka, kaT), (qb, qbT), (kb, kbT), (qi, qiT), (ki2, kiT))
                 for c in range(dst.shape[1])])
        unselected = k.sb("unselected", [P, TT, S], ctx=inner)
        select_keys(k, qiT, kiT, wi, unselected, ka)
        out_a, out_b = proj[:, :, 0:512], proj[:, :, 1536:2048]

        def half(a, h, cols):
            return a[64 * (h % 2):64 * (h % 2) + 64, h // 2, cols]

        attention(k, [{"q": [half(qaT, 2 * h + c, slice(t * P, (t + 1) * P)) for c in range(2)],
                       "k": [half(kaT, 2 * h + c, slice(0, (t + 1) * P)) for c in range(2)],
                       "keys": (t + 1) * P, "mask": (k.causal[:, :], t * P),
                       "v": [va[:, m, h * P:(h + 1) * P] for m in range(t + 1)],
                       "out": out_a[:, t, h * P:(h + 1) * P]} for h in range(4) for t in range(TT)],
                  64 ** -0.5, neg_lambda=k.neg_lambda[:, 0:1], probs=kb.rearrange("p (u c) s -> p u c s", u=2))
        attention(k, [{"q": [half(qbT, h, slice(t * P, (t + 1) * P))],
                       "k": [half(kbT, h, slice(0, (t + 1) * P))],
                       "keys": (t + 1) * P, "mask": (unselected[:, t, 0:(t + 1) * P], 0),
                       "v": [vb[:, m, h // 2 * P:(h // 2 + 1) * P] for m in range(t + 1)], "first": 64 * (h % 2),
                       "out": out_b[:, t, h * 64:(h + 1) * 64]} for h in range(8) for t in range(TT)],
                  64 ** -0.5, probs=kb.rearrange("p (u c) s -> p u c s", u=2))
        inner.close()
        heads_norm(k, [(by_head(out_a, P), by_head(out_a, P), None)])
        turn(k, [([src[:, t, c * P:(c + 1) * P] for t in range(TT)], k.hT[:, 4 * i + c, :],
                  k.col("g_sub_a", 0) if i == 0 else None)
                 for i, src in enumerate((out_a, out_b)) for c in range(4)])
    project_out(k, k.hT)


def select_keys(k, qiT, kiT, wi, unselected, relu):
    with ExitStack() as ctx:
        score = k.sb("index_score", [P, S], ctx=ctx)
        w = k.sb("index_weight", [P, TT, 4], ctx=ctx)
        best = k.sb("index_best", [P, 8], ctx=ctx)
        with k.block() as block:
            @block.tensor
            def _(pe):
                for t in range(TT):
                    if t >= 2:
                        pe.wait_ge(k.act_made.sem, k.act_made.at(t - 1))
                    for h in range(4):
                        rows = slice(64 * (h % 2), 64 * (h % 2) + 64)
                        ins = pe.matmul(k.psum[:, 4 * (t % 2) + h, 0:(t + 1) * P], qiT[rows, h // 2, t * P:(t + 1) * P],
                                        kiT[rows, 0, 0:(t + 1) * P], start=True, stop=True)
                    ins.then_inc(k.pe_made.sem, 1)

            @block.scalar
            def _(act):
                for t in range(TT):
                    act.wait_ge(k.pe_made.sem, k.pe_made.at(t + 1))
                    if t >= 1:
                        act.wait_ge(k.dve_made.sem, k.dve_made.at(t))
                    n = (t + 1) * P
                    act.activation(relu[:, :, 0:n], k.psum[:, 4 * (t % 2):4 * (t % 2) + 4, 0:n], ACT.Relu)\
                       .then_inc(k.act_made.sem, 1)

            @block.vector
            def _(dve):
                k.dve.step(dve, dve.tensor_scalar(w[:, :, :], wi, (4 * 64) ** -0.5, None, ALU.mult))
                for t in range(TT):
                    n = (t + 1) * P
                    dve.wait_ge(k.act_made.sem, k.act_made.at(t + 1))
                    s = score[:, 0:n]
                    k.dve.step(dve, dve.tensor_scalar(s, relu[:, 0, 0:n], w[:, t, 0:1], None, ALU.mult))
                    for h in range(1, 4):
                        k.dve.step(dve, dve.scalar_tensor_tensor(out=s, in0=relu[:, h, 0:n], scalar=w[:, t, h:h + 1],
                                                                 in1=s, op0=ALU.mult, op1=ALU.add))
                    diagonal = score[:, t * P:n]
                    k.dve.step(dve, dve.tensor_tensor(diagonal, diagonal, k.causal[:, :], ALU.add))
                    dve.tensor_copy(unselected[:, t, t * P:n], k.causal[:, :]).then_inc(k.dve_made.sem, 1)
                    if n > TOPK:
                        for r in range(TOPK // 8):
                            k.dve.step(dve, dve.max(best[:, :], s))
                            k.dve.step(dve, dve.match_replace(s, best[:, :], s, TAKEN))
                        dve.wait_ge(k.dve_made.sem, k.dve_made.at(t + 1))
                        k.dve.step(dve, dve.tensor_scalar(unselected[:, t, 0:n], s, TAKEN / 2, MASKED,
                                                          ALU.is_gt, ALU.mult))
    k.pe_made.passed(TT)
    k.act_made.passed(TT)
    k.dve_made.passed(TT)
def odd_mixer(k):
    norm_and_turn(k, k.x, TT, k.col("g_mix", KT, KT), k.hT)
    PAD = 16
    with ExitStack() as ctx:
        gb = k.sb("odd_gb", [P, 4, S], ctx=ctx)
        gc = k.sb("odd_gc", [P, 4, S], ctx=ctx)
        hc = k.sb("odd_hc", [P, 4, PAD + S], ctx=ctx)
        zd = k.sb("odd_zd", [P, 4, PAD + S], ctx=ctx)
        sums = k.sb("odd_sums", [P, 2, PAD + S], ctx=ctx)
        acc = k.sb("odd_acc", [P, S], ctx=ctx)
        wp = k.sb("odd_w_pool", [P, 4, P], ctx=ctx)
        with k.block() as block:
            @block.gpsimd
            def _(pool):
                pool.memset(sums[:, :, 0:PAD], 0.0)
                pool.memset(hc[:, :, 0:PAD], 0.0)
                k.pool.step(pool, pool.memset(zd[:, :, 0:PAD], 0.0))

            @block.scalar
            def _(act):
                act.dma_start(wp[:, :, :], k.ins["w_pool"][0].rearrange("g c d -> c g d"))\
                   .then_inc(k.small_loaded.sem, 16)
                act.wait_ge(k.small_loaded.sem, k.small_loaded.at(16))
        k.small_loaded.passed(16)
        u = k.consumed
        outs = [gb[:, :, :], gc[:, :, :], hc[:, :, PAD:], zd[:, :, PAD:]]
        with ExitStack() as inner:
            tokens = parts_of(k, k.hT, inner)
            project(k, [{"unit": u + j, "banks": feature_banks(k, u + j, tokens)} for j in range(4)],
                    lambda dve, j, b, bank: dve.tensor_copy(outs[j][:, b, :], bank), [tokens])
        mixT = k.hT
        with k.block() as block:
            @block.vector
            def _(dve):
                k.dve.step(dve, dve.tensor_tensor(hc[:, :, PAD:], hc[:, :, PAD:], gc[:, :, :], ALU.mult))
                for g in range(4):
                    k.dve.step(dve, dve.tensor_scalar(acc[:, :], hc[:, g, PAD - 2:PAD - 2 + S],
                                                      k.col("conv_w", g), None, ALU.mult))
                    for tap in (1, 2):
                        at = PAD - 2 + tap
                        k.dve.step(dve, dve.scalar_tensor_tensor(out=acc[:, :], in0=hc[:, g, at:at + S],
                                                                 scalar=k.col("conv_w", 4 * tap + g), in1=acc[:, :],
                                                                 op0=ALU.mult, op1=ALU.add))
                    k.dve.step(dve, dve.tensor_tensor(mixT[:, g, :], acc[:, :], gb[:, g, :], ALU.mult))
                for g in range(4):
                    src = zd[:, g, :]
                    for r in range(g + 1):
                        dst = sums[:, r % 2, :]
                        back = 2 ** r
                        k.dve.step(dve, dve.tensor_tensor(dst[:, PAD:], src[:, PAD:], src[:, PAD - back:PAD - back + S],
                                                          ALU.add))
                        src = dst
                    window = 2 ** (g + 1)
                    for t in range(window - 1):
                        k.dve.step(dve, dve.tensor_scalar(src[:, PAD + t:PAD + t + 1], src[:, PAD + t:PAD + t + 1],
                                                          window / (t + 1), None, ALU.mult))
                    dve.scalar_tensor_tensor(out=gb[:, g, :], in0=src[:, PAD:], scalar=1.0 / window,
                                             in1=zd[:, g, PAD:], op0=ALU.mult, op1=ALU.subtract)\
                       .then_inc(k.dve_made.sem, 1)
                    dve.wait_ge(k.dve_made.sem, k.dve_made.at(g + 1))
                for g in range(4):
                    dve.wait_ge(k.pe_made.sem, k.pe_made.at(g + 1))
                    k.dve.step(dve, dve.tensor_scalar(mixT[:, 4 + g, :], k.psum[:, g, :], k.col("pool_scale", g),
                                                      None, ALU.mult))

            @block.tensor
            def _(pe):
                for g in range(4):
                    pe.wait_ge(k.dve_made.sem, k.dve_made.at(g + 1))
                    pe.matmul(k.psum[:, g, :], wp[:, g, :], gb[:, g, :], start=True, stop=True)\
                      .then_inc(k.pe_made.sem, 1)
        k.dve_made.passed(4)
        k.pe_made.passed(4)
    project_out(k, k.hT)


PAD = 4


def stick_breaking(k, units, scale):
    n = len(units)
    with ExitStack() as ctx:
        probs = k.sb("sb_probs", [P, 2, 1, 512], ctx=ctx)
        attnT = k.sb("sb_attnT", [P, 2, 4, P], ctx=ctx)
        soft = k.sb("sb_soft", [P, 2, 512], ctx=ctx)
        pos = k.sb("sb_pos", [P, 512], ctx=ctx)
        run = k.sb("sb_run", [P, 2, 1 + 512], ctx=ctx)
        log_a = k.sb("sb_log_a", [P, 2, 512], ctx=ctx)
        neg_total = k.sb("sb_neg_total", [P, 2, 1], ctx=ctx)
        with k.block() as block:
            @block.tensor
            def _(pe):
                attention_products(k, pe, units, probs, attnT, 1)

            @block.scalar
            def _(act):
                def softs(u):
                    w = units[u]["keys"]
                    s = soft[:, u % 2, 0:w]
                    act.wait_ge(k.scores_ready.sem, k.scores_ready.at(u + 1))
                    if u >= 2:
                        act.wait_ge(k.negmax_ready.sem, k.negmax_ready.at(u - 1))
                    k.act.step(act, act.activation(s, score_bank(k, units, u, 0), ACT.Abs, scale=scale))
                    k.act.step(act, act.activation(s, s, ACT.Exp, scale=-1.0))
                    act.activation(s, s, ACT.Ln, bias=1.0).then_inc(k.act_made.sem, 1)

                softs(0)
                softs(1)
                for u in range(n):
                    w = units[u]["keys"]
                    act.wait_ge(k.negmax_ready.sem, k.negmax_ready.at(u + 1))
                    if u >= 2:
                        act.wait_ge(k.attn_turned.sem, k.attn_turned.at(u - 1))
                    act.activation(probs[:, u % 2, 0, 0:w], log_a[:, u % 2, 0:w], ACT.Exp,
                                   bias=neg_total[:, u % 2, :]).then_inc(k.probs_ready.sem, 1)
                    if u + 2 < n:
                        softs(u + 2)

            @block.vector
            def _(dve):
                k.dve.step(dve, dve.memset(run[:, :, 0:1], 0.0))

                def logs(u):
                    w = units[u]["keys"]
                    z = score_bank(k, units, u, 0)
                    r = run[:, u % 2, :]
                    dve.wait_ge(k.act_made.sem, k.act_made.at(u + 1))
                    if u >= 2:
                        dve.wait_ge(k.probs_ready.sem, k.probs_ready.at(u - 1))
                    k.dve.step(dve, dve.tensor_scalar(pos[:, 0:w], z, scale, 0.0, ALU.mult, ALU.max))
                    k.dve.step(dve, dve.tensor_tensor_scan(r[:, 1:1 + w], pos[:, 0:w], soft[:, u % 2, 0:w], 0.0,
                                                           ALU.add, ALU.add))
                    k.dve.step(dve, dve.scalar_tensor_tensor(out=log_a[:, u % 2, 0:w], in0=z, scalar=scale,
                                                             in1=r[:, 0:w], op0=ALU.mult, op1=ALU.add))
                    dve.tensor_scalar(neg_total[:, u % 2, :], r[:, w:w + 1], -1.0, None, ALU.mult)\
                       .then_inc(k.negmax_ready.sem, 1)

                logs(0)
                logs(1)
                for u in range(n):
                    save_attnT(k, dve, units, attnT, u)
                    if u >= 1:
                        save_out(k, dve, units, None, u - 1)
                    if u + 2 < n:
                        logs(u + 2)
                save_out(k, dve, units, None, n - 1)
    for s in (k.scores_ready, k.negmax_ready, k.attn_turned, k.attnT_ready, k.out_ready, k.out_saved, k.act_made,
              k.probs_ready):
        s.passed(n)


def conv4(k, dve, x, c, weight, bias, tiles, out):
    first = PAD - 3
    k.dve.step(dve, dve.tensor_scalar(out, x[:, c, first:first + S], k.col(weight, c), k.col(bias, c),
                                      ALU.mult, ALU.add))
    for tap in (1, 2, 3):
        at = first + tap
        k.dve.step(dve, dve.scalar_tensor_tensor(out=out, in0=x[:, c, at:at + S], scalar=k.col(weight, tiles * tap + c),
                                                 in1=out, op0=ALU.mult, op1=ALU.add))


def log1p_series(k, dve, e, w, sq, out):
    k.dve.step(dve, dve.tensor_scalar(w, e, 2.0, None, ALU.add))
    k.dve.step(dve, dve.reciprocal(w, w))
    k.dve.step(dve, dve.tensor_tensor(w, w, e, ALU.mult))
    k.dve.step(dve, dve.tensor_tensor(sq, w, w, ALU.mult))
    k.dve.step(dve, dve.tensor_scalar(out, sq, 2.0 / 17, 2.0 / 15, ALU.mult, ALU.add))
    for odd in (13, 11, 9, 7, 5, 3, 1):
        k.dve.step(dve, dve.tensor_tensor(out, out, sq, ALU.mult))
        k.dve.step(dve, dve.tensor_scalar(out, out, 2.0 / odd, None, ALU.add))
    k.dve.step(dve, dve.tensor_tensor(out, out, w, ALU.mult))


def feature_norm(k, o, ones, width, gain, dst, sq, rms, factor=None):
    both = width == 2 * P
    with k.block() as block:
        @block.vector
        def _(dve):
            dve.tensor_tensor(sq[:, :, :], o[:, :, :], o[:, :, :], ALU.mult).then_inc(k.dve_made.sem, 1)
            dve.wait_ge(k.act_made.sem, k.act_made.at(2))
            k.dve.step(dve, dve.reciprocal(rms[:, :, :], rms[:, :, :]))
            for c in range(2):
                ins = dve.scalar_tensor_tensor(out=dst[:, c, :], in0=o[:, c, :], scalar=k.col(gain, c),
                                               in1=rms[:, c, :], op0=ALU.mult, op1=ALU.mult)
            k.dve.step(dve, ins)
            if factor is not None:
                k.dve.step(dve, dve.tensor_tensor(dst, dst, factor, ALU.mult))

        @block.tensor
        def _(pe):
            pe.wait_ge(k.dve_made.sem, k.dve_made.at(1))
            for c in range(2):
                if both:
                    pe.matmul(k.psum[:, c, :], ones, sq[:, 0, :], start=True, stop=False)
                    ins = pe.matmul(k.psum[:, c, :], ones, sq[:, 1, :], start=False, stop=True)
                else:
                    ins = pe.matmul(k.psum[:, c, :], ones, sq[:, c, :], start=True, stop=True)
                ins.then_inc(k.pe_made.sem, 1)

        @block.scalar
        def _(act):
            for c in range(2):
                act.wait_ge(k.pe_made.sem, k.pe_made.at(c + 1))
                act.activation(rms[:, c, :], k.psum[:, c, :], ACT.Sqrt, bias=k.eps[:, 0:1], scale=1.0 / width)\
                   .then_inc(k.act_made.sem, 1)
    k.dve_made.passed(1)
    k.pe_made.passed(2)
    k.act_made.passed(2)


def rg_lru(k, x, gate, dst):
    with ExitStack() as ctx:
        wbd = k.sb("rg_weights", [P, 2, 2, P], ctx=ctx)
        xc = k.sb("rg_xc", [P, 2, S], ctx=ctx)
        r = k.sb("rg_r", [P, 2, S], ctx=ctx)
        ig = k.sb("rg_ig", [P, 2, S], ctx=ctx)
        a = k.sb("rg_a", [P, 2, S], ctx=ctx)
        th = k.sb("rg_tanh", [P, 2, S], ctx=ctx)
        mult = k.sb("rg_mult", [P, 2, S], ctx=ctx)
        g3 = k.sb("rg_gelu", [P, 2, S], ctx=ctx)
        tiny = k.sb("rg_tiny", [P, 6, 2], ctx=ctx)
        lam = k.col("rg_lambda_2", 0, 2)
        with k.block() as block:
            @block.gpsimd
            def _(pool):
                pool.memset(wbd[:], 0.0).then_inc(k.pool_made.sem, 1)

            @block.sync
            def _(sp):
                sp.wait_ge(k.pool_made.sem, k.pool_made.at(1))
                for i, name in enumerate(("rg_wa_2", "rg_wx_2")):
                    for c in range(2):
                        for n in range(2):
                            at = slice(64 * n, 64 * n + 64)
                            sp.dma_start(wbd[at, i, c, at], k.ins[name][0, 2 * c + n]).then_inc(k.small_loaded.sem, 16)

            @block.vector
            def _(dve):
                for c in range(2):
                    conv4(k, dve, x, c, "rg_conv_w_2", "rg_conv_b_2", 2, xc[:, c, :])
                dve.tensor_scalar(tiny[:, 0, :], lam, -1.0, None, ALU.mult).then_inc(k.dve_made.sem, 1)
                k.dve.step(dve, dve.tensor_tensor(g3[:, :, :], gate[:, :, :], gate[:, :, :], ALU.mult))
                k.dve.step(dve, dve.tensor_scalar(g3[:, :, :], g3[:, :, :], 0.044715, 1.0, ALU.mult, ALU.add))
                k.dve.step(dve, dve.tensor_tensor(g3[:, :, :], g3[:, :, :], gate[:, :, :], ALU.mult))
                dve.wait_ge(k.act_made.sem, k.act_made.at(1))
                log1p_series(k, dve, tiny[:, 1, :], tiny[:, 2, :], tiny[:, 3, :], tiny[:, 4, :])
                k.dve.step(dve, dve.tensor_scalar(tiny[:, 5, :], tiny[:, 0, :], 0.0, None, ALU.max))
                k.dve.step(dve, dve.tensor_tensor(tiny[:, 5, :], tiny[:, 5, :], tiny[:, 4, :], ALU.add))
                dve.tensor_scalar(tiny[:, 5, :], tiny[:, 5, :], -8.0, None, ALU.mult).then_inc(k.dve_made.sem, 1)
                dve.wait_ge(k.act_made.sem, k.act_made.at(2))
                k.dve.step(dve, dve.tensor_scalar(mult[:, :, :], th[:, :, :], -1.0, 1.0, ALU.mult, ALU.add))
                k.dve.step(dve, dve.reciprocal(mult[:, :, :], mult[:, :, :]))
                dve.scalar_tensor_tensor(out=mult[:, :, :], in0=th[:, :, :], scalar=-2.0, in1=mult[:, :, :],
                                         op0=ALU.mult, op1=ALU.mult).then_inc(k.dve_made.sem, 1)
                k.dve.step(dve, dve.tensor_tensor(xc[:, :, :], xc[:, :, :], ig[:, :, :], ALU.mult))
                dve.wait_ge(k.act_made.sem, k.act_made.at(3))
                k.dve.step(dve, dve.memset(mult[:, :, 0:1], 1.0))
                k.dve.step(dve, dve.tensor_tensor(xc[:, :, :], xc[:, :, :], mult[:, :, :], ALU.mult))
                for c in range(2):
                    ins = dve.tensor_tensor_scan(r[:, c, :], a[:, c, :], xc[:, c, :], 0.0, ALU.mult, ALU.add)
                k.dve.step(dve, ins)
                k.dve.step(dve, dve.tensor_tensor(r[:, :, :], r[:, :, :], gate[:, :, :], ALU.mult))
                k.dve.step(dve, dve.tensor_scalar(g3[:, :, :], g3[:, :, :], 0.5, 0.5, ALU.mult, ALU.add))
                k.dve.step(dve, dve.tensor_tensor(r[:, :, :], r[:, :, :], g3[:, :, :], ALU.mult))

            @block.tensor
            def _(pe):
                pe.wait_ge(k.dve_made.sem, k.dve_made.at(1))
                pe.wait_ge(k.small_loaded.sem, k.small_loaded.at(16 * 8))
                for i in range(2):
                    for c in range(2):
                        ins = pe.matmul(k.psum[:, 2 * i + c, :], wbd[:, i, c, :], xc[:, c, :], start=True, stop=True)
                ins.then_inc(k.pe_made.sem, 1)

            @block.scalar
            def _(act):
                act.wait_ge(k.dve_made.sem, k.dve_made.at(1))
                k.act.step(act, act.activation(tiny[:, 1, :], tiny[:, 0, :], ACT.Abs))
                act.activation(tiny[:, 1, :], tiny[:, 1, :], ACT.Exp, scale=-1.0).then_inc(k.act_made.sem, 1)
                act.wait_ge(k.pe_made.sem, k.pe_made.at(1))
                for c in range(2):
                    act.activation(r[:, c, :], k.psum[:, c, :], ACT.Sigmoid, bias=k.col("rg_ba_2", c))
                    ins = act.activation(ig[:, c, :], k.psum[:, 2 + c, :], ACT.Sigmoid, bias=k.col("rg_bx_2", c))
                k.act.step(act, ins)
                act.wait_ge(k.dve_made.sem, k.dve_made.at(2))
                for c in range(2):
                    act.activation(th[:, c, :], r[:, c, :], ACT.Tanh, scale=tiny[:, 5, c:c + 1])
                act.activation(g3[:, :, :], g3[:, :, :], ACT.Tanh, scale=0.7978845608028654)
                for c in range(2):
                    ins = act.activation(a[:, c, :], r[:, c, :], ACT.Exp, scale=tiny[:, 5, c:c + 1])
                ins.then_inc(k.act_made.sem, 1)
                act.wait_ge(k.dve_made.sem, k.dve_made.at(3))
                act.activation(mult[:, :, :], mult[:, :, :], ACT.Sqrt).then_inc(k.act_made.sem, 1)
        k.dve_made.passed(3)
        k.act_made.passed(3)
        k.pe_made.passed(1)
        k.pool_made.passed(1)
        k.small_loaded.passed(16 * 8)
        feature_norm(k, r, k.ones[:, :], 256, "rg_norm_g_2", dst, a, th)


def hgrn2(k, q, f, v, g, dst, scratch):
    with ExitStack() as ctx:
        key, state, read = scratch
        drive = v
        values = parts_of(k, v, ctx)
        pick = k.sb("hg_pick", [P, 3 * 64], ctx=ctx)
        pair = k.sb("hg_pair", [P, P], ctx=ctx)
        spread = k.sb("hg_spread", [P, 64, P], F32R, ctx=ctx)
        lb = k.sb("hg_lb", [P, 3, 2], ctx=ctx)
        with k.block() as block:
            @block.gpsimd
            def _(pool):
                k.pool.step(pool, pool.memset(pick[:, :], 0.0))
                k.pool.step(pool, pool.memset(pair[:, :], 0.0))
                pool.memset(pair[0:64, 0:64], 1.0)
                pool.memset(pair[64:P, 64:P], 1.0)
                pool.memset(pick[0:64, 63:64], 1.0)
                k.pool.step(pool, pool.memset(pick[64:P, 127:P], 1.0))

            @block.vector
            def _(dve):
                dve.wait_ge(k.input_rounded.sem, k.input_rounded.at(1))
                values.rest(dve)
                x = k.col("hg_lower_bounds_2", 0, 2)
                dve.tensor_tensor(lb[:, 0, :], x, x, ALU.subtract).then_inc(k.dve_made.sem, 1)
                dve.wait_ge(k.act_made.sem, k.act_made.at(1))
                k.dve.step(dve, dve.reciprocal(lb[:, 1, :], lb[:, 0, :]))
                k.dve.step(dve, dve.tensor_tensor(lb[:, 0, :], lb[:, 0, :], lb[:, 1, :], ALU.mult))
                k.dve.step(dve, dve.tensor_tensor(lb[:, 1, :], lb[:, 0, :], lb[:, 0, :], ALU.subtract))
                k.dve.step(dve, dve.tensor_scalar(lb[:, 2, :], lb[:, 1, :], -1.0, 1.0, ALU.mult, ALU.add))
                for c in range(2):
                    ins = dve.tensor_scalar(f[:, c, :], f[:, c, :], lb[:, 2, c:c + 1], lb[:, 1, c:c + 1],
                                            ALU.mult, ALU.add)
                k.dve.step(dve, ins)
                k.dve.step(dve, dve.tensor_scalar(key[:, :, :], f[:, :, :], -1.0, 1.0, ALU.mult, ALU.add))
                k.dve.step(dve, dve.tensor_tensor(q[:, :, :], q[:, :, :], read, ALU.mult))
                dve.wait_ge(k.act_made.sem, k.act_made.at(2))
                k.dve.step(dve, dve.tensor_tensor(g[:, :, :], g[:, :, :], state[:, :, :], ALU.mult))

            @block.scalar
            def _(act):
                values.round(act).then_inc(k.input_rounded.sem, 1)
                act.wait_ge(k.dve_made.sem, k.dve_made.at(1))
                act.activation(lb[:, 0, :], lb[:, 0, :], ACT.Exp)
                act.activation(f[:, :, :], f[:, :, :], ACT.Sigmoid)
                act.activation(read, q[:, :, :], ACT.Sigmoid).then_inc(k.act_made.sem, 1)
                act.activation(state[:, :, :], g[:, :, :], ACT.Sigmoid).then_inc(k.act_made.sem, 1)
                src = k.ident[:, :].rearrange("p (h v) -> p v h", h=2).unsqueeze(3).broadcast_to([P, 64, 2, 64])
                act.activation(spread[:, :, :].rearrange("p v (h m) -> p v h m", h=2), src, ACT.Copy)
        k.dve_made.passed(1)
        k.act_made.passed(2)
        k.input_rounded.passed(1)
        n = 2 * 64
        with k.block() as block:
            @block.tensor
            def _(pe):
                def spread_values(i):
                    c, w = divmod(i, 64)
                    if i >= 2:
                        pe.wait_ge(k.dve_made.sem, k.dve_made.at(i - 1))
                    pe.matmul(k.psum[:, i % 2, :], spread[:, w, :], values.high[:, c, :], start=True, stop=False)
                    pe.matmul(k.psum[:, i % 2, :], spread[:, w, :], values.low[:, c, :], start=False, stop=True)\
                      .then_inc(k.pe_made.sem, 1)

                def gather(i):
                    c, w = divmod(i, 64)
                    pe.wait_ge(k.pool_made.sem, k.pool_made.at(i + 1))
                    pe.matmul(k.psum[:, 2 + c, :], pick[:, 63 - w:63 - w + P], read[:, i % 2, :],
                              start=(w == 0), stop=(w == 63)).then_inc(k.out_ready.sem, 1)

                spread_values(0)
                spread_values(1)
                for i in range(n):
                    if i + 2 < n:
                        spread_values(i + 2)
                    gather(i)

            @block.vector
            def _(dve):
                for i in range(n):
                    c = i // 64
                    dve.wait_ge(k.pe_made.sem, k.pe_made.at(i + 1))
                    if i >= 2:
                        dve.wait_ge(k.attn_ready.sem, k.attn_ready.at(i - 1))
                    dve.tensor_tensor(drive[:, i % 2, :], k.psum[:, i % 2, :], key[:, c, :], ALU.mult)\
                       .then_inc(k.dve_made.sem, 1)
                    dve.wait_ge(k.dve_made.sem, k.dve_made.at(i + 1))
                    if i >= 2:
                        dve.wait_ge(k.pool_made.sem, k.pool_made.at(i - 1))
                    dve.tensor_tensor_scan(state[:, i % 2, :], f[:, c, :], drive[:, i % 2, :], 0.0,
                                           ALU.mult, ALU.add).then_inc(k.attn_ready.sem, 1)

            @block.gpsimd
            def _(pool):
                for i in range(n):
                    pool.wait_ge(k.attn_ready.sem, k.attn_ready.at(i + 1))
                    if i >= 2:
                        pool.wait_ge(k.out_ready.sem, k.out_ready.at(i - 1))
                    pool.tensor_tensor(read[:, i % 2, :], state[:, i % 2, :], q[:, i // 64, :], ALU.mult)\
                        .then_inc(k.pool_made.sem, 1)

            @block.scalar
            def _(act):
                for c in range(2):
                    act.wait_ge(k.out_ready.sem, k.out_ready.at(64 * (c + 1)))
                    act.activation(dst[:, c, :], k.psum[:, 2 + c, :], ACT.Copy).then_inc(k.act_made.sem, 1)
        k.pe_made.passed(n)
        k.dve_made.passed(n)
        k.attn_ready.passed(n)
        k.pool_made.passed(n)
        k.out_ready.passed(n)
        k.act_made.passed(2)
        feature_norm(k, dst, pair[:, :], 64, "hg_norm_g_2", dst, drive, state, factor=g[:, :, :])


def mamba2(k, z, xbc, dt, out, w_all):
    with ExitStack() as ctx:
        sig = k.sb("m2_sig", [P, 6, S], ctx=ctx)
        four = k.sb("m2_four", [4, 6, S], ctx=ctx)
        small = k.sb("m2_small", [4, 4], ctx=ctx)
        sel = k.sb("m2_sel", [4, 4, P], ctx=ctx)
        dtcs = k.sb("m2_dt_cs", [P, TT, 2, 4], ctx=ctx)
        xs = k.sb("m2_xs", [P, TT, 256], ctx=ctx)
        xd = k.sb("m2_xd", [P, TT, 256], ctx=ctx)
        skip = k.sb("m2_skip", [P, 4], ctx=ctx)
        later = k.sb("m2_later", [P, P], ctx=ctx)
        e, w, sq, cs, zero, lg = (four[:, i, :] for i in range(6))
        with k.block() as block:
            @block.gpsimd
            def _(pool):
                k.pool.step(pool, pool.memset(later[:, :], 0.0))
                k.pool.step(pool, pool.affine_select(out=later[:, :], in_=later[:, :], compare_op=ALU.is_ge,
                                                     fill=MASKED, base=0, pattern=[[1, P]], channel_multiplier=-1))

            @block.sync
            def _(sp):
                sp.dma_start(skip[:, :], k.ins["m2_d_2"][0].partition_broadcast(P)).then_inc(k.small_loaded.sem, 16)
                sp.dma_start(small[:, 0:1], k.ins["m2_dt_bias_2"][0].unsqueeze(1)).then_inc(k.small_loaded.sem, 16)
                sp.dma_start(small[:, 1:2], k.ins["m2_a_log_2"][0].unsqueeze(1)).then_inc(k.small_loaded.sem, 16)
                sp.wait_ge(k.small_loaded.sem, k.small_loaded.at(48))

            @block.vector
            def _(dve):
                for c in range(6):
                    conv4(k, dve, xbc, c, "m2_conv_w_2", "m2_conv_b_2", 6, sig[:, c, :])
                    dve.tensor_copy(xbc[:, c, PAD:], sig[:, c, :]).then_inc(k.dve_made.sem, 1)
                dve.wait_ge(k.small_loaded.sem, k.small_loaded.at(48))
                k.dve.step(dve, dve.tensor_scalar(dt, dt, small[:, 0:1], None, ALU.add))
                dve.tensor_scalar(lg, dt, 0.0, None, ALU.max).then_inc(k.dve_made.sem, 1)
                dve.wait_ge(k.act_made.sem, k.act_made.at(1))
                log1p_series(k, dve, e, w, sq, zero)
                k.dve.step(dve, dve.tensor_tensor(dt, zero, lg, ALU.add))
                k.dve.step(dve, dve.tensor_scalar(e, dt, small[:, 2:3], -1.0, ALU.mult, ALU.mult))
                k.dve.step(dve, dve.memset(zero, 0.0))
                dve.tensor_tensor_scan(cs, e, zero, 0.0, ALU.add, ALU.add).then_inc(k.dve_made.sem, 1)
                k.dve.step(dve, dve.tensor_copy(sel[:, :, :], k.ident[0:4, 0:4].unsqueeze(2).broadcast_to([4, 4, P])))
                for c in range(6):
                    dve.wait_ge(k.act_made.sem, k.act_made.at(c + 2))
                    ins = dve.tensor_tensor(xbc[:, c, PAD:], xbc[:, c, PAD:], sig[:, c, :], ALU.mult)
                k.dve.step(dve, ins)

            @block.scalar
            def _(act):
                act.wait_ge(k.dve_made.sem, k.dve_made.at(7))
                k.act.step(act, act.activation(e, dt, ACT.Abs))
                act.activation(small[:, 2:3], small[:, 1:2], ACT.Exp)
                act.activation(e, e, ACT.Exp, scale=-1.0).then_inc(k.act_made.sem, 1)
                for c in range(6):
                    act.activation(sig[:, c, :], sig[:, c, :], ACT.Sigmoid).then_inc(k.act_made.sem, 1)
        k.dve_made.passed(8)
        k.act_made.passed(7)
        k.small_loaded.passed(48)
        turn(k, [([xbc[:, c, PAD + t * P:PAD + (t + 1) * P] for c in range(2)], xs[:, t, :], None) for t in range(TT)]
             + [([a[:, t * P:(t + 1) * P]], dtcs[:, t, i, :], None)
                for t in range(TT) for i, a in enumerate((dt, cs))])
        arg = k.sb("m2_decay", [P, 2, S], ctx=ctx)
        steps = [(h, s) for h in range(4) for s in range(TT)]
        B, C = (xbc[:, 2:4, PAD:], xbc[:, 4:6, PAD:])
        with k.block() as block:
            @block.tensor
            def _(pe):
                for h in range(4):
                    if h >= 1:
                        pe.wait_ge(k.dve_made.sem, k.dve_made.at(1 + TT * h))
                    for s in range(TT):
                        pe.matmul(k.psum[:, s, 0:S - s * P], B[:, h // 2, s * P:(s + 1) * P], C[:, h // 2, s * P:],
                                  start=True, stop=True)
                    pe.matmul(k.psum[:, 4, :], sel[:, h, :], cs, start=True, stop=True).then_inc(k.pe_made.sem, 1)
                    pe.wait_ge(k.dve_made.sem, k.dve_made.at(1 + TT * (h + 1)))
                    if h >= 2:
                        pe.wait_ge(k.out_saved.sem, k.out_saved.at(h - 1))
                    for t in range(TT):
                        for s in range(t + 1):
                            ins = pe.matmul(k.psum[:, 5 + h % 2, t * 64:(t + 1) * 64],
                                            w_all[:, s, (t - s) * P:(t - s + 1) * P], xd[:, s, h * 64:(h + 1) * 64],
                                            start=(s == 0), stop=(s == t))
                    ins.then_inc(k.out_ready.sem, 1)

            @block.vector
            def _(dve):
                for h in range(4):
                    cols = slice(h * 64, (h + 1) * 64)
                    ins = dve.tensor_tensor(xd[:, :, cols], xs[:, :, cols],
                                            dtcs[:, :, 0, h:h + 1].broadcast_to([P, TT, 64]), ALU.mult)
                ins.then_inc(k.dve_made.sem, 1)

                def exponents(i):
                    h, s = steps[i]
                    n = S - s * P
                    a = arg[:, i % 2, 0:n]
                    if s == 0:
                        dve.wait_ge(k.pe_made.sem, k.pe_made.at(h + 1))
                    if i >= 2:
                        dve.wait_ge(k.dve_made.sem, k.dve_made.at(1 + i - 1))
                    k.dve.step(dve, dve.tensor_scalar(a, k.psum[:, 4, s * P:], dtcs[:, s, 1, h:h + 1], None,
                                                      ALU.subtract))
                    dve.tensor_tensor(a[:, 0:P], a[:, 0:P], later[:, :], ALU.add).then_inc(k.scores_ready.sem, 1)

                def weights(i):
                    h, s = steps[i]
                    n = S - s * P
                    dve.wait_ge(k.probs_ready.sem, k.probs_ready.at(i + 1))
                    if s == 0 and h >= 1:
                        dve.wait_ge(k.out_ready.sem, k.out_ready.at(h))
                    dve.tensor_tensor(w_all[:, s, 0:n], arg[:, i % 2, 0:n], k.psum[:, s, 0:n], ALU.mult)\
                       .then_inc(k.dve_made.sem, 1)

                def save(h):
                    dve.wait_ge(k.out_ready.sem, k.out_ready.at(h + 1))
                    cols = slice(h * 64, (h + 1) * 64)
                    y = k.psum[:, 5 + h % 2, 0:TT * 64].rearrange("p (t e) -> p t e", t=TT)
                    dve.scalar_tensor_tensor(out=out[:, :, cols], in0=xs[:, :, cols], scalar=skip[:, h:h + 1], in1=y,
                                             op0=ALU.mult, op1=ALU.add).then_inc(k.out_saved.sem, 1)

                for h in range(4):
                    exponents(TT * h)
                    for s in range(TT):
                        if s + 1 < TT:
                            exponents(TT * h + s + 1)
                        weights(TT * h + s)
                    if h >= 1:
                        save(h - 1)
                save(3)
                dve.wait_ge(k.out_saved.sem, k.out_saved.at(4))
                k.dve.step(dve, dve.tensor_tensor(out, out, z, ALU.mult))
                dve.wait_ge(k.act_made.sem, k.act_made.at(1))
                k.dve.step(dve, dve.tensor_tensor(out, out, sig[:, 0:2, :].rearrange("p a (b e) -> p (a b) e", b=2),
                                                  ALU.mult))

            @block.scalar
            def _(act):
                act.activation(sig[:, 0:2, :].rearrange("p a (b e) -> p (a b) e", b=2), z, ACT.Sigmoid)\
                   .then_inc(k.act_made.sem, 1)
                for i, (h, s) in enumerate(steps):
                    act.wait_ge(k.scores_ready.sem, k.scores_ready.at(i + 1))
                    a = arg[:, i % 2, 0:S - s * P]
                    act.activation(a, a, ACT.Exp).then_inc(k.probs_ready.sem, 1)
        k.pe_made.passed(4)
        k.out_ready.passed(4)
        k.out_saved.passed(4)
        k.dve_made.passed(1 + len(steps))
        k.scores_ready.passed(len(steps))
        k.probs_ready.passed(len(steps))
        k.act_made.passed(1)


def second_mixer(k, probe=None):
    norm_and_turn(k, k.x, TT, k.col("norm_mix_g_2", 0, KT), k.hT)
    with ExitStack() as ctx:
        sb_o = k.sb("sb_o", [P, TT, 256], ctx=ctx)
        rg_x = k.sb("rg_x", [P, 2, PAD + S], ctx=ctx)
        rg_g = k.sb("rg_g", [P, 2, S], ctx=ctx)
        hg = k.sb("hg_qfvg", [P, 8, S], ctx=ctx)
        z = k.sb("m2_z", [P, TT, 256], ctx=ctx)
        xbc = k.sb("m2_xbc", [P, 6, PAD + S], ctx=ctx)
        dt = k.sb("m2_dt", [4, S], ctx=ctx)
        inner = ctx.enter_context(ExitStack())
        sb_qk = k.sb("sb_qk", [P, 4, S], ctx=inner)
        sb_v = k.sb("sb_v", [P, TT, 256], ctx=inner)
        with k.block() as block:
            @block.gpsimd
            def _(pool):
                pool.memset(rg_x[:, :, 0:PAD], 0.0)
                k.pool.step(pool, pool.memset(xbc[:, :, 0:PAD], 0.0))
        u = k.consumed
        projection = inner.enter_context(ExitStack())
        tokens = parts_of(k, k.hT, projection)
        banks = [feature_banks(k, u, tokens), token_banks(k, u + 1, tokens), feature_banks(k, u + 2, tokens),
                 feature_banks(k, u + 3, tokens), feature_banks(k, u + 4, tokens), token_banks(k, u + 5, tokens),
                 feature_banks(k, u + 6, tokens), feature_banks(k, u + 7, tokens)]
        homes = [[sb_qk[:, b, :] for b in range(4)], [sb_v[:, t, :] for t in range(TT)],
                 [rg_x[:, 0, PAD:], rg_x[:, 1, PAD:], rg_g[:, 0, :], rg_g[:, 1, :]],
                 [hg[:, b, :] for b in range(4)], [hg[:, 4 + b, :] for b in range(4)],
                 [z[:, t, :] for t in range(TT)], [xbc[:, b, PAD:] for b in range(4)],
                 [xbc[:, 4, PAD:], xbc[:, 5, PAD:], dt[:, :]]]
        project(k, [{"unit": u + j, "banks": b} for j, b in enumerate(banks)],
                lambda dve, j, b, bank: dve.tensor_copy(homes[j][b], bank), [tokens])
        projection.close()
        mixT = k.hT

        def half(h, first, cols):
            return sb_qk[64 * (h % 2):64 * (h % 2) + 64, first + h // 2, cols]

        stick_breaking(k, [{"q": [half(h, 0, slice(t * P, (t + 1) * P))], "k": [half(h, 2, slice(0, (t + 1) * P))],
                            "keys": (t + 1) * P, "mask": (k.strict[:, :], t * P),
                            "v": [sb_v[:, m, h // 2 * P:(h // 2 + 1) * P] for m in range(t + 1)],
                            "first": 64 * (h % 2),
                            "out": sb_o[:, t, h * 64:(h + 1) * 64]} for h in range(4) for t in range(TT)],
                       64 ** -0.5)
        inner.close()
        heads_norm(k, [(by_head(sb_o[:, :, :], 256), by_head(sb_o[:, :, :], 256), None)])
        turn(k, [([sb_o[:, t, c * P:(c + 1) * P] for t in range(TT)], mixT[:, c, :], k.col("sb_norm_g_2", c))
                 for c in range(2)])
        rg_lru(k, rg_x, rg_g, mixT[:, 2:4, :])
        scratch = [sb_o[:, :, :].rearrange("p (c t) d -> p c (t d)", c=2), rg_g[:, :, :], rg_x[:, :, PAD:]]
        hgrn2(k, hg[:, 0:2, :], hg[:, 2:4, :], hg[:, 4:6, :], hg[:, 6:8, :], mixT[:, 4:6, :], scratch)
        mamba2(k, z[:, :, :], xbc, dt[:, :], sb_o[:, :, :], hg[:, 0:TT, :])
        heads_norm(k, [(by_head(sb_o[:, :, :], P), by_head(sb_o[:, :, :], P), None)])
        turn(k, [([sb_o[:, t, c * P:(c + 1) * P] for t in range(TT)], mixT[:, 6 + c, :], k.col("m2_norm_g_2", c))
                 for c in range(2)])
    if probe:
        probe(k)
    project_out(k, k.hT)
FF = 1024
ROUNDS = S // P
MOST_EXTRA = 4 * S // P - 1
BLOCKS = EXPERTS + MOST_EXTRA
HALF = P // 2
NOT_CHOSEN = -4096.0
PER_EXPERT = 6


class Experts:

    def __init__(self, k, name, ctx, tables, one_by_one):
        def signal(what):
            return k.ctx.enter_context(k.nc.semaphore(f"{name}_{what}"))

        self.k, self.tables = k, tables
        self.one_by_one = one_by_one
        self.ahead = 1 if one_by_one else 0
        self.loaded = [signal(f"loaded{r}") for r in range(RING)]
        self.sel_ready = signal("sel_ready")
        self.gathered = signal("gathered")
        self.xg_ready = signal("xg_ready")
        self.wsel_ready = signal("wsel_ready")
        self.sel_turned = signal("sel_turned")
        self.selT_ready = signal("selT_ready")
        self.slot_gated = signal("slot_gated")
        self.slot_gated_low = signal("slot_gated_low")
        self.up_full = signal("up_full")
        self.glu_ready = signal("glu_ready")
        self.gate_ready = signal("gate_ready")
        self.lin_ready = signal("lin_ready")
        self.prod_ready = signal("prod_ready")
        self.act_ready = signal("act_ready")
        self.act_turned = signal("act_turned")
        self.actT_ready = signal("actT_ready")
        self.down_full = signal("down_full")
        self.o_whole = signal("o_whole")
        self.o_rounded = signal("o_rounded")
        self.o_ready = signal("o_ready")
        self.scat_full = signal("scat_full")
        self.scat_added = signal("scat_added")

    def make_sel(self, dve, r, blocks=2):
        T = self.tables
        if not self.one_by_one and self.waits_from(r, 1):
            dve.wait_ge(self.gathered, 2 * r)
        for h in range(blocks):
            for t in range(TT):
                ins = dve.tensor_scalar(T.sel[:, t, h, :], T.iota[:, :], T.place[:, t, bass.ds(blocks * r + h, 1)], None,
                                        ALU.is_equal)
        ins.then_inc(self.sel_ready, 1)

    def make_wsel(self, dve, j, e, par):
        T = self.tables
        dve.tensor_copy(T.bias_ones[:, par, :], T.bias_pick[:, bass.ds(e, 1)].broadcast_to([P, P]))
        if not self.one_by_one and self.waits_from(j, 1):
            dve.wait_ge(self.sel_turned, j)
        at = bass.ds(j, 1)
        for t in range(TT):
            ins = dve.tensor_scalar(T.wsel[:, t, :], T.iota[:, :], T.place[:, t, at], T.gate[:, t, at],
                                    ALU.is_equal, ALU.mult)
        ins.then_inc(self.wsel_ready, 1)

    def save_gather(self, dve, n, half, par):
        k, T = self.k, self.tables
        dve.wait_ge(self.gathered, n + 1)
        for b in range(2):
            f = 4 * half + 2 * b
            gain = T.gain[:, f:f + 2].unsqueeze(2).broadcast_to([P, 2, 2 * P])
            ins = dve.tensor_tensor(T.xg[:, par, f:f + 2, :], k.psum[:, b, :].rearrange("p (f s) -> p f s", f=2),
                                    gain, ALU.mult)
        ins.then_inc(self.xg_ready, 1)

    def save_selT(self, dve, j, par):
        k, T = self.k, self.tables
        dve.wait_ge(self.sel_turned, j + 1)
        dve.tensor_scalar(T.selT[:, par, :], k.psum[:, 2, :], 0.0, None, ALU.is_gt).then_inc(self.selT_ready, 1)

    def rest_of_o(self, dve, j):
        dve.wait_ge(self.o_rounded, j + 1)
        self.tables.o.rest(dve).then_inc(self.o_ready, 1)

    def activate(self, dve, j, n):
        k, T = self.k, self.tables
        q = 4 * j + n
        bank = k.psum[:, 2 + n % 2, :].rearrange("p (f two) -> p f two", two=2)
        dve.wait_ge(self.up_full, q + 1)
        if n >= 2:
            dve.wait_ge(self.act_ready, q - 1)
        elif not self.one_by_one and self.waits_from(j, 1):
            dve.wait_ge(self.act_ready, q - 1)
        dve.tensor_scalar(T.glu[:, n % 2, :], bank[:, :, 0], 7.0, None, ALU.min).then_inc(self.glu_ready, 1)
        dve.tensor_scalar(T.lin[:, n % 2, :], bank[:, :, 1], 7.0, -7.0, ALU.min, ALU.max).then_inc(self.lin_ready, 1)
        dve.wait_ge(self.gate_ready, q + 1)
        dve.wait_ge(self.lin_ready, q + 1)
        dve.scalar_tensor_tensor(out=T.lin[:, n % 2, :], in0=T.lin[:, n % 2, :], scalar=1.0, in1=T.sig[:, n % 2, :],
                                 op0=ALU.add, op1=ALU.mult).then_inc(self.prod_ready, 1)
        dve.wait_ge(self.prod_ready, q + 1)
        dve.tensor_tensor(T.act[:, n * 256:(n + 1) * 256], T.lin[:, n % 2, :], T.glu[:, n % 2, :], ALU.mult)\
           .then_inc(self.act_ready, 1)

    def add(self, dve, j):
        k = self.k
        for s in range(8):
            dve.wait_ge(self.scat_full, 8 * j + s + 1)
            x = k.x[:, s // 2, (s % 2) * 512:(s % 2) * 512 + 512]
            dve.tensor_tensor(x, k.psum[:, SCATTER_BANKS[s % 4], :], x, ALU.add).then_inc(self.scat_added, 1)

    def sigmoids(self, act, j):
        T = self.tables
        for n in range(4):
            act.wait_ge(self.glu_ready, 4 * j + n + 1)
            act.activation(T.sig[:, n % 2, :], T.glu[:, n % 2, :], ACT.Sigmoid, scale=1.702)\
               .then_inc(self.gate_ready, 1)

    def save_act(self, act, j):
        k, T = self.k, self.tables
        act.wait_ge(self.act_turned, j + 1)
        act.activation(T.actT[:, :, :].rearrange("p (b f) s -> p b (f s)", b=2), k.psum[:, 4:6, :], ACT.Copy)\
           .then_inc(self.actT_ready, 1)

    def save_slot_gates(self, act, j, par):
        k, T = self.k, self.tables
        act.wait_ge(self.selT_ready, j + 1)
        act.activation(T.unread[:, :], k.psum[:, 2, :], ACT.Copy, accum_out=T.slot_gate[:, par, 0:1])\
           .then_inc(self.slot_gated, 1)
        act.wait_ge(self.slot_gated, j + 1)
        act.activation(T.slot_gate[HALF:P, par, 1:2], T.slot_gate[0:HALF, par, 0:1], ACT.Copy)\
           .then_inc(self.slot_gated_low, 1)

    def save_down(self, act, j, par):
        k, T = self.k, self.tables
        for half in range(2):
            act.wait_ge(self.down_full, 2 * j + half + 1)
            if half == 0:
                act.wait_ge(self.slot_gated_low, j + 1)
            act.activation(T.o.whole[:, half * 512:half * 512 + 512], k.psum[:, 6 + half, :], ACT.Copy,
                           scale=T.slot_gate[:, par, 0:1]).then_inc(self.o_whole, 1)
        self.round_o(act, j)

    def round_o(self, act, j):
        act.wait_ge(self.o_whole, 2 * j + 2)
        self.tables.o.round(act).then_inc(self.o_rounded, 1)

    def gather(self, pe, r, n, half):
        k, T = self.k, self.tables
        pe.wait_ge(self.sel_ready, r + 1)
        for f in range(4):
            features = slice((4 * half + f) * P, (4 * half + f + 1) * P)
            bank = k.psum[:, f // 2, (f % 2) * 2 * P:(f % 2 + 1) * 2 * P]
            for t in range(TT):
                chosen = T.sel[:, t, :, :].rearrange("p h s -> p (h s)")
                pe.matmul(bank, T.y.high[:, t, features], chosen, start=(t == 0), stop=False)
                ins = pe.matmul(bank, T.y.low[:, t, features], chosen, start=False, stop=(t == TT - 1))
        ins.then_inc(self.gathered, 1)

    def turn_sel(self, pe, j):
        k, T = self.k, self.tables
        pe.wait_ge(self.wsel_ready, j + 1)
        for t in range(TT):
            ins = pe.transpose(k.psum[:, 2, t * P:(t + 1) * P], T.wsel[:, t, :], k.ident[:, :])
        ins.then_inc(self.sel_turned, 1)

    def wait_for_up(self, pe, j, gatherings):
        pe.wait_ge(self.xg_ready, gatherings)
        pe.wait_ge(self.selT_ready, j + 1)
        pe.wait_ge(self.slot_gated, j + 1)

    def up(self, pe, j, wait_unit, xg, par):
        k, T = self.k, self.tables
        for n in range(4):
            w = wait_unit(pe, n)
            if n >= 2:
                pe.wait_ge(self.act_ready, 4 * j + n - 1)
            bank = k.psum[:, 2 + n % 2, :]
            for c in range(KT):
                pe.matmul(bank, xg[:, c, :], w[:, c, :], start=(c == 0), stop=False)
            pe.matmul(bank, T.bias_ones[:, par, :], T.bias_parts[:, n * 512:(n + 1) * 512], start=False, stop=True)\
              .then_inc(self.up_full, 1)

    def up_half(self, pe, j, wait_unit, xg, par):
        k, T = self.k, self.tables
        for pair in range(2):
            w = [wait_unit(pe, 2 * pair), wait_unit(pe, 2 * pair + 1)]
            banks = [k.psum[64 * g:64 * g + 64, 2 + pair, :] for g in range(2)]
            for c in range(KT):
                for g in range(2):
                    pe.matmul(banks[g], xg[:, c, 0:HALF], w[g][:, c, :], start=(c == 0), stop=False)
            for g in range(2):
                cols = slice((2 * pair + g) * 512, (2 * pair + g + 1) * 512)
                pe.matmul(banks[g], T.bias_ones[:, par, 0:HALF], T.bias_parts[:, cols], start=False, stop=True)\
                  .then_inc(self.up_full, 1)

    def turn_act_half(self, pe, j):
        k, T = self.k, self.tables
        pe.wait_ge(self.act_ready, 4 * j + 4)
        for i in range(4):
            ins = pe.transpose(k.psum[:, 4, i * P:(i + 1) * P], T.act[:, i * P:(i + 1) * P], k.ident[:, :])
        ins.then_inc(self.act_turned, 1)

    def down_half(self, pe, j, wait_unit):
        k, T = self.k, self.tables
        pe.wait_ge(self.actT_ready, j + 1)
        if not self.one_by_one and self.waits_from(j, 1):
            pe.wait_ge(self.scat_added, 8 * j)
        w = [wait_unit(pe, 4), wait_unit(pe, 5)]
        for c in range(KT):
            for g in range(2):
                ins = pe.matmul(k.psum[64 * g:64 * g + 64, 6, :], T.actT[:, c, 0:HALF], w[g][:, c, :],
                                start=(c == 0), stop=(c == KT - 1))
                if c == KT - 1:
                    ins.then_inc(self.down_full, 1)

    def activate_half(self, dve, j, pair):
        k, T = self.k, self.tables
        q = 4 * j + 2 * pair + 2
        bank = k.psum[:, 2 + pair, :].rearrange("p (f two) -> p f two", two=2)
        dve.wait_ge(self.up_full, q)
        if pair or (not self.one_by_one and self.waits_from(j, 1)):
            dve.wait_ge(self.act_ready, q - 2)
        dve.tensor_scalar(T.glu[:, pair, :], bank[:, :, 0], 7.0, None, ALU.min).then_inc(self.glu_ready, 2)
        dve.tensor_scalar(T.lin[:, pair, :], bank[:, :, 1], 7.0, -7.0, ALU.min, ALU.max).then_inc(self.lin_ready, 2)
        dve.wait_ge(self.gate_ready, q)
        dve.wait_ge(self.lin_ready, q)
        dve.scalar_tensor_tensor(out=T.lin[:, pair, :], in0=T.lin[:, pair, :], scalar=1.0, in1=T.sig[:, pair, :],
                                 op0=ALU.add, op1=ALU.mult).then_inc(self.prod_ready, 2)
        dve.wait_ge(self.prod_ready, q)
        dve.tensor_tensor(T.act[:, pair * 256:(pair + 1) * 256], T.lin[:, pair, :], T.glu[:, pair, :], ALU.mult)\
           .then_inc(self.act_ready, 2)

    def sigmoids_half(self, act, j):
        T = self.tables
        for pair in range(2):
            act.wait_ge(self.glu_ready, 4 * j + 2 * pair + 2)
            act.activation(T.sig[:, pair, :], T.glu[:, pair, :], ACT.Sigmoid, scale=1.702).then_inc(self.gate_ready, 2)

    def save_act_half(self, act, j):
        k, T = self.k, self.tables
        act.wait_ge(self.act_turned, j + 1)
        turned = k.psum[:, 4, :].rearrange("p (pair h g s) -> p pair g h s", pair=2, h=2, g=2)
        home = T.actT[:, :, :].rearrange("p (pair g h) s -> p pair g h s", pair=2, g=2)
        act.activation(home[:, 0, :, :, 0:HALF], turned[:, 0], ACT.Copy)
        act.activation(home[:, 1, :, :, 0:HALF], turned[:, 1], ACT.Copy).then_inc(self.actT_ready, 1)

    def save_down_half(self, act, j, par):
        k, T = self.k, self.tables
        act.wait_ge(self.down_full, 2 * j + 2)
        act.wait_ge(self.slot_gated_low, j + 1)
        for g in range(2):
            rows = slice(HALF * g, HALF * g + HALF)
            act.activation(T.o.whole[0:HALF, g * 512:g * 512 + 512], k.psum[rows, 6, :], ACT.Copy,
                           scale=T.slot_gate[rows, par, g:g + 1]).then_inc(self.o_whole, 1)
        self.round_o(act, j)

    def turn_act(self, pe, j):
        k, T = self.k, self.tables
        pe.wait_ge(self.act_ready, 4 * j + 4)
        for f in range(KT):
            ins = pe.transpose(k.psum[:, 4 + f // 4, (f % 4) * P:(f % 4 + 1) * P], T.act[:, f * P:(f + 1) * P],
                               k.ident[:, :])
        ins.then_inc(self.act_turned, 1)

    def down(self, pe, j, wait_unit):
        k, T = self.k, self.tables
        pe.wait_ge(self.actT_ready, j + 1)
        if not self.one_by_one and self.waits_from(j, 1):
            pe.wait_ge(self.scat_added, 8 * j)
        for half in range(2):
            w = wait_unit(pe, 4 + half)
            for c in range(KT):
                ins = pe.matmul(k.psum[:, 6 + half, :], T.actT[:, c, :], w[:, c, :], start=(c == 0),
                                stop=(c == KT - 1))
            ins.then_inc(self.down_full, 1)

    def scatter(self, pe, j, par, gatherings):
        k, T = self.k, self.tables
        pe.wait_ge(self.o_ready, j + 1)
        for s in range(8):
            if s == 2:
                pe.wait_ge(self.xg_ready, gatherings)
            if s >= 4:
                pe.wait_ge(self.scat_added, 8 * j + s - 3 + self.ahead)
            t, half = s // 2, s % 2
            bank, slots = k.psum[:, SCATTER_BANKS[s % 4], :], T.selT[:, par, t * P:(t + 1) * P]
            cols = slice(half * 512, half * 512 + 512)
            pe.matmul(bank, slots, T.o.high[:, cols], start=True, stop=False)
            pe.matmul(bank, slots, T.o.low[:, cols], start=False, stop=True).then_inc(self.scat_full, 1)

    def unit_used(self, eng, j, n):
        if n < 4:
            eng.wait_ge(self.up_full, 4 * j + n + 1)
        else:
            eng.wait_ge(self.down_full, 2 * j + n - 3)

    @staticmethod
    def waits_from(j, first):
        return not isinstance(j, int) or j >= first


SCATTER_BANKS = [6, 7, 0, 1]


class Tables:
    pass


def expert_unit(k, e, n):
    if n < 4:
        w = k.ins["moe_w_gu_2"][0][bass.ds(e, 1), :, n * 512:(n + 1) * 512]
    else:
        w = k.ins["moe_w_down_2"][0][bass.ds(e, 1), :, (n - 4) * 512:(n - 3) * 512]
    return w.rearrange("e (k p) n -> p (e k) n", p=P)


def ring_view(k, slot):
    return k.ring[:, slot, :].rearrange("p (k n) -> p k n", k=KT)


def experts(k):
    with ExitStack() as ctx:
        k.ring = k.sb("expert_ring", [P, RING, UNIT], ctx=ctx)
        T = Tables()
        T.y = Parts(None, *(k.sb(name, [P, TT, D], F32R, ctx=ctx)[:, :, :] for name in ("moe_y_high", "moe_y_low")))
        T.gain = k.col("norm_ffn_g_2", 0, KT)
        T.place = k.sb("moe_place", [P, TT, BLOCKS], ctx=ctx)
        T.gate = k.sb("moe_gate", [P, TT, BLOCKS], ctx=ctx)
        T.iota = k.sb("moe_iota", [P, P], ctx=ctx)
        T.ints = k.sb("moe_ints", [P, 2 + MOST_EXTRA], I32, ctx=ctx)
        T.ids = k.sb("moe_ids", [P, EXPERTS], ctx=ctx)
        T.counts = k.sb("moe_counts", [P, EXPERTS], ctx=ctx)
        T.left = k.sb("moe_left", [P, MOST_EXTRA], I32, ctx=ctx)
        T.count = k.sb("moe_count", [P, EXPERTS], I32, ctx=ctx)
        with k.block() as block:
            base = Experts(k, "first", ctx, T, False)

            @block.sync
            def _(sp):
                for n in range(RING):
                    sp.dma_start(ring_view(k, n), expert_unit(k, 0, n)).then_inc(base.loaded[n], 16)
        T.bias_parts = k.sb("moe_bias_parts", [P, 2 * FF], BF16, ctx=ctx)
        T.bias_pick = k.sb("moe_bias_pick", [P, EXPERTS], BF16, ctx=ctx)
        with ExitStack() as inner:
            y = k.sb("moe_y", [P, TT, D], ctx=inner)
            norm_and_turn(k, k.x, TT, T.gain, k.hT, y)
            T.y.whole = y[:, :, :]
            route(k, T)
        T.sel = k.sb("moe_sel", [P, TT, 2, P], F32R, ctx=ctx)
        T.bias_ones = k.sb("moe_bias_ones", [P, 2, P], BF16, ctx=ctx)
        T.wsel = k.sb("moe_wsel", [P, TT, P], ctx=ctx)
        T.selT = k.sb("moe_selT", [P, 2, S], F32R, ctx=ctx)
        T.unread = k.sb("moe_unread", [P, S], ctx=ctx)
        T.slot_gate = k.sb("moe_slot_gate", [P, 2, 2], ctx=ctx)
        T.xg = k.sb("moe_xg", [P, 2, KT, 2 * P], ctx=ctx)
        T.glu = k.sb("moe_glu", [P, 2, 256], ctx=ctx)
        T.lin = k.sb("moe_lin", [P, 2, 256], ctx=ctx)
        T.sig = k.sb("moe_sig", [P, 2, 256], ctx=ctx)
        T.act = k.sb("moe_act", [P, FF], ctx=ctx)
        T.actT = k.sb("moe_actT", [P, KT, P], ctx=ctx)
        T.o = parts_of(k, k.sb("moe_o", [P, D], ctx=ctx), ctx)
        extras = Extras(k, T, ctx)
        with k.block() as block:
            @block.gpsimd
            def _(pool):
                extras.count_off(pool)
                k.pool.step(pool, pool.memset(T.o.whole, 0.0))
        later = Experts(k, "extra", ctx, T, True)
        first_blocks(k, base, T, extras, later)
        extra_blocks(k, later, T)


class Extras:
    NC = (ROUNDS - 1) * EXPERTS

    def __init__(self, k, T, ctx):
        self.k, self.T = k, T
        self.known = k.ctx.enter_context(k.nc.semaphore("extras_known"))
        self.flag = k.sb("extra_flag", [P, ROUNDS - 1, EXPERTS], ctx=ctx)
        self.order = k.sb("extra_order", [P, 1 + self.NC], ctx=ctx)
        self.zero = k.sb("extra_zero", [P, self.NC], ctx=ctx)
        self.nth = k.sb("extra_nth", [P, MOST_EXTRA], ctx=ctx)
        self.pick = k.sb("extra_pick", [P, MOST_EXTRA, self.NC], ctx=ctx)
        self.prod = k.sb("extra_prod", [P, MOST_EXTRA, self.NC], ctx=ctx)
        self.cand = k.sb("extra_cand", [P, 2, ROUNDS - 1, EXPERTS], ctx=ctx)
        self.left = k.sb("extra_left", [P, MOST_EXTRA], ctx=ctx)
        self.num = k.sb("extra_num", [P, 2 + MOST_EXTRA], ctx=ctx)

    def count_off(self, pool):
        self.k.pool.step(pool, pool.iota(self.nth[:, :], pattern=[[1, MOST_EXTRA]], base=0, channel_multiplier=0,
                                         allow_small_or_imprecise_dtypes=True))

    def look_up(self, dve, values, out):
        spread = values.rearrange("p r e -> p (r e)").unsqueeze(1).broadcast_to([P, MOST_EXTRA, self.NC])
        self.k.dve.step(dve, dve.tensor_tensor(self.prod[:, :, :], self.pick[:, :, :], spread, ALU.mult))
        return dve.reduce_sum(out, self.prod[:, :, :], AX)

    def find(self, dve):
        k, T, NC = self.k, self.T, self.NC
        step = lambda ins: k.dve.step(dve, ins)
        for r in range(1, ROUNDS):
            ins = dve.tensor_scalar(self.flag[:, r - 1, :], T.counts[:, :], float(r * P), None, ALU.is_gt)
        step(ins)
        dve.memset(self.zero[:, :], 0.0)
        dve.memset(self.num[:, 1 + MOST_EXTRA:], 0.0)
        step(dve.memset(self.order[:, 0:1], 0.0))
        flat = self.flag[:, :, :].rearrange("p r e -> p (r e)")
        step(dve.tensor_tensor_scan(self.order[:, 1:], flat, self.zero[:, :], 0.0, ALU.add, ALU.add))
        step(dve.tensor_tensor(self.pick[:, :, :],
                               self.order[:, 0:NC].unsqueeze(1).broadcast_to([P, MOST_EXTRA, NC]),
                               self.nth[:, :].unsqueeze(2).broadcast_to([P, MOST_EXTRA, NC]), ALU.is_equal))
        step(dve.tensor_tensor(self.pick[:, :, :], self.pick[:, :, :],
                               flat.unsqueeze(1).broadcast_to([P, MOST_EXTRA, NC]), ALU.mult))
        step(dve.tensor_copy(self.num[:, 0:1], self.order[:, NC:NC + 1]))
        step(dve.tensor_copy(self.cand[:, 0], T.ids[:, :].unsqueeze(1).broadcast_to([P, ROUNDS - 1, EXPERTS])))
        step(self.look_up(dve, self.cand[:, 0], self.num[:, 1:1 + MOST_EXTRA]))
        for r in range(1, ROUNDS):
            step(dve.tensor_scalar(self.cand[:, 1, r - 1, :], T.counts[:, :], float(r * P), None, ALU.subtract))
        step(self.look_up(dve, self.cand[:, 1], self.left[:, :]))
        step(dve.tensor_copy(T.left[:, :], self.left[:, :]))
        dve.tensor_copy(T.ints[:, :], self.num[:, :]).then_inc(self.known, 1)

    def fill(self, dve, t):
        k, T = self.k, self.T
        for r in range(1, ROUNDS):
            k.dve.step(dve, dve.tensor_scalar(self.cand[:, 0, r - 1, :], T.place[:, t, 0:EXPERTS], float(r * P), None,
                                              ALU.subtract))
            k.dve.step(dve, dve.tensor_copy(self.cand[:, 1, r - 1, :], T.gate[:, t, 0:EXPERTS]))
        k.dve.step(dve, self.look_up(dve, self.cand[:, 0], T.place[:, t, EXPERTS:BLOCKS]))
        k.dve.step(dve, self.look_up(dve, self.cand[:, 1], T.gate[:, t, EXPERTS:BLOCKS]))


def first_blocks(k, E, T, extras, later):
    PER_ROUND = 4
    rounds = EXPERTS // PER_ROUND
    with k.block() as block:
        def wait_unit_of(i, b):
            def wait_unit(pe, n):
                m = PER_EXPERT * b + n
                pe.wait_ge(E.loaded[m % RING], 16 * (PER_EXPERT * i + m // RING + 1))
                return ring_view(k, m % RING)
            return wait_unit

        def in_rounds(eng, step):
            for b in range(PER_ROUND):
                step(0, b, b, True, False)
            with eng.Fori(1, rounds - 1) as i:
                for b in range(PER_ROUND):
                    step(i, b, PER_ROUND * i + b, False, False)
            for b in range(PER_ROUND):
                step(rounds - 1, b, PER_ROUND * (rounds - 1) + b, False, True)

        @block.sync
        def _(sp):
            def step(i, b, j, first, last):
                for n in range(PER_EXPERT):
                    m = PER_EXPERT * b + n + RING
                    if last and m >= PER_ROUND * PER_EXPERT:
                        continue
                    E.unit_used(sp, j, n)
                    e = PER_ROUND * i + m // PER_EXPERT
                    sp.dma_start(ring_view(k, m % RING), expert_unit(k, e, m % PER_EXPERT))\
                      .then_inc(E.loaded[m % RING], 16)
            in_rounds(sp, step)
            sp.wait_ge(extras.known, 1)
            e = sp.value_load(T.ints[0:1, 1:2], min_val=0, max_val=EXPERTS - 1)
            for r in range(RING):
                E.unit_used(sp, EXPERTS - 1, PER_EXPERT - RING + r)
                sp.dma_start(ring_view(k, r), expert_unit(k, e, r)).then_inc(later.loaded[r], 16)

        def is_half(eng, j):
            return eng.value_load(T.count[0:1, bass.ds(j, 1)], min_val=0, max_val=S) < HALF + 1

        @block.tensor
        def _(pe):
            def step(i, b, j, first, last):
                half = is_half(pe, j)
                h = b % 2
                pair = (PER_ROUND // 2) * i + b // 2
                xg = T.xg[:, b // 2, :, h * P:(h + 1) * P]
                with pe.If(half):
                    E.wait_for_up(pe, j, 2 * pair + 2)
                    E.up_half(pe, j, wait_unit_of(i, b), xg, h)
                with pe.Else():
                    E.wait_for_up(pe, j, 2 * pair + 2)
                    E.up(pe, j, wait_unit_of(i, b), xg, h)
                if not (first and b == 0):
                    E.scatter(pe, j - 1, 1 - h, EXPERTS if last and b >= 2 else j + 2)
                with pe.If(half):
                    E.turn_act_half(pe, j)
                with pe.Else():
                    E.turn_act(pe, j)
                if not (last and b >= 2):
                    if not (first and b == 0):
                        pe.wait_ge(E.scat_added, 8 * j)
                    else:
                        pe.wait_ge(E.xg_ready, 2)
                    E.gather(pe, pair + 1, j + 2, h)
                if not (last and b == 3):
                    E.turn_sel(pe, j + 1)
                with pe.If(half):
                    E.down_half(pe, j, wait_unit_of(i, b))
                with pe.Else():
                    E.down(pe, j, wait_unit_of(i, b))

            E.gather(pe, 0, 0, 0)
            pe.wait_ge(E.xg_ready, 1)
            E.gather(pe, 0, 1, 1)
            E.turn_sel(pe, 0)
            in_rounds(pe, step)
            E.scatter(pe, EXPERTS - 1, 1, EXPERTS)

        @block.vector
        def _(dve):
            def step(i, b, j, first, last):
                with dve.If(is_half(dve, j)):
                    E.activate_half(dve, j, 0)
                    E.activate_half(dve, j, 1)
                with dve.Else():
                    for n in range(4):
                        E.activate(dve, j, n)
                if not (first and b == 0):
                    E.add(dve, j - 1)
                if not (last and b >= 2):
                    E.save_gather(dve, j + 2, b % 2, 1 - b // 2)
                if not (last and b == 3):
                    E.save_selT(dve, j + 1, 1 - b % 2)
                if not (last and b >= 2):
                    E.make_wsel(dve, j + 2, j + 2, b % 2)
                if b % 2 == 1 and not (last and b >= 1):
                    E.make_sel(dve, (PER_ROUND // 2) * i + b // 2 + 2)
                E.rest_of_o(dve, j)
                if first:
                    extras.fill(dve, b)

            E.make_sel(dve, 0)
            E.make_wsel(dve, 0, 0, 0)
            E.save_gather(dve, 0, 0, 0)
            E.save_gather(dve, 1, 1, 0)
            E.make_sel(dve, 1)
            E.save_selT(dve, 0, 0)
            E.make_wsel(dve, 1, 1, 1)
            extras.find(dve)
            in_rounds(dve, step)
            E.add(dve, EXPERTS - 1)

        @block.scalar
        def _(act):
            def step(i, b, j, first, last):
                half = is_half(act, j)
                with act.If(half):
                    E.sigmoids_half(act, j)
                    E.save_act_half(act, j)
                with act.Else():
                    E.sigmoids(act, j)
                    E.save_act(act, j)
                if not (last and b == 3):
                    E.save_slot_gates(act, j + 1, 1 - b % 2)
                with act.If(half):
                    E.save_down_half(act, j, b % 2)
                with act.Else():
                    E.save_down(act, j, b % 2)

            E.save_slot_gates(act, 0, 0)
            in_rounds(act, step)


def extra_blocks(k, E, T):
    place, gate = T.place, T.gate
    T.place, T.gate = place[:, :, EXPERTS:BLOCKS], gate[:, :, EXPERTS:BLOCKS]
    with k.block() as block:
        def each(eng, body):
            count = eng.value_load(T.ints[0:1, 0:1], min_val=0, max_val=MOST_EXTRA)
            with eng.Fori(0, MOST_EXTRA) as b:
                with eng.If(b < count):
                    body(b)

        def is_half(eng, b):
            return eng.value_load(T.left[0:1, bass.ds(b, 1)], min_val=0, max_val=S) < HALF + 1

        def expert_of(eng, b):
            return eng.value_load(T.ints[0:1, bass.ds(b + 1, 1)], min_val=0, max_val=EXPERTS - 1)

        def wait_unit_of(b):
            def wait_unit(pe, n):
                slot = n % RING
                per_block = 2 if slot < PER_EXPERT - RING else 1
                pe.wait_ge(E.loaded[slot], 16 * (per_block * b + n // RING + 1))
                return ring_view(k, slot)
            return wait_unit

        @block.sync
        def _(sp):
            def load(e, n):
                sp.dma_start(ring_view(k, n % RING), expert_unit(k, e, n)).then_inc(E.loaded[n % RING], 16)

            def body(b):
                e = expert_of(sp, b)
                for n in range(RING, PER_EXPERT):
                    E.unit_used(sp, b, n - RING)
                    load(e, n)
                with sp.If(b + 1 < count):
                    following = expert_of(sp, b + 1)
                    for n in range(RING):
                        E.unit_used(sp, b, n if n >= PER_EXPERT - RING else n + RING)
                        load(following, n)

            for r in range(RING):
                sp.wait_ge(E.loaded[r], 16)
            count = sp.value_load(T.ints[0:1, 0:1], min_val=0, max_val=MOST_EXTRA)
            each(sp, body)

        @block.tensor
        def _(pe):
            def body(b):
                pe.wait_ge(E.scat_added, 8 * b + 1)
                E.gather(pe, b, 2 * b, 0)
                pe.wait_ge(E.xg_ready, 2 * b + 1)
                E.gather(pe, b, 2 * b + 1, 1)
                E.turn_sel(pe, b)
                with pe.If(is_half(pe, b)):
                    E.wait_for_up(pe, b, 2 * b + 2)
                    E.up_half(pe, b, wait_unit_of(b), T.xg[:, 0, :, 0:P], 0)
                    E.turn_act_half(pe, b)
                    E.down_half(pe, b, wait_unit_of(b))
                with pe.Else():
                    E.wait_for_up(pe, b, 2 * b + 2)
                    E.up(pe, b, wait_unit_of(b), T.xg[:, 0, :, 0:P], 0)
                    E.turn_act(pe, b)
                    E.down(pe, b, wait_unit_of(b))
                E.scatter(pe, b, 0, 2 * b + 2)
            each(pe, body)

        @block.vector
        def _(dve):
            def body(b):
                E.make_sel(dve, b, blocks=1)
                E.make_wsel(dve, b, expert_of(dve, b), 0)
                E.save_gather(dve, 2 * b, 0, 0)
                E.save_gather(dve, 2 * b + 1, 1, 0)
                E.save_selT(dve, b, 0)
                with dve.If(is_half(dve, b)):
                    E.activate_half(dve, b, 0)
                    E.activate_half(dve, b, 1)
                with dve.Else():
                    for n in range(4):
                        E.activate(dve, b, n)
                E.rest_of_o(dve, b)
                E.add(dve, b)
            dve.memset(T.glu[:, 0, 0:1], 0.0).then_inc(E.scat_added, 1)
            each(dve, body)

        @block.scalar
        def _(act):
            def body(b):
                E.save_slot_gates(act, b, 0)
                with act.If(is_half(act, b)):
                    E.sigmoids_half(act, b)
                    E.save_act_half(act, b)
                    E.save_down_half(act, b, 0)
                with act.Else():
                    E.sigmoids(act, b)
                    E.save_act(act, b)
                    E.save_down(act, b, 0)
            each(act, body)


def route(k, T):
    with ExitStack() as ctx:
        bias = k.sb("moe_bias", [P, 2 * FF], ctx=ctx)
        rows = [slice(i * EXPERTS, (i + 1) * EXPERTS) for i in range(3)]
        wr = k.sb("router_w", [P, KT, EXPERTS], ctx=ctx)
        br = k.sb("router_b", [P, EXPERTS], ctx=ctx)
        bd = k.sb("b_down", [EXPERTS, D], ctx=ctx)
        logits = k.sb("logits", [P, TT, EXPERTS], ctx=ctx)
        best = k.sb("best", [P, TT, 8], ctx=ctx)
        index = k.sb("best_index", [P, TT, 8], U32, ctx=ctx)
        index_f = k.sb("best_index_f", [P, TT, 8], ctx=ctx)
        gates = k.sb("gates", [P, TT, 4], ctx=ctx)
        neg = k.sb("neg_best", [P, TT], ctx=ctx)
        total = k.sb("gate_total", [P, TT], ctx=ctx)
        hot = k.sb("chosen_one", [P, TT, EXPERTS], ctx=ctx)
        chosen = k.sb("chosen", [P, TT, EXPERTS], ctx=ctx)
        before = k.sb("before", [P, P], ctx=ctx)
        placeT = k.sb("gateT", [EXPERTS, S], ctx=ctx)
        place, gate = T.place[:, :, 0:EXPERTS], T.gate[:, :, 0:EXPERTS]
        with k.block() as block:
            @block.gpsimd
            def _(pool):
                pool.iota(T.iota[:, :], pattern=[[1, P]], base=0, channel_multiplier=0,
                          allow_small_or_imprecise_dtypes=True)
                pool.iota(T.ids[:, :], pattern=[[1, EXPERTS]], base=0, channel_multiplier=0,
                          allow_small_or_imprecise_dtypes=True)
                pool.memset(bias[:, :], 0.0).then_inc(k.pool_made.sem, 1)
                pool.memset(T.place[:, :, EXPERTS:BLOCKS], NOT_CHOSEN)
                pool.memset(T.gate[:, :, EXPERTS:BLOCKS], 0.0)
                k.pool.step(pool, pool.memset(before[:, :], 1.0))
                pool.affine_select(out=before[:, :], in_=before[:, :], compare_op=ALU.is_gt, fill=0.0, base=0,
                                   pattern=[[1, P]], channel_multiplier=-1).then_inc(k.pool_made.sem, 1)

            @block.sync
            def _(sp):
                sp.dma_start(wr[:, :, :], k.ins["router_w_2"][0].rearrange("(k p) e -> p k e", p=P))\
                  .then_inc(k.small_loaded.sem, 16)
                sp.dma_start(br[:, :], k.ins["router_b_2"][0].partition_broadcast(P)).then_inc(k.small_loaded.sem, 16)
                sp.dma_start(bd[:, :], k.ins["moe_b_down_2"][0]).then_inc(k.small_loaded.sem, 16)
                sp.wait_ge(k.pool_made.sem, k.pool_made.at(1))
                for r in rows:
                    sp.dma_start(bias[r, :], k.ins["moe_b_gu_2"][0]).then_inc(k.bias_loaded.sem, 16)

            @block.tensor
            def _(pe):
                pe.wait_ge(k.small_loaded.sem, k.small_loaded.at(48))
                for t in range(TT):
                    for c in range(KT):
                        ins = pe.matmul(k.psum[:, 0, t * EXPERTS:(t + 1) * EXPERTS], k.hT[:, c, t * P:(t + 1) * P],
                                        wr[:, c, :], start=(c == 0), stop=(c == KT - 1))
                ins.then_inc(k.pe_made.sem, 1)
                pe.wait_ge(k.dve_made.sem, k.dve_made.at(2))
                pe.wait_ge(k.pool_made.sem, k.pool_made.at(2))
                for t in range(TT):
                    for s in range(t + 1):
                        pe.matmul(k.psum[:, 1, t * EXPERTS:(t + 1) * EXPERTS],
                                  before[:, :] if s == t else k.ones[:, :], chosen[:, s, :],
                                  start=(s == 0), stop=(s == t))
                for s in range(TT):
                    ins = pe.matmul(k.psum[:, 2, 0:EXPERTS], k.ones[:, :], chosen[:, s, :], start=(s == 0),
                                    stop=(s == TT - 1))
                ins.then_inc(k.pe_made.sem, 1)
                pe.wait_ge(k.dve_made.sem, k.dve_made.at(3))
                for t in range(TT):
                    ins = pe.transpose(k.psum[0:EXPERTS, 3, t * P:(t + 1) * P], gate[:, t, :], k.ident[:, :])
                ins.then_inc(k.pe_made.sem, 1)
                pe.wait_ge(k.act_made.sem, k.act_made.at(2))
                for s in range(8):
                    if s >= 4:
                        pe.wait_ge(k.out_saved.sem, k.out_saved.at(s - 3))
                    pe.matmul(k.psum[:, 4 + s % 4, :], placeT[:, (s // 2) * P:(s // 2 + 1) * P],
                              bd[:, (s % 2) * 512:(s % 2) * 512 + 512], start=True, stop=True)\
                      .then_inc(k.out_ready.sem, 1)

            @block.vector
            def _(dve):
                step = lambda ins: k.dve.step(dve, ins)
                pick = T.bias_pick[:, :]
                step(dve.tensor_tensor(pick, k.ident[:, rows[0]], k.ident[:, rows[1]], ALU.add))
                step(dve.tensor_tensor(pick, pick, k.ident[:, rows[2]], ALU.add))
                dve.wait_ge(k.input_rounded.sem, k.input_rounded.at(1))
                T.y.rest(dve)
                for i in (1, 2):
                    dve.wait_ge(k.bias_rounded.sem, k.bias_rounded.at(i))
                    for r in rows[i:]:
                        ins = dve.tensor_tensor(bias[r, :], bias[r, :], T.bias_parts[r, :], ALU.subtract)
                    ins.then_inc(k.bias_rest.sem, 1)
                dve.wait_ge(k.pe_made.sem, k.pe_made.at(1))
                dve.wait_ge(k.pool_made.sem, k.pool_made.at(2))
                step(dve.tensor_tensor(logits[:, :, :], k.psum[:, 0, 0:TT * EXPERTS].rearrange("p (t e) -> p t e", t=TT),
                                       br[:, :].unsqueeze(1).broadcast_to([P, TT, EXPERTS]), ALU.add))
                for t in range(TT):
                    step(dve.max(best[:, t, :], logits[:, t, :]))
                    step(dve.max_index(index[:, t, :], best[:, t, :], logits[:, t, :]))
                dve.tensor_scalar(neg[:, :], best[:, :, 0], -1.0, None, ALU.mult).then_inc(k.dve_made.sem, 1)
                step(dve.tensor_copy(index_f[:, :, :], index[:, :, :]))
                every = T.ids[:, :].unsqueeze(1).broadcast_to([P, TT, EXPERTS])
                step(dve.memset(chosen[:, :, :], 0.0))
                for n in range(4):
                    which = index_f[:, :, n:n + 1].broadcast_to([P, TT, EXPERTS])
                    step(dve.tensor_tensor(hot[:, :, :], every, which, ALU.is_equal))
                    if n < 3:
                        step(dve.tensor_tensor(chosen[:, :, :], chosen[:, :, :], hot[:, :, :], ALU.add))
                    else:
                        dve.tensor_tensor(chosen[:, :, :], chosen[:, :, :], hot[:, :, :], ALU.add)\
                           .then_inc(k.dve_made.sem, 1)
                dve.wait_ge(k.act_made.sem, k.act_made.at(1))
                step(dve.reciprocal(total[:, :], total[:, :]))
                step(dve.tensor_tensor(gates[:, :, :], gates[:, :, :],
                                       total[:, :].unsqueeze(2).broadcast_to([P, TT, 4]), ALU.mult))
                dve.wait_ge(k.dve_made.sem, k.dve_made.at(2))
                step(dve.memset(gate, 0.0))
                for n in range(4):
                    which = index_f[:, :, n:n + 1].broadcast_to([P, TT, EXPERTS])
                    step(dve.tensor_tensor(hot[:, :, :], every, which, ALU.is_equal))
                    step(dve.tensor_tensor(hot[:, :, :], hot[:, :, :],
                                           gates[:, :, n:n + 1].broadcast_to([P, TT, EXPERTS]), ALU.mult))
                    if n < 3:
                        step(dve.tensor_tensor(gate, gate, hot[:, :, :], ALU.add))
                    else:
                        dve.tensor_tensor(gate, gate, hot[:, :, :], ALU.add).then_inc(k.dve_made.sem, 1)
                dve.wait_ge(k.pe_made.sem, k.pe_made.at(2))
                dve.wait_ge(k.dve_made.sem, k.dve_made.at(3))
                step(dve.tensor_scalar(hot[:, :, :], chosen[:, :, :], -NOT_CHOSEN, NOT_CHOSEN, ALU.mult, ALU.add))
                step(dve.tensor_tensor(place, k.psum[:, 1, 0:TT * EXPERTS].rearrange("p (t e) -> p t e", t=TT),
                                       hot[:, :, :], ALU.add))
                step(dve.tensor_copy(T.counts[:, :], k.psum[:, 2, 0:EXPERTS]))
                step(dve.tensor_copy(T.count[:, :], T.counts[:, :]))
                for s in range(8):
                    dve.wait_ge(k.out_ready.sem, k.out_ready.at(s + 1))
                    x = k.x[:, s // 2, (s % 2) * 512:(s % 2) * 512 + 512]
                    dve.tensor_tensor(x, k.psum[:, 4 + s % 4, :], x, ALU.add).then_inc(k.out_saved.sem, 1)

            @block.scalar
            def _(act):
                T.y.round(act).then_inc(k.input_rounded.sem, 1)
                act.wait_ge(k.bias_loaded.sem, k.bias_loaded.at(48))
                act.activation(T.bias_parts[:, :], bias[:, :], ACT.Copy).then_inc(k.bias_rounded.sem, 1)
                for i in (1, 2):
                    act.wait_ge(k.bias_rest.sem, k.bias_rest.at(i))
                    for r in rows[i:]:
                        ins = act.activation(T.bias_parts[r, :], bias[r, :], ACT.Copy)
                    ins.then_inc(k.bias_rounded.sem, 1)
                act.wait_ge(k.dve_made.sem, k.dve_made.at(1))
                for t in range(TT):
                    ins = act.activation(gates[:, t, :], best[:, t, 0:4], ACT.Exp, bias=neg[:, t:t + 1],
                                         accum_out=total[:, t:t + 1])
                ins.then_inc(k.act_made.sem, 1)
                act.wait_ge(k.pe_made.sem, k.pe_made.at(3))
                act.activation(placeT[:, :], k.psum[0:EXPERTS, 3, :], ACT.Copy).then_inc(k.act_made.sem, 1)
        k.small_loaded.passed(48)
        k.pool_made.passed(2)
        k.bias_loaded.passed(48)
        k.bias_rounded.passed(3)
        k.bias_rest.passed(2)
        k.input_rounded.passed(1)
        k.pe_made.passed(3)
        k.dve_made.passed(3)
        k.act_made.passed(2)
        k.out_ready.passed(8)
        k.out_saved.passed(8)


def finish(k):
    with ExitStack() as ctx:
        y = k.sb("final_y", [P, TT, D], ctx=ctx)
        gain = k.sb("final_gain", [P, D], ctx=ctx)
        row_norm(k, k.x, TT, y, ctx)
        with k.block() as block:
            @block.sync
            def _(sp):
                sp.dma_start(gain[:, :], k.ins["final_norm_g_2"].partition_broadcast(P))\
                  .then_inc(k.small_loaded.sem, 16)
                out = k.out[0].rearrange("(t p) d -> t p d", p=P)
                for t in range(TT):
                    sp.wait_ge(k.dve_made.sem, k.dve_made.at(t + 1))
                    sp.dma_start(out[t], y[:, t, :]).then_inc(k.stored.sem, 16)
                sp.wait_ge(k.stored.sem, k.stored.at(16 * TT))

            @block.vector
            def _(dve):
                dve.wait_ge(k.small_loaded.sem, k.small_loaded.at(16))
                for t in range(TT):
                    dve.tensor_tensor(y[:, t, :], y[:, t, :], gain[:, :], ALU.mult).then_inc(k.dve_made.sem, 1)
        k.stored.passed(16 * TT)


def build(nc, ins, out):
    with ExitStack() as ctx:
        k = Core(nc, ctx, ins, out)
        with ExitStack() as weights:
            setup(k, weights)
            even_mixer(k)
            cross(k, 0)
            mlp(k, 0)
            odd_mixer(k)
            cross(k, 1)
            mlp(k, 1)
            second_mixer(k)
        experts(k)
        finish(k)


def kernel(**inputs):
    import numpy as np
    import concourse.bacc as bacc
    from concourse.bass_utils import run_bass_kernel_spmd

    nc = bacc.Bacc("TRN2", target_bir_lowering=False, num_devices=1)
    arrays, ins = {}, {}
    for name, value in inputs.items():
        a = np.ascontiguousarray(value)
        arrays[f"in_{name}"] = a
        ins[name] = nc.dram_tensor(f"in_{name}", a.shape, mybir.dt.from_np(a.dtype), kind="ExternalInput").ap()
    out = nc.dram_tensor("out", (1, S, D), F32, kind="ExternalOutput").ap()
    build(nc, ins, out)
    result = run_bass_kernel_spmd(nc, [arrays], core_ids=[0])
    return result.results[0]["out"]
```
